# Optimizing a Trainium2 kernel written in Bass

```python
import math
import jax, jax.numpy as jnp
from jax import lax
import numpy as np

D_MODEL = 1024
BATCH = 1
SEQ = 256
DEPTH = 1

CHUNK = 64
D_CONV = D_MODEL
CONV_WIDTH = 31
SSM_EXPAND = 2
D_INNER = SSM_EXPAND * D_MODEL
HEAD_DIM = 64
N_SSM_HEADS = D_INNER // HEAD_DIM
D_STATE = 128
N_GROUPS = 4
SSM_CONV_WIDTH = 4
D_XBC = D_INNER + 2 * N_GROUPS * D_STATE
D_FF = ((8 * D_MODEL // 3 + 255) // 256) * 256
IN_COLS = 2 * D_CONV + D_INNER + D_XBC + N_SSM_HEADS + 2 * D_MODEL
NORM_EPS = 1e-6
LN_EPS = 1e-5


def rms_norm(x, w, eps=NORM_EPS):
    xf = x.astype(jnp.float32)
    y = xf * lax.rsqrt(jnp.mean(xf * xf, axis=-1, keepdims=True) + eps)
    return (y * w.astype(jnp.float32)).astype(x.dtype)

def layer_norm(x, w, b, eps=LN_EPS):
    xf = x.astype(jnp.float32)
    mu = jnp.mean(xf, axis=-1, keepdims=True)
    var = jnp.mean(jnp.square(xf - mu), axis=-1, keepdims=True)
    y = (xf - mu) * lax.rsqrt(var + eps)
    return (y * w.astype(jnp.float32) + b.astype(jnp.float32)).astype(x.dtype)

def causal_depthwise_conv(u, w, b):
    k, ch = w.shape
    out = lax.conv_general_dilated(
        u, w[:, None, :].astype(u.dtype), window_strides=(1,), padding=[(k - 1, 0)],
        dimension_numbers=("NWC", "WIO", "NWC"), feature_group_count=ch)
    return out + b.astype(u.dtype)

def adaln(c, w, b):
    mod = jax.nn.silu(c) @ w + b
    shift, scale, gate = jnp.split(mod, 3, axis=-1)
    return shift[:, None, :], scale[:, None, :], gate[:, None, :]

def ssd_chunked_scan(xs, dt, a, bm, cm):
    b, L, H, P = xs.shape
    G, N = bm.shape[2], bm.shape[3]
    J = H // G
    nc = L // CHUNK

    def to_chunks(t):
        return jnp.moveaxis(t.reshape(b, nc, CHUNK, *t.shape[2:]), 1, 0)

    xdt = (xs * dt[..., None]).reshape(b, L, G, J, P)
    da = (dt * a).reshape(b, L, G, J)
    xc, ac, bc, cc = to_chunks(xdt), to_chunks(da), to_chunks(bm), to_chunks(cm)
    causal = jnp.tril(jnp.ones((CHUNK, CHUNK), dtype=bool))[None, :, :, None, None]

    def step(state, inp):
        xk, ak, bk, ck = inp
        acs = jnp.cumsum(ak, axis=1)
        seg = acs[:, :, None] - acs[:, None, :]
        decay = jnp.exp(jnp.where(causal, seg, -jnp.inf))
        cb = jnp.einsum("blgn,bsgn->blsg", ck, bk)
        y_diag = jnp.einsum("blsg,blsgj,bsgjp->blgjp", cb, decay, xk)
        y_off = jnp.einsum("blgn,bgjpn,blgj->blgjp", ck, state, jnp.exp(acs))
        last = acs[:, -1]
        w_in = jnp.exp(last[:, None] - acs)
        new_state = state * jnp.exp(last)[..., None, None] + jnp.einsum(
            "bsgn,bsgj,bsgjp->bgjpn", bk, w_in, xk)
        return new_state, y_diag + y_off

    init = jnp.zeros((b, G, J, P, N), jnp.float32)
    _, ys = lax.scan(step, init, (xc, ac, bc, cc))
    return jnp.moveaxis(ys, 0, 1).reshape(b, L, H, P)

def mixer_sublayer(h, w_in, conv_dw_w, conv_dw_b, conv_ln_w, conv_ln_b, w_conv_out,
                   ssm_conv_w, ssm_conv_b, dt_bias, a_log, d_skip, ssm_norm_w, w_ssm_out, w_out):
    b, L, _ = h.shape
    proj = h @ w_in
    splits = np.cumsum([2 * D_CONV, D_INNER, D_XBC, N_SSM_HEADS, D_MODEL]).tolist()
    conv_in, z, xbc, dt_raw, g_conv, g_ssm = jnp.split(proj, splits, axis=-1)

    a_half, b_half = jnp.split(conv_in, 2, axis=-1)
    u = a_half * jax.nn.sigmoid(b_half)
    u = causal_depthwise_conv(u, conv_dw_w, conv_dw_b)
    u = jax.nn.silu(layer_norm(u, conv_ln_w, conv_ln_b))
    y_conv = u @ w_conv_out

    xbc = jax.nn.silu(causal_depthwise_conv(xbc, ssm_conv_w, ssm_conv_b))
    xs, bm, cm = jnp.split(xbc, [D_INNER, D_INNER + N_GROUPS * D_STATE], axis=-1)
    xs_f = xs.astype(jnp.float32).reshape(b, L, N_SSM_HEADS, HEAD_DIM)
    bm_f = bm.astype(jnp.float32).reshape(b, L, N_GROUPS, D_STATE)
    cm_f = cm.astype(jnp.float32).reshape(b, L, N_GROUPS, D_STATE)
    dt = jax.nn.softplus(dt_raw.astype(jnp.float32) + dt_bias.astype(jnp.float32))
    a = -jnp.exp(a_log.astype(jnp.float32))
    y = ssd_chunked_scan(xs_f, dt, a, bm_f, cm_f) + d_skip.astype(jnp.float32)[:, None] * xs_f
    y = y.reshape(b, L, D_INNER) * jax.nn.silu(z.astype(jnp.float32))
    yg = y.reshape(b, L, N_GROUPS, D_INNER // N_GROUPS)
    yg = yg * lax.rsqrt(jnp.mean(yg * yg, axis=-1, keepdims=True) + NORM_EPS)
    y = (yg.reshape(b, L, D_INNER) * ssm_norm_w.astype(jnp.float32)).astype(h.dtype)
    y_ssm = y @ w_ssm_out

    merged = jax.nn.sigmoid(g_conv) * y_conv + jax.nn.sigmoid(g_ssm) * y_ssm
    return merged @ w_out

def ffn_sublayer(h, w_ffn_in, w_ffn_down):
    gate, up = jnp.split(h @ w_ffn_in, 2, axis=-1)
    return (jax.nn.silu(gate) * up) @ w_ffn_down

def first_inputs(seed: int = 0) -> dict:
    key = jax.random.key(seed)
    ks = jax.random.split(key, 32)
    f32 = jnp.float32
    nrm = lambda k, shape, s: jax.random.normal(k, shape, f32) * s
    gain = lambda k, shape: 1.0 + 0.05 * jax.random.normal(k, shape, f32)
    Ld = DEPTH
    u_dt = jax.random.uniform(ks[13], (Ld, N_SSM_HEADS), f32)
    dt0 = jnp.exp(u_dt * (math.log(0.1) - math.log(0.001)) + math.log(0.001))
    dt_bias = dt0 + jnp.log(-jnp.expm1(-dt0))
    a_log = jnp.log(jax.random.uniform(ks[14], (Ld, N_SSM_HEADS), f32, 1.0, 16.0))
    return {
        "x": jax.random.normal(ks[0], (BATCH, SEQ, D_MODEL), f32),
        "c": jax.random.normal(ks[1], (BATCH, D_MODEL), f32),
        "w_ada_mix": nrm(ks[2], (Ld, D_MODEL, 3 * D_MODEL), D_MODEL ** -0.5),
        "b_ada_mix": nrm(ks[3], (Ld, 3 * D_MODEL), 0.01),
        "norm_mix_w": gain(ks[4], (Ld, D_MODEL)),
        "w_in": nrm(ks[5], (Ld, D_MODEL, IN_COLS), D_MODEL ** -0.5),
        "conv_dw_w": nrm(ks[6], (Ld, CONV_WIDTH, D_CONV), CONV_WIDTH ** -0.5),
        "conv_dw_b": nrm(ks[7], (Ld, D_CONV), 0.01),
        "conv_ln_w": gain(ks[8], (Ld, D_CONV)),
        "conv_ln_b": nrm(ks[9], (Ld, D_CONV), 0.01),
        "w_conv_out": nrm(ks[10], (Ld, D_CONV, D_MODEL), D_CONV ** -0.5),
        "ssm_conv_w": nrm(ks[11], (Ld, SSM_CONV_WIDTH, D_XBC), SSM_CONV_WIDTH ** -0.5),
        "ssm_conv_b": nrm(ks[12], (Ld, D_XBC), 0.01),
        "dt_bias": dt_bias,
        "a_log": a_log,
        "d_skip": gain(ks[15], (Ld, N_SSM_HEADS)),
        "ssm_norm_w": gain(ks[16], (Ld, D_INNER)),
        "w_ssm_out": nrm(ks[17], (Ld, D_INNER, D_MODEL), D_INNER ** -0.5),
        "w_out": nrm(ks[18], (Ld, D_MODEL, D_MODEL), D_MODEL ** -0.5),
        "w_ada_ffn": nrm(ks[19], (Ld, D_MODEL, 3 * D_MODEL), D_MODEL ** -0.5),
        "b_ada_ffn": nrm(ks[20], (Ld, 3 * D_MODEL), 0.01),
        "norm_ffn_w": gain(ks[21], (Ld, D_MODEL)),
        "w_ffn_in": nrm(ks[22], (Ld, D_MODEL, 2 * D_FF), D_MODEL ** -0.5),
        "w_ffn_down": nrm(ks[23], (Ld, D_FF, D_MODEL), D_FF ** -0.5),
        "final_norm_w": gain(ks[24], (D_MODEL,)),
    }

def first_block(x, c, w_ada_mix, b_ada_mix, norm_mix_w, w_in, conv_dw_w, conv_dw_b, conv_ln_w,
              conv_ln_b, w_conv_out, ssm_conv_w, ssm_conv_b, dt_bias, a_log, d_skip, ssm_norm_w,
              w_ssm_out, w_out, w_ada_ffn, b_ada_ffn, norm_ffn_w, w_ffn_in, w_ffn_down,
              final_norm_w):
    for i in range(DEPTH):
        shift, scale, gate = adaln(c, w_ada_mix[i], b_ada_mix[i])
        h = rms_norm(x, norm_mix_w[i]) * (1.0 + scale) + shift
        x = x + gate * mixer_sublayer(
            h, w_in[i], conv_dw_w[i], conv_dw_b[i], conv_ln_w[i], conv_ln_b[i], w_conv_out[i],
            ssm_conv_w[i], ssm_conv_b[i], dt_bias[i], a_log[i], d_skip[i], ssm_norm_w[i],
            w_ssm_out[i], w_out[i])
        shift, scale, gate = adaln(c, w_ada_ffn[i], b_ada_ffn[i])
        h = rms_norm(x, norm_ffn_w[i]) * (1.0 + scale) + shift
        x = x + gate * ffn_sublayer(h, w_ffn_in[i], w_ffn_down[i])
    return rms_norm(x, final_norm_w)


DEPTH_2 = 2

N_MIXERS = 2
A_HEADS = 8
A_DK = 128
A_DV = 128
A_CONV = 5
A_W = A_HEADS * A_DK
A_VW = A_HEADS * A_DV
A_CONV_CH = 2 * A_W + A_VW
A_IN = 2 * A_W + 2 * A_VW + 4 * A_HEADS
B_HEADS = 4
B_DK = 128
B_DV = 256
B_RANK = 16
B_TAU = 16.0
B_KW = B_HEADS * B_DK
B_VW = B_HEADS * B_DV
B_IN = 2 * B_KW + 2 * B_VW + 2 * B_RANK
D_FF_2 = 4 * D_MODEL
DEEPNORM_ALPHA = (2 * DEPTH_2) ** 0.25
DEEPNORM_BETA = (8 * DEPTH_2) ** -0.25
RMS_EPS = 1e-6
N_A_LAYERS = (DEPTH_2 + 1) // 2
N_B_LAYERS = DEPTH_2 // 2


F32 = jnp.float32

def _layernorm(x, g, b):
    xf = x.astype(F32)
    mu = jnp.mean(xf, axis=-1, keepdims=True)
    xc = xf - mu
    var = jnp.mean(xc * xc, axis=-1, keepdims=True)
    return (xc * lax.rsqrt(var + LN_EPS) * g.astype(F32) + b.astype(F32)).astype(x.dtype)

def _rmsnorm(x, g):
    return x * lax.rsqrt(jnp.mean(x * x, axis=-1, keepdims=True) + RMS_EPS) * g.astype(F32)

def _l2norm(x):
    return x * lax.rsqrt(jnp.sum(x * x, axis=-1, keepdims=True) + 1e-6)

def _flip(t):
    return jnp.flip(t, axis=2)

def _depthwise_conv(u, w):
    k = w.shape[0]
    return lax.conv_general_dilated(
        u, w[:, None, :], window_strides=(1,), padding=[(k // 2, k // 2)],
        dimension_numbers=("NWC", "WIO", "NWC"), feature_group_count=u.shape[-1])

def _gated_delta_chunked(q, k, v, beta, g):
    bn, h, s, dk = q.shape
    dv = v.shape[-1]
    n = s // CHUNK
    q = q.reshape(bn, h, n, CHUNK, dk)
    k = k.reshape(bn, h, n, CHUNK, dk)
    v = v.reshape(bn, h, n, CHUNK, dv)
    beta = beta.reshape(bn, h, n, CHUNK)
    gc = jnp.cumsum(g.reshape(bn, h, n, CHUNK), axis=-1)
    causal = jnp.tril(jnp.ones((CHUNK, CHUNK), bool))
    strict = jnp.tril(jnp.ones((CHUNK, CHUNK), bool), -1)
    decay_mat = jnp.exp(jnp.where(causal, gc[..., :, None] - gc[..., None, :], -jnp.inf))
    kb = k * beta[..., None]
    a_mat = jnp.where(strict, jnp.einsum('bhncd,bhnsd->bhncs', kb, k) * decay_mat, 0.0)
    lhs = a_mat + jnp.eye(CHUNK, dtype=F32)
    rhs = jnp.concatenate([v * beta[..., None], kb * jnp.exp(gc)[..., None]], axis=-1)
    sol = lax.linalg.triangular_solve(lhs, rhs, left_side=True, lower=True, unit_diagonal=True)
    u, w = sol[..., :dv], sol[..., dv:]
    qk = jnp.einsum('bhncd,bhnsd->bhncs', q, k) * decay_mat
    q_dec = q * jnp.exp(gc)[..., None]
    k_dec = k * jnp.exp(gc[..., -1:] - gc)[..., None]
    g_last = jnp.exp(gc[..., -1])
    xs = tuple(jnp.moveaxis(t, 2, 0) for t in (qk, q_dec, k_dec, u, w, g_last))

    def step(state, inp):
        qk_c, qd_c, kd_c, u_c, w_c, gl_c = inp
        v_new = u_c - jnp.einsum('bhcd,bhde->bhce', w_c, state)
        o = jnp.einsum('bhcd,bhde->bhce', qd_c, state) + jnp.einsum('bhcs,bhse->bhce', qk_c, v_new)
        state = state * gl_c[..., None, None] + jnp.einsum('bhcd,bhce->bhde', kd_c, v_new)
        return state, o

    s0 = jnp.zeros((bn, h, dk, dv), F32)
    _, o = lax.scan(step, s0, xs)
    return jnp.moveaxis(o, 0, 2).reshape(bn, h, s, dv)

def _gla_chunked(q, k, v, log_a):
    bn, h, s, dk = q.shape
    dv = v.shape[-1]
    n = s // CHUNK

    def to_chunks(t):
        return jnp.moveaxis(t.reshape(bn, h, n, CHUNK, t.shape[-1]), 2, 0)

    qc, kc, vc = to_chunks(q), to_chunks(k), to_chunks(v)
    bc = jnp.cumsum(to_chunks(log_a), axis=3)
    causal = jnp.tril(jnp.ones((CHUNK, CHUNK), bool))[:, :, None]

    def step(state, inp):
        q_c, k_c, v_c, b_c = inp
        dec = jnp.exp(jnp.where(causal, b_c[:, :, :, None, :] - b_c[:, :, None, :, :], -jnp.inf))
        scores = jnp.einsum('bhid,bhjd,bhijd->bhij', q_c, k_c, dec)
        o = jnp.einsum('bhid,bhde->bhie', q_c * jnp.exp(b_c), state) + jnp.einsum('bhij,bhje->bhie', scores, v_c)
        b_last = b_c[:, :, -1:, :]
        state = jnp.exp(b_last[:, :, 0, :])[..., None] * state + jnp.einsum(
            'bhjd,bhje->bhde', k_c * jnp.exp(b_last - b_c), v_c)
        return state, o

    s0 = jnp.zeros((bn, h, dk, dv), F32)
    _, o = lax.scan(step, s0, (qc, kc, vc, bc))
    return jnp.moveaxis(o, 0, 2).reshape(bn, h, s, dv)

def _mixer_gdn(h, w_in, conv_w, a_log, dt_bias, norm_g, w_out):
    bn, s, _ = h.shape
    proj = jnp.matmul(h, w_in).astype(F32)
    qkv = jax.nn.silu(_depthwise_conv(proj[..., :A_CONV_CH], conv_w.astype(F32)))
    z = proj[..., A_CONV_CH:A_CONV_CH + A_VW]
    ba = proj[..., A_CONV_CH + A_VW:].reshape(bn, s, 2, 2, A_HEADS)

    def heads(t, d):
        return t.reshape(bn, s, A_HEADS, d).transpose(0, 2, 1, 3)

    q = _l2norm(heads(qkv[..., :A_W], A_DK)) * (A_DK ** -0.5)
    k = _l2norm(heads(qkv[..., A_W:2 * A_W], A_DK))
    v = heads(qkv[..., 2 * A_W:], A_DV)
    beta = jax.nn.sigmoid(ba[:, :, 0]).transpose(2, 0, 3, 1)
    g = (-jnp.exp(a_log.astype(F32)) * jax.nn.softplus(ba[:, :, 1] + dt_bias.astype(F32))).transpose(2, 0, 3, 1)
    o_f = _gated_delta_chunked(q, k, v, beta[0], g[0])
    o_b = _flip(_gated_delta_chunked(_flip(q), _flip(k), _flip(v), _flip(beta[1]), _flip(g[1])))
    o = (o_f + o_b).transpose(0, 2, 1, 3)
    o = _rmsnorm(o, norm_g) * jax.nn.silu(z.reshape(bn, s, A_HEADS, A_DV))
    return jnp.matmul(o.reshape(bn, s, A_VW).astype(w_out.dtype), w_out)

def _mixer_gla(h, w_in, gate_w2, gate_b, norm_g, w_out):
    bn, s, _ = h.shape
    proj = jnp.matmul(h, w_in).astype(F32)

    def heads(t, d):
        return t.reshape(bn, s, B_HEADS, d).transpose(0, 2, 1, 3)

    q = heads(proj[..., :B_KW], B_DK) * (B_DK ** -0.5)
    k = heads(proj[..., B_KW:2 * B_KW], B_DK)
    v = heads(proj[..., 2 * B_KW:2 * B_KW + B_VW], B_DV)
    r = proj[..., 2 * B_KW + B_VW:2 * B_KW + 2 * B_VW]
    gl = proj[..., 2 * B_KW + 2 * B_VW:].reshape(bn, s, 2, B_RANK)
    gate_logit = jnp.einsum('bsnr,nrk->nbsk', gl, gate_w2.astype(F32)) + gate_b.astype(F32)[:, None, None, :]
    log_a = (jax.nn.log_sigmoid(gate_logit) / B_TAU).reshape(2, bn, s, B_HEADS, B_DK).transpose(0, 1, 3, 2, 4)
    o_f = _gla_chunked(q, k, v, log_a[0])
    o_b = _flip(_gla_chunked(_flip(q), _flip(k), _flip(v), _flip(log_a[1])))
    o = (o_f + o_b).transpose(0, 2, 1, 3)
    o = _rmsnorm(o, norm_g) * jax.nn.silu(r.reshape(bn, s, B_HEADS, B_DV))
    return jnp.matmul(o.reshape(bn, s, B_VW).astype(w_out.dtype), w_out)

def _sq_relu_mlp(h, w1, w2):
    a = jax.nn.relu(jnp.matmul(h, w1))
    return jnp.matmul(a * a, w2)

def second_inputs(seed: int = 0) -> dict:
    key = jax.random.key(seed)
    ks = jax.random.split(key, 20)
    nrm = jax.random.normal
    x = nrm(ks[0], (BATCH, SEQ, D_MODEL), F32)
    a_w_in = nrm(ks[1], (N_A_LAYERS, D_MODEL, A_IN), F32) * D_MODEL ** -0.5
    a_conv = nrm(ks[2], (N_A_LAYERS, A_CONV, A_CONV_CH), F32) * A_CONV ** -0.5
    a_alog = jnp.log(jax.random.uniform(ks[3], (N_A_LAYERS, 2, A_HEADS), F32, 1.0, 16.0))
    dt = jnp.exp(jax.random.uniform(ks[4], (N_A_LAYERS, 2, A_HEADS), F32, math.log(1e-3), math.log(1e-1)))
    a_dt_bias = dt + jnp.log(-jnp.expm1(-dt))
    a_norm_g = 1.0 + 0.02 * nrm(ks[5], (N_A_LAYERS, A_DV), F32)
    a_w_out = nrm(ks[6], (N_A_LAYERS, A_VW, D_MODEL), F32) * (A_VW ** -0.5 * DEEPNORM_BETA)
    b_w_in = nrm(ks[7], (N_B_LAYERS, D_MODEL, B_IN), F32) * D_MODEL ** -0.5
    b_gate_w2 = nrm(ks[8], (N_B_LAYERS, 2, B_RANK, B_KW), F32) * B_RANK ** -0.5
    b_gate_b = 0.1 * nrm(ks[9], (N_B_LAYERS, 2, B_KW), F32)
    b_norm_g = 1.0 + 0.02 * nrm(ks[10], (N_B_LAYERS, B_DV), F32)
    b_w_out = nrm(ks[11], (N_B_LAYERS, B_VW, D_MODEL), F32) * (B_VW ** -0.5 * DEEPNORM_BETA)
    ln1_g = 1.0 + 0.02 * nrm(ks[12], (DEPTH_2, D_MODEL), F32)
    ln1_b = 0.02 * nrm(ks[13], (DEPTH_2, D_MODEL), F32)
    mlp_w1 = nrm(ks[14], (DEPTH_2, D_MODEL, D_FF_2), F32) * D_MODEL ** -0.5
    mlp_w2 = nrm(ks[15], (DEPTH_2, D_FF_2, D_MODEL), F32) * (D_FF_2 ** -0.5 * DEEPNORM_BETA)
    ln2_g = 1.0 + 0.02 * nrm(ks[16], (DEPTH_2, D_MODEL), F32)
    ln2_b = 0.02 * nrm(ks[17], (DEPTH_2, D_MODEL), F32)
    return {"x": x, "a_w_in": a_w_in, "a_conv": a_conv, "a_alog": a_alog, "a_dt_bias": a_dt_bias,
            "a_norm_g": a_norm_g, "a_w_out": a_w_out, "b_w_in": b_w_in, "b_gate_w2": b_gate_w2,
            "b_gate_b": b_gate_b, "b_norm_g": b_norm_g, "b_w_out": b_w_out, "ln1_g": ln1_g,
            "ln1_b": ln1_b, "mlp_w1": mlp_w1, "mlp_w2": mlp_w2, "ln2_g": ln2_g, "ln2_b": ln2_b}

def second_block(x, a_w_in, a_conv, a_alog, a_dt_bias, a_norm_g, a_w_out, b_w_in, b_gate_w2,
              b_gate_b, b_norm_g, b_w_out, ln1_g, ln1_b, mlp_w1, mlp_w2, ln2_g, ln2_b):
    for i in range(DEPTH_2):
        j = i // N_MIXERS
        if i % N_MIXERS == 0:
            m = _mixer_gdn(x, a_w_in[j], a_conv[j], a_alog[j], a_dt_bias[j], a_norm_g[j], a_w_out[j])
        else:
            m = _mixer_gla(x, b_w_in[j], b_gate_w2[j], b_gate_b[j], b_norm_g[j], b_w_out[j])
        x = _layernorm(DEEPNORM_ALPHA * x + m.astype(x.dtype), ln1_g[i], ln1_b[i])
        x = _layernorm(DEEPNORM_ALPHA * x + _sq_relu_mlp(x, mlp_w1[i], mlp_w2[i]).astype(x.dtype), ln2_g[i], ln2_b[i])
    return x


def setup_inputs(seed=0):
    out = dict(first_inputs(seed))
    for name, value in second_inputs(seed + 1).items():
        if name != "x":
            out[name + "_2"] = value
    return out


def reference(
    x, c, w_ada_mix, b_ada_mix, norm_mix_w, w_in, conv_dw_w, conv_dw_b, conv_ln_w, conv_ln_b,
    w_conv_out, ssm_conv_w, ssm_conv_b, dt_bias, a_log, d_skip, ssm_norm_w, w_ssm_out, w_out,
    w_ada_ffn, b_ada_ffn, norm_ffn_w, w_ffn_in, w_ffn_down, final_norm_w, a_w_in_2, a_conv_2,
    a_alog_2, a_dt_bias_2, a_norm_g_2, a_w_out_2, b_w_in_2, b_gate_w2_2, b_gate_b_2, b_norm_g_2,
    b_w_out_2, ln1_g_2, ln1_b_2, mlp_w1_2, mlp_w2_2, ln2_g_2, ln2_b_2,
):
    x = first_block(
        x, c, w_ada_mix, b_ada_mix, norm_mix_w, w_in, conv_dw_w, conv_dw_b, conv_ln_w,
        conv_ln_b, w_conv_out, ssm_conv_w, ssm_conv_b, dt_bias, a_log, d_skip, ssm_norm_w,
        w_ssm_out, w_out, w_ada_ffn, b_ada_ffn, norm_ffn_w, w_ffn_in, w_ffn_down, final_norm_w,
    )
    return second_block(
        x, a_w_in_2, a_conv_2, a_alog_2, a_dt_bias_2, a_norm_g_2, a_w_out_2, b_w_in_2,
        b_gate_w2_2, b_gate_b_2, b_norm_g_2, b_w_out_2, ln1_g_2, ln1_b_2, mlp_w1_2, mlp_w2_2,
        ln2_g_2, ln2_b_2,
    )


_drawn_inputs = setup_inputs


def setup_inputs(seed=0):
    import zlib

    import numpy as np

    out = dict(_drawn_inputs(seed))
    spreads = {}
    factors = {'b_ada_mix': 5.066,
     'conv_dw_b': 8.0,
     'conv_ln_w': 3.951,
     'conv_ln_b': 8.0,
     'ssm_conv_b': 8.0,
     'd_skip': 8.0,
     'ssm_norm_w': 2.867,
     'b_ada_ffn': 4.08,
     'a_norm_g_2': 8.0,
     'b_gate_b_2': 5.967,
     'b_norm_g_2': 8.0}
    for name, (base, spread) in spreads.items():
        noise = np.random.default_rng([zlib.crc32(name.encode()), seed]).standard_normal(out[name].shape)
        drawn = base * np.exp(spread * noise) if base else spread * noise
        out[name] = __import__('jax').numpy.asarray(drawn.astype(out[name].dtype))
    for name, factor in factors.items():
        out[name] = (out[name] * factor).astype(out[name].dtype)
    return out
```

```python
import math
from contextlib import ExitStack

import concourse.bass as bass
from concourse import mybir

F32 = mybir.dt.float32
F32R = mybir.dt.float32r
I32 = mybir.dt.int32
ALU = mybir.AluOpType
ACT = mybir.ActivationFunctionType

P = 128
T = 256
NT = T // P
D = 1024
DT = D // P
KT = 8
COLS = 256
D_INNER = 2048
NH = 32
NG = 4
D_FF = 2816
FF_T = D_FF // P
FF_CHUNKS = [6, 6, 5, 5]
D_FF2 = 4096
CW = 31
SW = 4
AW = 5
A_HEADS = 8
B_HEADS = 4
RMS_EPS = 1e-6
LN_EPS = 1e-5
ALPHA = (2 * 2) ** 0.25


def ds(a, n):
    return bass.ds(a, n)


class Chain:

    def __init__(self, eng, sem):
        self.eng, self.sem, self.n, self.off = eng, sem, 0, 0

    def link(self, ins):
        self.tick(ins)
        self.wait()

    def tick(self, ins):
        ins.then_inc(self.sem, 1)
        self.n += 1

    def wait(self, back=0):
        self.eng.wait_ge(self.sem, self.n - back + self.off)

    def loop(self, j, per, times):
        self.start, self.per, self.times = self.n, per, times
        self.off = j * per

    def done(self):
        assert self.n - self.start == self.per, (self.n - self.start, self.per)
        self.n, self.off = self.start + self.per * self.times, 0


class Section:

    def __init__(self, name, src, nb, kts=(KT,), lo="vector"):
        self.name, self.src, self.nb, self.kts = name, src, nb, list(kts)
        self.lo = lo
        self.chunks = len(self.kts)


def program(nc, a, out):
    def cols(w, c0, kt=KT):
        v = w.rearrange("(k p) c -> p k c", p=P)
        return lambda b: v[:, 0:kt, ds(b * COLS + c0, COLS)]

    def pairs(w, c0, c1):
        v = w.rearrange("(k p) c -> p k c", p=P)
        return lambda j, which: v[:, :, ds(j * COLS + (c1 if which else c0), COLS)]

    w_in = a["w_in"][0]
    a_in = a["a_w_in_2"][0]
    b_in = a["b_w_in_2"][0]
    OFF_Z, OFF_XBC = 2 * D, 2 * D + D_INNER
    OFF_DT = OFF_XBC + D_INNER + 2 * NG * P
    OFF_G = OFF_DT + NH
    A_QKV, A_Z = 3 * D, 3 * D
    A_BA = A_Z + D
    B_QK, B_V, B_R = D, D, 2 * D
    B_GL = 3 * D
    SECS = [
        Section("conv_b", cols(w_in, D), 4),
        Section("conv_a", cols(w_in, 0), 4),
        Section("xbc", cols(w_in, OFF_XBC), 12, lo="gpsimd"),
        Section("z", cols(w_in, OFF_Z), 8, lo="gpsimd"),
        Section("g", cols(w_in, OFF_G), 8, lo="gpsimd"),
        Section("conv_out", cols(a["w_conv_out"][0], 0), 4),
        Section("ssm_out", a["w_ssm_out"][0], 8, (8, 8)),
        Section("w_out", cols(a["w_out"][0], 0), 4),
        Section("ffn_in", pairs(a["w_ffn_in"][0], 0, D_FF), 22),
        Section("ffn_down", a["w_ffn_down"][0], 16, FF_CHUNKS),
        Section("a_qkv", cols(a_in, 0), 12, lo="gpsimd"),
        Section("a_z", cols(a_in, A_Z), 4),
        Section("a_out", cols(a["a_w_out_2"][0], 0), 4),
        Section("mlp1_0", cols(a["mlp_w1_2"][0], 0), 16),
        Section("mlp2_0", a["mlp_w2_2"][0], 16, (8, 8, 8, 8)),
        Section("b_qk", cols(b_in, 0), 4),
        Section("b_v", cols(b_in, B_V), 4),
        Section("b_r", cols(b_in, B_R), 4),
        Section("b_out", cols(a["b_w_out_2"][0], 0), 4),
        Section("mlp1_1", cols(a["mlp_w1_2"][1], 0), 16),
        Section("mlp2_1", a["mlp_w2_2"][1], 16, (8, 8, 8, 8)),
    ]
    SEC = {s.name: s for s in SECS}
    ADA_FIRST = [("w_ada_mix", b) for b in range(8)]
    ADA_REST = [("w_ada_mix", b) for b in range(8, 12)] + [("w_ada_ffn", b) for b in range(12)]
    g = len(ADA_FIRST)
    t = o = 0
    before = None
    for s in SECS:
        s.g0, s.t0, s.o0 = g, t, o
        s.ahead = before is not None and before.lo == s.lo and before.name != "g"
        if before:
            before.next = s
        g, t, o = g + s.nb, t + 2 * s.nb, o + 2 * s.nb // s.chunks
        if s.name == "g":
            ada_g0 = g
            g += len(ADA_REST)
        before = s
    before.next = None

    def kt_of(s, u):
        return s.kts[u % s.chunks]

    def over_blocks(eng, s, body, chain=None, per=0):
        turns = (s.nb - 1) // 4
        if turns:
            with eng.Fori(0, turns) as j:
                if chain:
                    chain.loop(j, per, turns)
                for u in range(4):
                    body(4 * j + u, u, False, j)
                if chain:
                    chain.done()
        for b in range(4 * turns, s.nb):
            body(b, b % 4, b == s.nb - 1, turns)

    with ExitStack() as ctx:
        TILE = T * 4
        base = (nc.sbuf_base + 63) // 64 * 64

        def at(name, tile, shape, dt=F32):
            return nc.alloc_sbuf_tensor_at(name, shape, dt, offset=base + int(tile * TILE))

        def psum(name, shape):
            return ctx.enter_context(nc.psum_tensor(name, shape, F32))

        def sem(name):
            return ctx.enter_context(nc.semaphore(name))

        raw = at("raw", 0, [P, 4, KT, COLS])
        whi = at("whi", 32, [P, 4, KT, P], F32R)
        wlo = at("wlo", 48, [P, 4, KT, P], F32R)
        X = at("X", 64, [P, DT, T])
        H = at("H", 72, [P, DT, T])
        HH = at("HH", 80, [P, DT, T], F32R)
        HL = at("HL", 88, [P, DT, T], F32R)
        maskf = at("maskf", 96, [P, 3 * P])
        maskb = at("maskb", 97.5, [P, 3 * P])
        slo = at("slo", 99, [P, 2 * P])
        suo = at("suo", 100, [P, 2 * P])
        ident = at("ident", 101, [P, P])
        ones = maskf[:, P:2 * P]
        par = at("par", 102, [P, 768])
        SM = 105
        small_at = [0]

        def small(name, n, dt=F32):
            ap = at(name, SM + small_at[0] / 256, [P, n], dt)
            small_at[0] += (n + 7) // 8 * 8
            assert small_at[0] <= 3 * 256
            return ap

        sc = small("sc", 8)
        dtb = small("dtb", 2 * NH)
        gab = small("gab", 64)
        dtt = small("dtt", 2 * NH)
        dat = small("dat", 2 * NH)
        spt = [small(f"spt{i}", 64) for i in range(4)]
        dsk = small("dsk", 32 + 16)
        AR = 108

        def ar(name, tile, shape, dt=F32):
            return at(name, AR + tile, shape, dt)

        UP = ar("UP", 0, [P, DT, T + CW - 1])
        UH = ar("UH", 0, [P, DT, T], F32R)
        ACC = ar("ACC", 9, [P, DT, T])
        UL = ar("UL", 9, [P, DT, T], F32R)
        XP = ar("XP", 17, [P, 4, T + SW - 1])
        XBC = ar("XBC", 22, [P, 24, T])
        Z = ar("Z", 46, [P, 16, T])
        YL = ar("YL", 46, [P, 16, T], F32R)
        G = ar("G", 62, [P, 16, T])
        CB = ar("CB", 78, [P, NG, 3 * P])
        LS = ar("LS", 84, [P, 2, 3 * P])
        ES = ar("ES", 87, [P, 2, 3 * P])
        XD = ar("XD", 90, [P, 2, NT, 64])
        XT = at("XT", 80, [P, NT, D_INNER])
        YH = at("YH", 80, [P, 16, T], F32R)
        PRW = ar("PRW", 78, [P, 6, P])
        XIN = ar("XIN", 22, [P, NT, D])
        ADA = ar("ADA", 30, [P, 2 * D])
        MOD = ar("MOD", 95, [P, 48])
        NR = ar("NR", 96, [P, 2, T])
        HIDH = ar("HIDH", 0, [P, 32, T], F32R)
        HIDL = ar("HIDL", 32, [P, 32, T], F32R)
        TMP = ar("TMP", 64, [P, 4, T])
        TMQ = ar("TMQ", 68, [P, 4, T])

        acc = psum("acc", [P, 4, 512])
        pm = psum("pm", [P, 4, 512])

        landed = [sem(f"landed{i}") for i in range(4)]
        raw_used = sem("raw_used")
        hi_ready = sem("hi_ready")
        w_used = sem("w_used")
        acc_free = sem("acc_free")
        vchain, achain, gchain = sem("vchain"), sem("achain"), sem("gchain")
        par_in, x_in = sem("par_in"), sem("x_in")
        masks = sem("masks")
        par_t, par_ok = sem("par_t"), sem("par_ok")
        silu_c = sem("silu_c")
        ada_part, ada_sum, mod_ok = sem("ada_part"), sem("ada_sum"), sem("mod_ok")
        xt_p, x_ok = sem("xt_p"), sem("x_ok")
        n_x, n_mean, n_sq, n_sum, n_std, n_h, n_hh, n_hl = (sem(f"norm_{k}") for k in
                                                   ("x", "mean", "sq", "sum", "std", "h", "hh", "hl"))
        evac_a = sem("evac_a")
        evac_v = sem("evac_v")
        out_sem = sem("out_sem")
        running = ExitStack()
        block = running.enter_context(nc.Block())

        rows, prow = [], {}

        def param(name, ap, n):
            prow[name] = sum(r[1] for r in rows)
            rows.append((ap, n))

        def vec(v):
            return v.rearrange("(t p) -> t p", p=P)

        param("c", vec(a["c"][0]), 8)
        param("b_ada_mix", vec(a["b_ada_mix"][0]), 24)
        param("b_ada_ffn", vec(a["b_ada_ffn"][0]), 24)
        param("norm_mix_w", vec(a["norm_mix_w"][0]), 8)
        param("conv_ln_w", vec(a["conv_ln_w"][0]), 8)
        param("conv_ln_b", vec(a["conv_ln_b"][0]), 8)
        param("conv_dw_b", vec(a["conv_dw_b"][0]), 8)
        param("ssm_conv_b", vec(a["ssm_conv_b"][0]), 24)
        param("ssm_norm_w", vec(a["ssm_norm_w"][0]), 16)
        param("norm_ffn_w", vec(a["norm_ffn_w"][0]), 8)
        param("final_norm_w", vec(a["final_norm_w"]), 8)
        param("ssm_conv_w", a["ssm_conv_w"][0].rearrange("w (t p) -> (w t) p", p=P), SW * 24)
        param("conv_dw_w", a["conv_dw_w"][0].rearrange("w (t p) -> (w t) p", p=P), CW * DT)
        param("a_conv", a["a_conv_2"][0].rearrange("w (t p) -> (w t) p", p=P), AW * 24)
        param("a_norm_g", a["a_norm_g_2"], 1)
        param("b_norm_g", vec(a["b_norm_g_2"][0]), 2)
        param("gate_b", a["b_gate_b_2"][0].rearrange("d (t p) -> (d t) p", p=P), 8)
        for k in ("ln1_g", "ln1_b", "ln2_g", "ln2_b"):
            param(k, a[k + "_2"].rearrange("l (t p) -> (l t) p", p=P), 16)
        NPAR = sum(n for _, n in rows)
        NPT = -(-NPAR // P)
        assert NPT <= 6

        def pc(name, i, n=1):
            return par[:, ds(i + prow[name], n)]

        pieces, r0 = [], 0
        for ap, n in rows:
            done = 0
            while done < n:
                m = min(n - done, P - (r0 + done) % P)
                pieces.append((ap[done:done + m, :], (r0 + done) % P, (r0 + done) // P, m))
                done += m
            r0 += n

        def bcast(v, n):
            return bass.AP(tensor=v.tensor, offset=v.offset, ap=[[0, P], [1, n]])

        def ada_src(name, b):
            w = a[name][0].rearrange("(k p) c -> p k c", p=P)
            if b < 8:
                return w[:, b, 0:2 * D]
            return w[:, 2 * (b - 8):2 * (b - 8) + 2, 2 * D:3 * D]

        @block.sync
        def _(sp):
            sp.dma_start(XIN[:], a["x"][0].rearrange("(t p) d -> p t d", p=P)).then_inc(x_in, 16)

            def load_ada(name, b, gb):
                if gb >= 4:
                    sp.wait_ge(raw_used, 2 * (gb - 3))
                dst = raw[:, gb % 4].rearrange("p k c -> p (k c)")
                if b >= 8:
                    dst = dst.rearrange("p (k c) -> p k c", k=2)
                sp.dma_start(dst, ada_src(name, b)).then_inc(landed[gb % 4], 16)

            for n, (name, b) in enumerate(ADA_FIRST):
                load_ada(name, b, n)

            def load(s, b, u, j):
                gb = s.g0 + b
                slot = (s.g0 + u) % 4
                sp.wait_ge(raw_used, 2 * (gb - 3))
                k = kt_of(s, u)
                if s.name == "ffn_in":
                    src = s.src(2 * j + u // 2, u % 2)
                elif s.chunks == 1:
                    src = s.src(b)
                else:
                    pair = 2 * j + u // 2 if s.chunks == 2 else j
                    k0 = sum(s.kts[:u % s.chunks])
                    src = s.src.rearrange("(k p) c -> p k c", p=P)[:, k0:k0 + k, ds(pair * COLS, COLS)]
                sp.dma_start(raw[:, slot, 0:k, :], src).then_inc(landed[slot], 16)

            for s in SECS:
                over_blocks(sp, s, lambda b, u, last, j, s=s: load(s, b, u, j))
                if s.name == "g":
                    for m, (name, b) in enumerate(ADA_REST):
                        load_ada(name, b, ada_g0 + m)
            sp.wait_ge(out_sem, 16 * 2)

        def landed_wait(eng, s, b, u):
            gb = s.g0 + u
            j4 = b - u
            eng.wait_ge(landed[gb % 4], 16 * (gb // 4 + 1) + 4 * j4)

        def split_hi(act, s, b, u, h):
            k = kt_of(s, u)
            if h == 0:
                landed_wait(act, s, b, u)
            tt = 2 * b + s.t0 + h
            act.wait_ge(w_used, tt + 1)
            act.activation(whi[:, (s.t0 + 2 * u + h) % 4, 0:k], raw[:, (s.g0 + u) % 4, 0:k, h * P:h * P + P],
                           ACT.Copy).then_inc(hi_ready, 1)

        def split_lo(v, s, b, u, h):
            k = kt_of(s, u)
            slot = (s.t0 + 2 * u + h) % 4
            if h == 0:
                landed_wait(v, s, b, u)
            v.wait_ge(w_used, 2 * b + s.t0 + h + 1)
            v.wait_ge(hi_ready, 2 * b + s.t0 + h + 1)
            v.tensor_tensor(wlo[:, slot, 0:k], raw[:, (s.g0 + u) % 4, 0:k, h * P:h * P + P],
                            whi[:, slot, 0:k].bitcast(F32), ALU.subtract).then_inc(raw_used, 1)

        def split_section(eng, split, s, evac, chain=None, per=0):
            if split and not s.ahead:
                if split is split_lo:
                    eng.wait_ge(raw_used, 2 * s.g0)
                for h in range(2):
                    split(eng, s, 0, 0, h)

            def body(b, u, last, j):
                for h in range(2):
                    if split and not last:
                        split(eng, s, b + 1, u + 1, h)
                    elif split and s.next and s.next.ahead:
                        split(eng, s.next, 0, 0, h)
                if evac and (u + 1) % s.chunks == 0:
                    for h in range(2):
                        evac(b, u, h, j)
            over_blocks(eng, s, body, chain, per)

        def tile_done(eng, s, b, h):
            eng.wait_ge(w_used, 2 * b + s.t0 + h + 5)

        def out_slot(s, u, h):
            if s.chunks == 1:
                return (s.o0 + 2 * u + h) % 4
            if s.chunks == 2:
                return (s.o0 + u // 2 * 2 + h) % 4
            return (s.o0 + h) % 4

        def pe_section(pe, s, rhs, tok_major=False, free=None):
            pe.wait_ge(acc_free, s.o0 + 4)

            def body(b, u, last, j):
                k = kt_of(s, u)
                k0 = sum(s.kts[:u % s.chunks])
                first, final = u % s.chunks == 0, (u + 1) % s.chunks == 0
                for h in range(2):
                    tt = 2 * b + s.t0 + h
                    pe.wait_ge(hi_ready, tt + 1)
                    pe.wait_ge(raw_used, 2 * (b + s.g0) + h + 1)
                    if first:
                        if free:
                            free(b, u, h, j)
                        elif s.chunks == 1:
                            pe.wait_ge(acc_free, 2 * b + s.o0 + h + 1)
                        elif s.chunks == 2:
                            pe.wait_ge(acc_free, 4 * j + s.o0 + u // 2 * 2 + h + 1)
                        else:
                            pe.wait_ge(acc_free, 2 * j + s.o0 + h + 3)
                    slot, q = (s.t0 + 2 * u + h) % 4, out_slot(s, u, h)
                    if tok_major:
                        for tk in range(NT):
                            o_ = acc[:, q, tk * P:tk * P + P]
                            for i in range(k):
                                hh, hl = rhs(i)
                                pe.matmul(o_, hh[:, tk * P:tk * P + P], whi[:, slot, i], start=i == 0, stop=False)
                                pe.matmul(o_, hl[:, tk * P:tk * P + P], whi[:, slot, i], start=False, stop=False)
                                m = pe.matmul(o_, hh[:, tk * P:tk * P + P], wlo[:, slot, i], start=False, stop=i == k - 1)
                    else:
                        for i in range(k):
                            hh, hl = rhs(k0 + i)
                            pe.matmul(acc[:, q, 0:T], whi[:, slot, i], hh, start=first and i == 0, stop=False)
                            pe.matmul(acc[:, q, 0:T], whi[:, slot, i], hl, start=False, stop=False)
                            m = pe.matmul(acc[:, q, 0:T], wlo[:, slot, i], hh, start=False, stop=final and i == k - 1)
                    m.then_inc(w_used, 1)
            over_blocks(pe, s, body)

        def hrhs(k):
            return HH[:, k], HL[:, k]

        def urhs(k):
            return UH[:, k], UL[:, k]

        def yrhs(k):
            return YH[:, k], YL[:, k]

        def hidrhs(k):
            return HIDH[:, k], HIDL[:, k]

        def each(ap, n):
            return bass.AP(tensor=ap.tensor, offset=ap.offset, ap=[ap.ap[0], [0, n], [1, T]])

        MEANS = {}
        norm_list = [("mix", 0, X), ("conv", 1, ACC), ("ffn", 0, X), ("final", 0, X), ("ln1_0", 1, X), ("ln2_0", 1, X),
                     ("ln1_1", 1, X), ("ln2_1", 1, X)]
        NORM = {}
        for n, (name, mean, src) in enumerate(norm_list):
            NORM[name] = (n, mean, sum(m for _, m, _ in norm_list[:n]), src)

        def norm_pe(pe, name):
            n, mean, nm, src = NORM[name]
            if mean:
                pe.wait_ge(n_x, nm + 1)
                for k in range(DT):
                    m = pe.matmul(pm[:, 0, 0:T], ones, src[:, k], start=k == 0, stop=k == DT - 1)
                m.then_inc(n_mean, 1)
            pe.wait_ge(n_sq, n + 1)
            sq = SQ[name]
            for k in range(DT):
                m = pe.matmul(pm[:, 1, 0:T], ones, sq[:, k], start=k == 0, stop=k == DT - 1)
            m.then_inc(n_sum, 1)

        def norm_act(act, name):
            n, mean, nm, src = NORM[name]
            act.wait_ge(n_sum, n + 1)
            act.activation(NR[:, 1], pm[:, 1, 0:T], ACT.Sqrt, bias=sc[:, 1:2] if mean else sc[:, 0:1],
                           scale=1.0 / D).then_inc(n_std, 1)

        def norm_dve(v, c, name, scale, shift, dst):
            n, mean, nm, src = NORM[name]
            sq = SQ[name]
            if mean:
                v.wait_ge(n_mean, nm + 1)
                c.link(v.tensor_scalar(NR[:, 0], pm[:, 0, 0:T], 1.0 / D, None, ALU.mult))
                c.link(v.tensor_tensor(src[:], src[:], each(NR[:, 0], DT), ALU.subtract))
            v.tensor_tensor(sq[:], src[:], src[:], ALU.mult).then_inc(n_sq, 1)
            v.wait_ge(n_std, n + 1)
            c.link(v.reciprocal(NR[:, 1], NR[:, 1]))
            c.link(v.tensor_tensor(sq[:], src[:], each(NR[:, 1], DT), ALU.mult))
            for k in range(DT):
                if shift is None:
                    c.tick(v.tensor_scalar(dst[:, k], sq[:, k], scale(k), None, ALU.mult))
                else:
                    c.tick(v.tensor_scalar(dst[:, k], sq[:, k], scale(k), shift(k), ALU.mult, ALU.add))
            c.wait()

        SQX = ar("SQX", 72, [P, DT, T])
        SQ = {name: SQX for name in NORM}
        SQ["mix"], SQ["conv"] = ACC, H

        ADA2 = at("ADA2", 80, [P, 4 * D])
        SQ2 = ar("SQ2", 78, [P, 8, T])
        NR4 = ar("NR4", 86, [P, NG, T])
        QKV = ar("QKV", 0, [P, 24, T])
        ZA = ar("ZA", 24, [P, 8, T])
        VT = ar("VT", 32, [P, NT, D])
        lm = ar("lm", 84, [P, 7, 2, P])
        gm = ar("gm", 80, [P, 7, P])
        KS = ar("KS", 40, [P, 2, T])
        LF = ar("LF", 42, [P, 2, 3 * P])
        LB = ar("LB", 45, [P, 2, 3 * P])
        DF = ar("DF", 48, [P, 2, 3 * P])
        DB = ar("DB", 51, [P, 2, 3 * P])
        ATT = ar("ATT", 54, [P, 2, 4 * P])
        KDX = ar("KDX", 58, [P, 2, 2 * P])
        AM = ar("AM", 60, [P, 2, 2, 4 * P])
        XI = ar("XI", 68, [P, 2, 4 * P])
        ZI = ar("ZI", 72, [P, 2, 4 * P])
        PS = ar("PS", 76, [P, 2, 4 * P])
        VN = ar("VN", 20, [P, 2, 4 * P])
        RH = ar("RH", 16, [P, 2, 2 * P])
        QK2 = ar("QK2", 0, [P, 8, T])
        VT2 = ar("VT2", 8, [P, NT, D])
        RG = ar("RG", 16, [P, 8, T])
        LA = ar("LA", 24, [P, 8, T])
        LT = ar("LT", 32, [P, 8, T])
        BS = ar("BS", 40, [P, 8, T])
        onet = ar("onet", 48, [P, T])
        gw = ar("gw", 49, [NH, 2, 512])
        glt = ar("glt", 53, [NH, T])
        BH = ar("BH", 54, [P, 2, T])
        QKH = ar("QKH", 56, [P, 2, T])
        VH = ar("VH", 58, [P, NT, T])
        DD = ar("DD", 60, [P, 2, 2, T])
        KQ = ar("KQ", 64, [P, 2, 2, T])
        SS = ar("SS", 68, [P, NT, T])
        XOUT = ar("XOUT", 0, [P, NT, D])

        ws1 = ar("ws1", 91, [P, DT, NH])
        ws2 = ar("ws2", 92, [P, DT, NH])
        ws3 = ar("ws3", 93, [P, DT, NH])

        dt_in, ba_in, gl_in = sem("dt_in"), sem("ba_in"), sem("gl_in")
        dt_p, dt_ok, sp_x, sp_e = sem("dt_p"), sem("dt_ok"), sem("sp_x"), sem("sp_e")
        ez = sem("ez")
        rest_part, rest_sum = sem("rest_part"), sem("rest_sum")
        u_n, u_s, u_hi, u_lo = sem("u_n"), sem("u_s"), sem("u_hi"), sem("u_lo")
        xbc_ok = sem("xbc_ok")
        xs_t, xs_ok, cb_p, cb_ok = sem("xs_t"), sem("xs_ok"), sem("cb_p"), sem("cb_ok")
        l_ok, seg_p, e_ok, m_ok, y_p, y_ok = (sem(k) for k in ("l_ok", "seg_p", "e_ok", "m_ok", "y_p", "y_ok"))
        ysq, ysum, ystd, yn, yhi, ylo = (sem(k) for k in ("ysq", "ysum", "ystd", "yn", "yhi", "ylo"))
        mg_ok, mg_hi, mg_lo = sem("mg_ok"), sem("mg_hi"), sem("mg_lo")
        hid_lo = sem("hid_lo")
        x_hi, x_lo = sem("x_hi"), sem("x_lo")
        mask2 = sem("mask2")
        yz_ok, hid_ok = sem("yz_ok"), sem("hid_ok")
        qkv_ok, ba_p, bet_ok, qkn_ok = (sem(k) for k in ("qkv_ok", "ba_p", "bet_ok", "qkn_ok"))
        l2_sq, l2_sum, l2_std = (sem(k) for k in ("l2_sq", "l2_sum", "l2_std"))
        vt_p, vt_ok, at_ok, am_ok, p_p, ps_ok, vw_p, xz_ok = (sem(k) for k in (
            "vt_p", "vt_ok", "at_ok", "am_ok", "p_p", "ps_ok", "vw_p", "xz_ok"))
        ks_ok, kq_p, gl_l, gs_p, gd_ok, qd_ok, s1_p, vn1, r_p, rh_ok, s2_p, vn2, go_p, go_ok = (sem(k) for k in (
            "ks_ok", "kq_p", "gl_l", "gs_p", "gd_ok", "qd_ok", "s1_p", "vn1", "r_p", "rh_ok", "s2_p", "vn2",
            "go_p", "go_ok"))
        gz, gw_in, gl_p, gl_ok, lg_p, lt_ok, lt_e, bs_ok = (sem(k) for k in (
            "gz", "gw_in", "gl_p", "gl_ok", "lg_p", "lt_ok", "lt_e", "bs_ok"))
        st_ok, dd_ok, ee_ok, kq_ok, sc_p, s_ok, dg_p, dg_ok, bo_p, bo_ok = (sem(k) for k in (
            "st_ok", "dd_ok", "ee_ok", "kq_ok", "sc_p", "s_ok", "dg_p", "dg_ok", "bo_p", "bo_ok"))
        ot_p, ot_ok = sem("ot_p"), sem("ot_ok")
        cs = small("cs", 8)
        bet = small("bet", 2 * 16)[:].rearrange("p (t c) -> p t c", t=NT)
        gd = small("gd", 2 * 16)[:].rearrange("p (t c) -> p t c", t=NT)
        HSRC = [H, H, X, H, X, X, H, X]
        EV = {"xbc": 0, "ffn_in": 24, "a_qkv": 46, "mlp1_0": 70, "mlp1_1": 102}

        def bank(u, i):
            return (pm if u else acc)[:, i]

        def ffn_in_pe(pe):
            s = SEC["ffn_in"]

            def free(b, u, h, j):
                m = 2 * j + u // 2
                if u % 2 == 0:
                    pe.wait_ge(evac_a, 2 * m + EV["ffn_in"] + h - 1)
                else:
                    pe.wait_ge(acc_free, 4 * m + s.o0 + 2 * h + 2)
            pe_section(pe, s, hrhs, free=free)

        @block.gpsimd
        def _(pool):
            c = Chain(pool, gchain)
            c.link(pool.memset(ident[:], 0.0))
            c.link(pool.affine_select(out=ident[:], in_=ident[:], compare_op=ALU.not_equal, fill=1.0, base=0,
                                      pattern=[[-1, P]], channel_multiplier=1))
            pool.nop().then_inc(masks, 1)

            def tri(ap, cm, step, base_):
                c.link(pool.affine_select(out=ap, in_=ap, compare_op=ALU.is_ge, fill=0.0, base=base_,
                                          pattern=[[step, P]], channel_multiplier=cm))
            for m in (maskf, maskb, slo, suo):
                c.link(pool.memset(m[:], 1.0))
            tri(maskf[:, 0:P], -1, 1, 0)
            tri(maskf[:, 2 * P:], -1, 1, 0)
            tri(maskb[:, P:2 * P], 1, -1, 0)
            tri(maskb[:, 2 * P:], 1, -1, 0)
            tri(slo[:, 0:P], 1, -1, -1)
            tri(suo[:, 0:P], -1, 1, -1)
            pool.nop().then_inc(masks, 1)

            def lo_section(s):
                split_section(pool, split_lo, s, None)
            lo_section(SEC["xbc"])
            lo_section(SEC["z"])
            lo_section(SEC["g"])
            pool.wait_ge(ylo, 1)
            for lv in range(7):
                b = 1 << lv
                nb = P // (2 * b)
                for d in range(2):
                    c.link(pool.memset(lm[:, lv, d], 0.0))
                    v = lm[:, lv, d].rearrange("p (n t b) -> p n t b", n=nb, t=2)[:, :, 1 - d]
                    c.link(pool.memset(v, 1.0))
                    lo_, hi_ = (0, b - 1) if d == 0 else (b, 2 * b - 1)
                    c.link(pool.affine_select(out=v, in_=v, compare_op=ALU.is_ge, fill=0.0, base=-lo_,
                                              pattern=[[-2 * b, nb], [0, b]], channel_multiplier=1))
                    c.link(pool.affine_select(out=v, in_=v, compare_op=ALU.is_ge, fill=0.0, base=hi_,
                                              pattern=[[2 * b, nb], [0, b]], channel_multiplier=-1))
            c.link(pool.tensor_tensor(gm[:], lm[:, :, 0], lm[:, :, 1], ALU.add))
            pool.nop().then_inc(mask2, 1)
            lo_section(SEC["a_qkv"])
            with pool.Fori(0, A_HEADS // 2) as j:
                c.loop(j, 0, A_HEADS // 2)
                for lv in range(7):
                    for u in range(2):
                        if lv == 0:
                            pool.wait_ge(at_ok, 2 * j + u + 1)
                        if lv >= 2:
                            pool.wait_ge(p_p, 14 * j + 2 * (lv - 2) + u + 1)
                        if lv == 2:
                            pool.wait_ge(xz_ok, 14 * j + u + 1)
                        m = lm[:, lv]
                        mask = bass.AP(tensor=m.tensor, offset=m.offset, ap=[m.ap[0], [P, 2], [0, 2], [1, P]])
                        pool.tensor_tensor(AM[:, u, lv % 2].rearrange("p (d t c) -> p d t c", d=2, t=2),
                                           ATT[:, u].rearrange("p (d t c) -> p d t c", d=2, t=2), mask,
                                           ALU.mult).then_inc(am_ok, 1)
                c.done()
            pool.wait_ge(n_hl, 6)
            pool.memset(gw[:], 0.0).then_inc(gz, 1)
            pool.sem_inc(dd_ok, 1)
            with pool.Fori(0, B_HEADS) as h:
                c.loop(h, 0, B_HEADS)
                for lv in range(8):
                    b = 1 << lv
                    nb = T // (2 * b)
                    if lv == 0:
                        pool.wait_ge(st_ok, h + 1)
                    pool.wait_ge(kq_ok, 8 * h + lv + 1)

                    def half(ap, side):
                        return ap.rearrange("p (n t b) -> p n t b", n=nb, t=2)[:, :, side]

                    def edge(ap, side, i):
                        e = half(ap, side)[:, :, i:i + 1]
                        return bass.AP(tensor=e.tensor, offset=e.offset, ap=[e.ap[0], [2 * b, nb], [0, b]])
                    kd, qd = DD[:, lv % 2, 0], DD[:, lv % 2, 1]
                    f, r = BH[:, 0], BH[:, 1]
                    pool.tensor_tensor(half(kd, 0), edge(f, 0, b - 1), half(f, 0), ALU.subtract)
                    pool.tensor_tensor(half(kd, 1), edge(r, 1, 0), half(r, 1), ALU.subtract)
                    pool.tensor_tensor(half(qd, 0), half(r, 0), edge(r, 1, 0), ALU.subtract)
                    pool.tensor_tensor(half(qd, 1), half(f, 1), edge(f, 0, b - 1), ALU.subtract).then_inc(dd_ok, 1)
                c.done()

        @block.scalar
        def _(act):
            c = Chain(act, achain)
            for ap, p0, i, m in pieces:
                act.dma_start(PRW[p0:p0 + m, i, :], ap).then_inc(par_in, 16)
            act.dma_start(dtb[:, 0:NH], bcast(a["dt_bias"][0], NH)).then_inc(dt_in, 16)
            act.dma_start(dtb[:, NH:], bcast(a["a_log"][0], NH)).then_inc(dt_in, 16)
            act.dma_start(dsk[:, 0:NH], bcast(a["d_skip"][0], NH)).then_inc(dt_in, 16)
            act.dma_start(gab[:, 0:16], bcast(a["a_dt_bias_2"][0].rearrange("d h -> (d h)"), 16)).then_inc(dt_in, 16)
            act.dma_start(gab[:, 16:32], bcast(a["a_alog_2"][0].rearrange("d h -> (d h)"), 16)).then_inc(dt_in, 16)
            for w_, src, off in ((ws1, w_in, OFF_DT), (ws2, a_in, A_BA), (ws3, b_in, B_GL)):
                act.dma_start(w_[:], src.rearrange("(k p) c -> p k c", p=P)[:, :, off:off + NH]).then_inc(dt_in, 16)
            for q in range(4):
                act.wait_ge(xt_p, q + 1)
                act.activation(X[:, 2 * q:2 * q + 2], acc[:, q].rearrange("p (d t) -> p d t", d=2), ACT.Copy)\
                   .then_inc(x_ok, 1)
            act.wait_ge(par_ok, 2)
            act.activation(cs[:], pc("c", 0, 8), ACT.Silu).then_inc(silu_c, 1)
            norm_act(act, "mix")

            def h_hi(n):
                act.wait_ge(n_h, n + 1)
                act.activation(HH[:], HSRC[n][:], ACT.Copy).then_inc(n_hh, 1)
            h_hi(0)

            def conv_b(b, u, h, j):
                tile_done(act, SEC["conv_b"], b, h)
                act.activation(G[:, ds(2 * b + h, 1)], acc[:, out_slot(SEC["conv_b"], u, h), 0:T], ACT.Sigmoid)\
                   .then_inc(acc_free, 1)
            split_section(act, split_hi, SEC["conv_b"], conv_b)
            split_section(act, split_hi, SEC["conv_a"], None)
            act.wait_ge(sp_x, 1)
            act.activation(spt[2][:], spt[1][:], ACT.Exp, scale=-1.0).then_inc(sp_e, 1)
            act.wait_ge(dt_in, 16 * 8)
            act.activation(dtb[:, NH:], dtb[:, NH:], ACT.Exp).then_inc(ez, 1)
            act.activation(gab[:, 16:32], gab[:, 16:32], ACT.Exp).then_inc(ez, 1)

            def conv_first(s, dst, w, bias):
                def evac(b, u, h, j):
                    tile_done(act, s, b, h)
                    act.activation(dst[:, ds(2 * b + h, 1)], acc[:, out_slot(s, u, h), 0:T], ACT.Identity,
                                   scale=pc(w[0], 2 * b + h + w[1]), bias=pc(bias, 2 * b + h) if bias else 0.0)\
                       .then_inc(evac_a, 1)
                return evac
            split_section(act, split_hi, SEC["xbc"], conv_first(SEC["xbc"], XBC, ("ssm_conv_w", 3 * 24), "ssm_conv_b"))

            def table_evac(s, dst, func):
                def evac(b, u, h, j):
                    tile_done(act, s, b, h)
                    act.activation(dst[:, ds(2 * b + h, 1)], acc[:, out_slot(s, u, h), 0:T], func)\
                       .then_inc(acc_free, 1)
                return evac
            split_section(act, split_hi, SEC["z"], table_evac(SEC["z"], Z, ACT.Silu))
            act.wait_ge(acc_free, SEC["xbc"].o0 + 24 + 4)
            act.activation(XBC[:], XBC[:], ACT.Silu).then_inc(xbc_ok, 1)
            split_section(act, split_hi, SEC["g"], table_evac(SEC["g"], G, ACT.Sigmoid))
            norm_act(act, "conv")
            act.wait_ge(u_n, 1)
            act.activation(H[:], H[:], ACT.Silu).then_inc(u_s, 1)
            act.wait_ge(u_s, 1)
            act.activation(UH[:], H[:], ACT.Copy).then_inc(u_hi, 1)
            act.sem_inc(e_ok, 2)
            for gi in range(NG):
                with act.Fori(0, 4) as j:
                    for u in range(2):
                        act.wait_ge(seg_p, 2 * j + 8 * gi + u + 3)
                        act.wait_ge(y_p, 2 * j + 8 * gi + u + 1)
                        act.activation(ES[:, u], pm[:, u, 0:3 * P], ACT.Exp).then_inc(e_ok, 1)
            act.wait_ge(ysum, 1)
            act.activation(NR4[:], pm[:, 0:2].rearrange("p b (g t) -> p (b g) t", g=2), ACT.Sqrt,
                           bias=sc[:, 0:1], scale=1.0 / (D_INNER // NG)).then_inc(ystd, 1)
            act.wait_ge(yn, 1)
            act.activation(YH[:], XBC[:, 0:16], ACT.Copy).then_inc(yhi, 1)
            split_section(act, split_hi, SEC["conv_out"], None)
            split_section(act, split_hi, SEC["ssm_out"], None)
            act.wait_ge(mg_ok, 1)
            act.activation(UH[:], H[:], ACT.Copy).then_inc(mg_hi, 1)
            split_section(act, split_hi, SEC["w_out"], None)
            norm_act(act, "ffn")
            h_hi(1)

            def ffn_gate(b, u, h, j):
                if u % 2 == 0:
                    tile_done(act, SEC["ffn_in"], b, h)
                    q = (u // 2) * 2 + h
                    act.wait_ge(acc_free, 2 * b + SEC["ffn_in"].o0 + 2 * h - 2)
                    act.activation(TMP[:, q], acc[:, out_slot(SEC["ffn_in"], u, h), 0:T], ACT.Silu)\
                       .then_inc(evac_a, 1)
            split_section(act, split_hi, SEC["ffn_in"], ffn_gate)
            split_section(act, split_hi, SEC["ffn_down"], None)
            norm_act(act, "final")
            h_hi(2)
            split_section(act, split_hi, SEC["a_qkv"], conv_first(SEC["a_qkv"], QKV, ("a_conv", 2 * 24), None))
            split_section(act, split_hi, SEC["a_z"], table_evac(SEC["a_z"], ZA, ACT.Silu))
            act.wait_ge(acc_free, SEC["a_qkv"].o0 + 24 + 4)
            act.activation(QKV[:], QKV[:], ACT.Silu).then_inc(qkv_ok, 1)
            act.wait_ge(ba_p, 1)
            act.activation(bet[:], pm[:, 2, 0:2 * NH].rearrange("p (t c) -> p t c", t=NT)[:, :, 0:16], ACT.Sigmoid)\
               .then_inc(bet_ok, 1)
            act.wait_ge(sp_x, 2)
            act.activation(spt[2][:, 0:32], spt[1][:, 0:32], ACT.Exp, scale=-1.0).then_inc(sp_e, 1)
            def l2_act(i, scale, bias):
                act.wait_ge(l2_sum, i + 1)
                act.activation(SQX[:], acc[:].rearrange("p b (h t) -> p (b h) t", h=2), ACT.Sqrt,
                               bias=bias, scale=scale).then_inc(l2_std, 1)
            l2_act(0, 1.0, sc[:, 0:1])
            l2_act(1, 1.0, sc[:, 0:1])
            for q in range(4):
                act.wait_ge(vt_p, q + 1)
                act.activation(VT[:, q // 2, ds((q % 2) * 512, 512)], pm[:, q], ACT.Copy).then_inc(vt_ok, 1)
            with act.Fori(0, A_HEADS // 2) as j:
                for u in range(2):
                    act.wait_ge(go_p, 2 * j + u + 1)
                    act.activation(KS[:, u], QKV[:, ds(2 * j + u + 8, 1)], ACT.Copy).then_inc(ks_ok, 1)
                for u in range(2):
                    act.wait_ge(gs_p, 2 * j + u + 1)
                    act.activation(DF[:, u], bank(u, 2)[:, 0:3 * P], ACT.Exp)
                    act.activation(DB[:, u], bank(u, 3)[:, 0:3 * P], ACT.Exp).then_inc(gd_ok, 1)
                for lv in range(1, 7):
                    for u in range(2):
                        act.wait_ge(p_p, 14 * j + 2 * lv + u + 1)
                        act.activation(PS[:, u], bank(u, 0), ACT.Copy).then_inc(ps_ok, 1)
            l2_act(2, 1.0 / P, sc[:, 0:1])
            h_hi(3)
            split_section(act, split_hi, SEC["a_out"], None)
            norm_act(act, "ln1_0")
            h_hi(4)

            def mlp(k):
                s = SEC[f"mlp1_{k}"]

                def relu(b, u, h, j):
                    q = (2 * u + h) % 4
                    tile_done(act, s, b, h)
                    act.wait_ge(hid_lo, 2 * b + 32 * k + h + 1)
                    act.activation(TMP[:, q], acc[:, out_slot(s, u, h), 0:T], ACT.Relu).then_inc(acc_free, 1)
                    act.wait_ge(acc_free, 2 * b + s.o0 + h + 5)
                    act.activation(HIDH[:, ds(2 * b + h, 1)], TMP[:, q], ACT.Square).then_inc(evac_a, 1)
                split_section(act, split_hi, s, relu)
                split_section(act, split_hi, SEC[f"mlp2_{k}"], None)
                norm_act(act, f"ln2_{k}")
            mlp(0)
            h_hi(5)

            act.wait_ge(gz, 1)
            for d in range(2):
                act.dma_start(gw[16 * d:16 * d + 16, d, :], a["b_gate_w2_2"][0, d]).then_inc(gw_in, 16)

            def b_qk(b, u, h, j):
                tile_done(act, SEC["b_qk"], b, h)
                act.activation(QK2[:, ds(2 * b + h, 1)], acc[:, out_slot(SEC["b_qk"], u, h), 0:T], ACT.Copy,
                               scale=P ** -0.5 if b < 2 else 1.0).then_inc(acc_free, 1)

            def b_v(b, u, h, j):
                tile_done(act, SEC["b_v"], b, h)
                act.activation(VT2[:, :, ds((2 * b + h) * P, P)],
                               acc[:, out_slot(SEC["b_v"], u, h), 0:T].rearrange("p (t c) -> p t c", t=NT), ACT.Copy)\
                   .then_inc(acc_free, 1)
            split_section(act, split_hi, SEC["b_qk"], b_qk)
            split_section(act, split_hi, SEC["b_v"], b_v)
            split_section(act, split_hi, SEC["b_r"], table_evac(SEC["b_r"], RG, ACT.Silu))
            act.wait_ge(gl_p, 1)
            act.activation(glt[:], pm[0:NH, 2, 0:T], ACT.Copy).then_inc(gl_ok, 1)
            act.wait_ge(lt_ok, 1)
            act.activation(LT[:], LT[:], ACT.Exp, scale=-1.0).then_inc(lt_e, 1)
            act.wait_ge(lt_e, 1)
            act.activation(LT[:], LT[:], ACT.Ln, bias=1.0).then_inc(lt_e, 1)
            act.sem_inc(ee_ok, 1)
            with act.Fori(0, B_HEADS) as h:
                act.wait_ge(bs_ok, 1)
                act.wait_ge(kq_ok, 8 * h + 2)
                act.wait_ge(dd_ok, 8 * h + 1)
                act.wait_ge(bo_p, h + 1)
                act.activation(BH[:], BS[:].rearrange("p (d h) t -> p d h t", d=2)[:, :, ds(h, 1)], ACT.Copy)
                act.activation(QKH[:, 1], QK2[:, ds(h, 1)], ACT.Copy)
                act.activation(QKH[:, 0], QK2[:, ds(h + 4, 1)], ACT.Copy)
                act.activation(VH[:], VT2[:, :, ds(h * T, T)], ACT.Copy).then_inc(st_ok, 1)
                for lv in range(8):
                    act.wait_ge(dd_ok, 8 * h + lv + 2)
                    act.activation(DD[:, lv % 2], DD[:, lv % 2], ACT.Exp, scale=1.0 / 16).then_inc(ee_ok, 1)
            l2_act(3, 1.0 / T, sc[:, 0:1])
            h_hi(6)
            split_section(act, split_hi, SEC["b_out"], None)
            norm_act(act, "ln1_1")
            h_hi(7)
            mlp(1)
            for q in range(4):
                act.wait_ge(ot_p, q + 1)
                act.activation(XOUT[:, q // 2, ds((q % 2) * 512, 512)], pm[:, q], ACT.Copy).then_inc(ot_ok, 1)
            for tk in range(NT):
                act.wait_ge(ot_ok, 2 * tk + 2)
                act.dma_start(out[0].rearrange("(t p) d -> p t d", p=P)[:, tk], XOUT[:, tk]).then_inc(out_sem, 16)

        @block.vector
        def _(v):
            c = Chain(v, vchain)
            c.link(v.memset(sc[:, 0:1], RMS_EPS))
            c.link(v.memset(sc[:, 1:2], LN_EPS))
            for bk in range(2):
                v.wait_ge(par_t, bk + 1)
                n = min(512, NPAR - 512 * bk)
                v.tensor_copy(par[:, 512 * bk:512 * bk + n], pm[:, bk, 0:n]).then_inc(par_ok, 1)
            v.wait_ge(par_ok, 2)
            v.wait_ge(silu_c, 1)

            def ada_step(dst, src, k, first, free):
                if first:
                    ins = v.tensor_scalar(dst, src, cs[:, k:k + 1], None, ALU.mult)
                else:
                    ins = v.scalar_tensor_tensor(dst, src, cs[:, k:k + 1], dst, ALU.mult, ALU.add)
                if free:
                    ins.then_inc(raw_used, 2)
                else:
                    c.link(ins)

            for n, (name, b) in enumerate(ADA_FIRST):
                v.wait_ge(landed[n % 4], 16 * (n // 4 + 1))
                if n:
                    v.wait_ge(raw_used, 2 * n)
                ada_step(ADA[:], raw[:, n % 4].rearrange("p k c -> p (k c)"), b, b == 0, True)
            v.wait_ge(raw_used, 2 * len(ADA_FIRST))
            v.nop().then_inc(ada_part, 1)
            v.wait_ge(ada_sum, 1)
            c.link(v.tensor_tensor(MOD[:, 0:16], pm[:, 3, 0:16], pc("b_ada_mix", 0, 16), ALU.add))
            c.link(v.scalar_tensor_tensor(MOD[:, 8:16], MOD[:, 8:16], 1.0, pc("norm_mix_w", 0, 8), ALU.add, ALU.mult))
            v.wait_ge(x_ok, 4)
            norm_dve(v, c, "mix", lambda k: MOD[:, 8 + k:9 + k], lambda k: MOD[:, k:k + 1], H)

            def h_lo(n):
                v.nop().then_inc(n_h, 1)
                v.wait_ge(n_hh, n + 1)
                v.tensor_tensor(HL[:], HSRC[n][:], HH[:].bitcast(F32), ALU.subtract).then_inc(n_hl, 1)
            h_lo(0)
            c.link(v.memset(UP[:], 0.0))
            split_section(v, split_lo, SEC["conv_b"], None)

            def conv_a(b, u, h, j):
                tile_done(v, SEC["conv_a"], b, h)
                v.tensor_tensor(UP[:, ds(2 * b + h, 1), CW - 1:], acc[:, out_slot(SEC["conv_a"], u, h), 0:T],
                                G[:, ds(2 * b + h, 1)], ALU.mult).then_inc(acc_free, 1)
            v.wait_ge(acc_free, 8 + 4)
            split_section(v, split_lo, SEC["conv_a"], conv_a)

            def softplus(n, x, dst):
                ax, e, s_, = spt[1][:, 0:x.shape[1]], spt[2][:, 0:x.shape[1]], spt[3][:, 0:x.shape[1]]
                c.link(v.scalar_tensor_tensor(ax, x, -1.0, x, ALU.mult, ALU.max))
                v.nop().then_inc(sp_x, 1)
                v.wait_ge(sp_e, n + 1)
                c.link(v.tensor_scalar(ax, e, 2.0, None, ALU.add))
                c.link(v.reciprocal(ax, ax))
                c.link(v.tensor_tensor(e, e, ax, ALU.mult))
                c.link(v.tensor_tensor(s_, e, e, ALU.mult))
                c.link(v.tensor_scalar(ax, s_, 1.0 / 17, None, ALU.mult))
                for k in range(7, 0, -1):
                    c.link(v.scalar_tensor_tensor(ax, ax, 1.0 / (2 * k + 1), s_, ALU.add, ALU.mult))
                c.link(v.scalar_tensor_tensor(ax, ax, 1.0, e, ALU.add, ALU.mult))
                c.link(v.tensor_scalar(ax, ax, 2.0, None, ALU.mult))
                c.link(v.scalar_tensor_tensor(dst, x, 0.0, ax, ALU.max, ALU.add))

            v.wait_ge(dt_in, 16 * 8)
            v.wait_ge(dt_p, 1)
            for tk in range(NT):
                c.link(v.tensor_tensor(spt[0][:, tk * NH:tk * NH + NH], pm[:, 2, tk * NH:tk * NH + NH],
                                       dtb[:, 0:NH], ALU.add))
            softplus(0, spt[0][:, 0:2 * NH], dtt[:])
            v.wait_ge(ez, 1)
            for tk in range(NT):
                c.link(v.scalar_tensor_tensor(dat[:, tk * NH:tk * NH + NH], dtt[:, tk * NH:tk * NH + NH], -1.0,
                                              dtb[:, NH:], ALU.mult, ALU.mult))
            c.link(v.tensor_copy(dsk[0:64, NH:], dsk[0:64, 0:NH:2]))
            c.link(v.tensor_copy(dsk[64:P, NH:], dsk[64:P, 1:NH:2]))

            def conv_rest(s, dst, w, taps):
                def evac(b, u, h, j):
                    i = 2 * b + h
                    q = acc[:, out_slot(s, u, h), :]
                    v.wait_ge(evac_a, EV[s.name] + 2 * b + h + 1)
                    for n, (tap, sh) in enumerate(taps):
                        o0_, o1 = (sh, T) if sh > 0 else (0, T + sh)
                        d_ = dst[:, ds(i, 1), o0_:o1]
                        x_ = q[:, o0_ - sh:o1 - sh]
                        ins = v.scalar_tensor_tensor(d_, x_, pc(w, i + 24 * tap), d_, ALU.mult, ALU.add)
                        if n == len(taps) - 1:
                            ins.then_inc(acc_free, 1)
                        else:
                            c.link(ins)
                return evac
            split_section(v, None, SEC["xbc"], conv_rest(SEC["xbc"], XBC, "ssm_conv_w", [(2, 1), (1, 2), (0, 3)]),
                          c, 4 * 2 * 2)
            with v.Fori(0, DT // 2) as j:
                c.loop(j, 2 * CW, DT // 2)
                for w_ in range(CW):
                    for u in range(2):
                        src = UP[:, ds(2 * j + u, 1), w_:w_ + T]
                        d_ = ACC[:, ds(2 * j + u, 1)]
                        wt = pc("conv_dw_w", 2 * j + u + w_ * DT)
                        if w_ == 0:
                            c.tick(v.tensor_scalar(d_, src, wt, pc("conv_dw_b", 2 * j + u), ALU.mult, ALU.add))
                        else:
                            c.wait(1)
                            c.tick(v.scalar_tensor_tensor(d_, src, wt, d_, ALU.mult, ALU.add))
                c.done()
            c.wait()
            v.nop().then_inc(n_x, 1)
            norm_dve(v, c, "conv", lambda k: pc("conv_ln_w", k), lambda k: pc("conv_ln_b", k), H)
            v.nop().then_inc(u_n, 1)
            v.wait_ge(u_hi, 1)
            v.tensor_tensor(UL[:], H[:], UH[:].bitcast(F32), ALU.subtract).then_inc(u_lo, 1)
            v.wait_ge(w_used, SEC["g"].t0 + 16 + 4)
            for n, (name, b) in enumerate(ADA_REST):
                gb = ada_g0 + n
                v.wait_ge(landed[gb % 4], 16 * (gb // 4 + 1))
                v.wait_ge(raw_used, 2 * gb)
                r = raw[:, gb % 4].rearrange("p k c -> p (k c)")
                if b < 8:
                    ada_step(ADA2[:, D:3 * D], r, b, b == 0, True)
                else:
                    dst = ADA2[:, 0:D] if name == "w_ada_mix" else ADA2[:, 3 * D:]
                    ada_step(dst, r[:, 0:D], 2 * (b - 8), b == 8, False)
                    ada_step(dst, r[:, D:], 2 * (b - 8) + 1, False, True)
            v.wait_ge(raw_used, 2 * (ada_g0 + len(ADA_REST)))
            v.nop().then_inc(rest_part, 1)
            v.wait_ge(rest_sum, 1)
            c.link(v.tensor_tensor(MOD[:, 16:24], pm[:, 3, 0:8], pc("b_ada_mix", 16, 8), ALU.add))
            c.link(v.tensor_tensor(MOD[:, 24:48], pm[:, 3, 8:32], pc("b_ada_ffn", 0, 24), ALU.add))
            c.link(v.scalar_tensor_tensor(MOD[:, 32:40], MOD[:, 32:40], 1.0, pc("norm_ffn_w", 0, 8), ALU.add, ALU.mult))
            v.nop().then_inc(mod_ok, 1)
            for q in range(8):
                v.wait_ge(xs_t, q + 1)
                v.tensor_copy(XT[:, q // 4, 512 * (q % 4):512 * (q % 4) + 512], pm[:, q % 3]).then_inc(xs_ok, 1)
            for gi in range(NG):
                v.wait_ge(cb_p, gi + 1)
                v.tensor_tensor(CB[:, gi], acc[:, gi, 0:3 * P], maskf[:], ALU.mult).then_inc(cb_ok, 1)
            v.wait_ge(xs_ok, 8)
            v.wait_ge(cb_ok, 4)
            v.sem_inc(y_ok, 1)
            for gi in range(NG):
                with v.Fori(0, 4) as j:
                    c.loop(j, 4, 4)
                    for u in range(2):
                        h = 2 * j + 8 * gi + u
                        v.wait_ge(seg_p, h + 1)
                        v.tensor_scalar(LS[:, u, 0:P], slo[:, 0:P], dat[:, ds(h, 1)], None, ALU.mult)
                        v.tensor_scalar(LS[:, u, P:], slo[:], dat[:, ds(h + NH, 1)], None, ALU.mult).then_inc(l_ok, 1)
                    for u in range(2):
                        h = 2 * j + 8 * gi + u
                        v.wait_ge(y_p, h + 1)
                        for tk in range(NT):
                            c.tick(v.tensor_scalar(XD[:, u, tk], XT[:, tk, ds(h * 64, 64)],
                                                   dtt[:, ds(h + tk * NH, 1)], None, ALU.mult))
                    for u in range(2):
                        h = 2 * j + 8 * gi + u
                        v.wait_ge(e_ok, h + 3)
                        c.wait(2 * (1 - u))
                        v.tensor_tensor(ES[:, u], ES[:, u], CB[:, gi], ALU.mult).then_inc(m_ok, 1)
                    v.wait_ge(y_p, 2 * j + 8 * gi + 4)
                    yt = XBC[:, ds(j + 4 * gi, 1)]
                    ins = v.scalar_tensor_tensor(yt, yt, dsk[:, ds(j + 4 * gi + NH, 1)], pm[:, 2, 0:T], ALU.mult, ALU.add)
                    ins.then_inc(y_ok, 1)
                    v.wait_ge(y_ok, j + 4 * gi + 2)
                    v.tensor_tensor(yt, yt, Z[:, ds(j + 4 * gi, 1)], ALU.mult).then_inc(yz_ok, 1)
                    c.done()
            v.wait_ge(yz_ok, 16)
            c.link(v.tensor_tensor(H[:], XBC[:, 0:8], XBC[:, 0:8], ALU.mult))
            v.tensor_tensor(SQ2[:], XBC[:, 8:16], XBC[:, 8:16], ALU.mult).then_inc(ysq, 1)
            v.wait_ge(ystd, 1)
            c.link(v.reciprocal(NR4[:], NR4[:]))
            for gi in range(NG):
                c.tick(v.tensor_tensor(XBC[:, 4 * gi:4 * gi + 4], XBC[:, 4 * gi:4 * gi + 4], each(NR4[:, gi], 4), ALU.mult))
            c.wait()
            for k in range(16):
                c.tick(v.tensor_scalar(XBC[:, k], XBC[:, k], pc("ssm_norm_w", k), None, ALU.mult))
            c.wait()
            v.nop().then_inc(yn, 1)
            v.wait_ge(yhi, 1)
            v.tensor_tensor(YL[:], XBC[:, 0:16], YH[:].bitcast(F32), ALU.subtract).then_inc(ylo, 1)

            def conv_out(b, u, h, j):
                tile_done(v, SEC["conv_out"], b, h)
                i = 2 * b + h
                v.tensor_tensor(H[:, ds(i, 1)], acc[:, out_slot(SEC["conv_out"], u, h), 0:T], G[:, ds(i, 1)], ALU.mult)\
                 .then_inc(acc_free, 1)
            split_section(v, split_lo, SEC["conv_out"], conv_out)

            def ssm_out(b, u, h, j):
                s = SEC["ssm_out"]
                tile_done(v, s, b, h)
                i = 4 * j + 2 * (u // 2) + h
                gt = G[:, ds(i + 8, 1)]
                v.tensor_tensor(gt, acc[:, out_slot(s, u, h), 0:T], gt, ALU.mult).then_inc(acc_free, 1)
                v.wait_ge(acc_free, 4 * j + s.o0 + 2 * (u // 2) + h + 5)
                c.tick(v.tensor_tensor(H[:, ds(i, 1)], H[:, ds(i, 1)], gt, ALU.add))
            v.wait_ge(acc_free, SEC["ssm_out"].o0 + 4)
            split_section(v, split_lo, SEC["ssm_out"], ssm_out, c, 4)
            c.wait()
            v.nop().then_inc(mg_ok, 1)
            v.wait_ge(mg_hi, 1)
            v.tensor_tensor(UL[:], H[:], UH[:].bitcast(F32), ALU.subtract).then_inc(mg_lo, 1)

            def residual(s, scale):
                def evac(b, u, h, j):
                    tile_done(v, s, b, h)
                    i = 2 * b + h if s.chunks == 1 else 2 * j + h
                    xt_, ot = X[:, ds(i, 1)], acc[:, out_slot(s, u, h), 0:T]
                    if scale is None:
                        v.scalar_tensor_tensor(xt_, xt_, ALPHA, ot, ALU.mult, ALU.add).then_inc(acc_free, 1)
                    else:
                        v.scalar_tensor_tensor(xt_, ot, MOD[:, ds(i + scale, 1)], xt_, ALU.mult, ALU.add)\
                         .then_inc(acc_free, 1)
                return evac
            split_section(v, split_lo, SEC["w_out"], residual(SEC["w_out"], 16))
            v.wait_ge(acc_free, SEC["ffn_in"].o0 + 4)
            norm_dve(v, c, "ffn", lambda k: MOD[:, 32 + k:33 + k], lambda k: MOD[:, 24 + k:25 + k], H)
            h_lo(1)

            def ffn_up(b, u, h, j):
                s = SEC["ffn_in"]
                if u % 2 == 1:
                    tile_done(v, s, b, h)
                    q = (u // 2) * 2 + h
                    pair2 = 4 * j + 2 * (u // 2) + h
                    v.wait_ge(evac_a, EV["ffn_in"] + 4 * j + 2 * (u // 2) + h + 1)
                    v.tensor_tensor(TMQ[:, q], acc[:, out_slot(s, u, h), 0:T], TMP[:, q], ALU.mult)\
                     .then_inc(acc_free, 2)
                    v.wait_ge(acc_free, 8 * j + s.o0 + 4 * (u // 2) + 2 * h + 6)
                    c.link(v.tensor_copy(HIDH[:, ds(pair2, 1)], TMQ[:, q]))
                    c.tick(v.tensor_tensor(HIDL[:, ds(pair2, 1)], TMQ[:, q],
                                           HIDH[:, ds(pair2, 1)].bitcast(F32), ALU.subtract))
                    c.wait()
            split_section(v, split_lo, SEC["ffn_in"], ffn_up, c, 8)
            v.nop().then_inc(hid_ok, 1)
            split_section(v, split_lo, SEC["ffn_down"], residual(SEC["ffn_down"], 40))
            v.wait_ge(acc_free, SEC["a_qkv"].o0 + 4)
            norm_dve(v, c, "final", lambda k: pc("final_norm_w", k), None, X)
            h_lo(2)
            split_section(v, None, SEC["a_qkv"],
                          conv_rest(SEC["a_qkv"], QKV, "a_conv", [(0, 2), (1, 1), (3, -1), (4, -2)]), c, 4 * 2 * 3)
            split_section(v, split_lo, SEC["a_z"], None)
            v.wait_ge(ba_p, 1)
            v.wait_ge(bet_ok, 1)
            for tk in range(NT):
                c.link(v.tensor_tensor(spt[0][:, 16 * tk:16 * tk + 16], pm[:, 2, NH * tk + 16:NH * tk + NH],
                                       gab[:, 0:16], ALU.add))
            softplus(1, spt[0][:, 0:32], gd[:].rearrange("p t c -> p (t c)"))
            v.wait_ge(ez, 2)
            for tk in range(NT):
                c.link(v.scalar_tensor_tensor(gd[:, tk], gd[:, tk], -1.0, gab[:, 16:32], ALU.mult, ALU.mult))
            v.wait_ge(qkv_ok, 1)
            for i in range(2):
                q8 = QKV[:, 8 * i:8 * i + 8]
                v.tensor_tensor(SQX[:], q8, q8, ALU.mult).then_inc(l2_sq, 1)
                v.wait_ge(l2_std, i + 1)
                c.link(v.reciprocal(SQX[:], SQX[:]))
                flat = "p k t -> p (k t)"
                c.link(v.scalar_tensor_tensor(q8.rearrange(flat), q8.rearrange(flat), P ** -0.5 if i == 0 else 1.0,
                                              SQX[:].rearrange(flat), ALU.mult, ALU.mult))
            v.nop().then_inc(qkn_ok, 1)
            v.wait_ge(vt_ok, 4)
            v.wait_ge(mask2, 1)
            v.sem_inc(go_ok, 2)
            with v.Fori(0, A_HEADS // 2) as j:
                NK = 2 * (2 + 3) + 2 * 6
                c.loop(j, NK, A_HEADS // 2)

                def gcol(t_, d, tk, u):
                    return t_[:, tk, ds(2 * j + u + 8 * d, 1)]
                for u in range(2):
                    v.wait_ge(go_p, 2 * j + u + 1)
                    v.tensor_scalar(LF[:, u, 0:P], slo[:, 0:P], gcol(gd, 0, 0, u), None, ALU.mult)
                    v.tensor_scalar(LF[:, u, P:], slo[:], gcol(gd, 0, 1, u), None, ALU.mult)
                    v.tensor_scalar(LB[:, u, 0:P], suo[:, 0:P], gcol(gd, 1, 1, u), None, ALU.mult)
                    v.tensor_scalar(LB[:, u, P:], suo[:], gcol(gd, 1, 0, u), None, ALU.mult).then_inc(gl_l, 1)
                for u in range(2):
                    kk, qk = bank(u, 0), bank(u, 1)
                    v.wait_ge(gd_ok, 2 * j + u + 1)
                    c.tick(v.tensor_tensor(DF[:, u], DF[:, u], maskf[:], ALU.mult))
                    c.link(v.tensor_tensor(DB[:, u], DB[:, u], maskb[:], ALU.mult))
                    v.wait_ge(kq_p, 2 * j + u + 1)
                    for n, (dd_, d0, tk, d) in enumerate(((DF, 0, 0, 0), (DF, 2, 1, 0), (DB, 2, 0, 1), (DB, 1, 1, 1))):
                        ins = v.scalar_tensor_tensor(ATT[:, u, n * P:n * P + P], dd_[:, u, d0 * P:d0 * P + P],
                                                     gcol(bet, d, tk, u), kk[:, (0 if tk == 0 else 3) * P:][:, 0:P],
                                                     ALU.mult, ALU.mult)
                    c.tick(v.tensor_tensor(KDX[:, u, 0:P], DF[:, u, P:2 * P], kk[:, P:2 * P], ALU.mult))
                    v.tensor_tensor(KDX[:, u, P:], DB[:, u, 0:P], kk[:, 2 * P:3 * P], ALU.mult).then_inc(at_ok, 1)
                    v.wait_ge(at_ok, 2 * j + u + 1)
                    c.tick(v.tensor_tensor(DF[:, u, 0:2 * P], DF[:, u, 0:2 * P], qk[:, 0:2 * P], ALU.mult))
                    c.tick(v.tensor_tensor(DF[:, u, 2 * P:], DF[:, u, 2 * P:], qk[:, 3 * P:], ALU.mult))
                    v.tensor_tensor(DB[:, u, 0:2 * P], DB[:, u, 0:2 * P], qk[:, 2 * P:], ALU.mult)
                    v.tensor_tensor(DB[:, u, 2 * P:], DB[:, u, 2 * P:], qk[:, 0:P], ALU.mult).then_inc(qd_ok, 1)
                id4 = bass.AP(tensor=ident[:].tensor, offset=ident[:].offset, ap=[ident[:].ap[0], [0, 4], [1, P]])
                for lv in range(7):
                    for u in range(2):
                        x4 = XI[:, u].rearrange("p (s c) -> p s c", s=4)
                        z4 = ZI[:, u].rearrange("p (s c) -> p s c", s=4)
                        if lv == 0:
                            v.wait_ge(am_ok, 14 * j + u + 1)
                            c.tick(v.tensor_tensor(z4, id4, AM[:, u, 0].rearrange("p (s c) -> p s c", s=4), ALU.subtract))
                            v.wait_ge(p_p, 14 * j + u + 1)
                            v.tensor_tensor(x4, id4, bank(u, 0).rearrange("p (s c) -> p s c", s=4), ALU.subtract)\
                             .then_inc(xz_ok, 1)
                        else:
                            v.wait_ge(vw_p, 12 * j + 2 * (lv - 1) + u + 1)
                            if lv < 6:
                                c.tick(v.tensor_tensor(XI[:, u], XI[:, u], bank(u, 1), ALU.subtract))
                            v.tensor_tensor(ZI[:, u], ZI[:, u], bank(u, 2), ALU.subtract).then_inc(xz_ok, 1)
                for u in range(2):
                    v.wait_ge(s1_p, 2 * j + u + 1)
                    b3 = bank(u, 3)
                    v.tensor_scalar(VN[:, u, 0:P], b3[:, 0:P], gcol(bet, 0, 0, u), None, ALU.mult)
                    v.tensor_scalar(VN[:, u, 3 * P:], b3[:, P:2 * P], gcol(bet, 1, 1, u), None, ALU.mult).then_inc(vn1, 1)
                for u in range(2):
                    v.wait_ge(r_p, 2 * j + u + 1)
                    b3 = bank(u, 3)
                    hc = ds((2 * j + u) * P, P)
                    v.tensor_tensor(RH[:, u, 0:P], VT[:, 1, hc], b3[:, 2 * P:3 * P], ALU.subtract)
                    v.tensor_tensor(RH[:, u, P:], VT[:, 0, hc], b3[:, 3 * P:], ALU.subtract).then_inc(rh_ok, 1)
                for u in range(2):
                    v.wait_ge(s2_p, 2 * j + u + 1)
                    b3 = bank(u, 3)
                    v.tensor_scalar(VN[:, u, P:2 * P], b3[:, 0:P], gcol(bet, 0, 1, u), None, ALU.mult)
                    v.tensor_scalar(VN[:, u, 2 * P:3 * P], b3[:, P:2 * P], gcol(bet, 1, 0, u), None, ALU.mult)\
                     .then_inc(vn2, 1)
                for u in range(2):
                    v.wait_ge(go_p, 2 * j + u + 3)
                    v.tensor_copy(H[:, ds(2 * j + u, 1)], bank(u, 1)[:, 0:T]).then_inc(go_ok, 1)
                c.done()
            v.wait_ge(go_ok, 8 + 2)

            def head_norm(i):
                v.tensor_tensor(SQX[:], H[:], H[:], ALU.mult).then_inc(l2_sq, 1)
                v.wait_ge(l2_std, i + 1)
                c.link(v.reciprocal(SQX[:], SQX[:]))
                c.link(v.tensor_tensor(H[:], H[:], SQX[:], ALU.mult))
            head_norm(2)
            flat = "p k t -> p (k t)"
            c.link(v.scalar_tensor_tensor(H[:].rearrange(flat), H[:].rearrange(flat), pc("a_norm_g", 0),
                                          ZA[:].rearrange(flat), ALU.mult, ALU.mult))
            h_lo(3)
            split_section(v, split_lo, SEC["a_out"], residual(SEC["a_out"], None))
            v.wait_ge(acc_free, SEC["mlp1_0"].o0 + 4)

            def ln(name, g_, b_, l_):
                v.nop().then_inc(n_x, 1)
                norm_dve(v, c, name, lambda k: pc(g_, 8 * l_ + k), lambda k: pc(b_, 8 * l_ + k), X)
            ln("ln1_0", "ln1_g", "ln1_b", 0)
            h_lo(4)

            def mlp(k):
                s = SEC[f"mlp1_{k}"]
                if k == 0:
                    v.sem_inc(hid_lo, 4)

                def lo(b, u, h, j):
                    q = (2 * u + h) % 4
                    i = 2 * b + h
                    v.wait_ge(evac_a, EV[s.name] + 2 * b + h + 1)
                    c.link(v.tensor_tensor(TMQ[:, q], TMP[:, q], TMP[:, q], ALU.mult))
                    v.tensor_tensor(HIDL[:, ds(i, 1)], TMQ[:, q], HIDH[:, ds(i, 1)].bitcast(F32), ALU.subtract)\
                     .then_inc(hid_lo, 1)
                split_section(v, split_lo, s, lo, c, 8)
                s2 = SEC[f"mlp2_{k}"]
                split_section(v, split_lo, s2, residual(s2, None))
                v.wait_ge(acc_free, s2.o0 + 8 + 4)
                ln(f"ln2_{k}", "ln2_g", "ln2_b", k)
            mlp(0)
            h_lo(5)
            for name in ("b_qk", "b_v", "b_r"):
                split_section(v, split_lo, SEC[name], None)
            c.link(v.memset(onet[:], 1.0))
            v.wait_ge(lg_p, 1)
            for d in range(2):
                for k in range(4):
                    i = 4 * d + k
                    c.tick(v.tensor_scalar(LA[:, i], acc[:, i // 2, (i % 2) * T:(i % 2) * T + T], pc("gate_b", i), None, ALU.add))
            c.wait()
            flat = "p k t -> p (k t)"
            v.scalar_tensor_tensor(LT[:].rearrange(flat), LA[:].rearrange(flat), -1.0, LA[:].rearrange(flat),
                                   ALU.mult, ALU.max).then_inc(lt_ok, 1)
            v.wait_ge(lt_e, 2)
            c.link(v.scalar_tensor_tensor(LA[:].rearrange(flat), LA[:].rearrange(flat), 0.0, LT[:].rearrange(flat),
                                          ALU.min, ALU.subtract))
            for i in range(8):
                c.tick(v.tensor_tensor_scan(BS[:, i], onet[:], LA[:, i], 0.0, ALU.mult, ALU.add))
            c.wait()
            v.tensor_tensor(BS[:, 4:8], LA[:, 4:8], BS[:, 4:8], ALU.subtract).then_inc(bs_ok, 1)
            v.sem_inc(kq_ok, 2)
            v.sem_inc(s_ok, 4)
            v.sem_inc(bo_ok, 2)
            with v.Fori(0, B_HEADS) as h:
                diag = SS[:, 0, 0:P]
                diag = bass.AP(tensor=diag.tensor, offset=diag.offset, ap=[diag.ap[0], [T + P, 2], [1, P]])
                cross = SS[:, 0, P:T]
                cross = bass.AP(tensor=cross.tensor, offset=cross.offset, ap=[cross.ap[0], [P, 2], [1, P]])
                id2 = bass.AP(tensor=ident[:].tensor, offset=ident[:].offset, ap=[ident[:].ap[0], [0, 2], [1, P]])
                v.wait_ge(dg_p, h + 1)
                v.wait_ge(bo_p, h + 1)
                v.scalar_tensor_tensor(diag, acc[:, 3, 0:T].rearrange("p (t c) -> p t c", t=2), 2.0, id2,
                                       ALU.mult, ALU.mult).then_inc(dg_ok, 1)
                def scores(lv):
                    return pm[:, lv % 4, 0:T].rearrange("p (t c) -> p t c", t=2)

                def take(lv):
                    m = gm[:, lv]
                    mask = bass.AP(tensor=m.tensor, offset=m.offset, ap=[m.ap[0], [0, 2], [1, P]])
                    v.copy_predicated(diag, mask.bitcast(I32), scores(lv)).then_inc(s_ok, 1)

                for lv in range(8):
                    v.wait_ge(ee_ok, 8 * h + lv + 2)
                    if lv == 2:
                        v.wait_ge(dg_ok, h + 1)
                    if lv > 2:
                        v.wait_ge(s_ok, 8 * h + lv + 2)
                    v.wait_ge(sc_p, 8 * h + lv + 1)
                    v.tensor_tensor(KQ[:, lv % 2], DD[:, lv % 2], QKH[:], ALU.mult).then_inc(kq_ok, 1)
                    if lv >= 2:
                        take(lv - 2)
                v.wait_ge(s_ok, 8 * h + 6 + 4)
                v.wait_ge(sc_p, 8 * h + 8 + 2)
                v.tensor_copy(cross, scores(7)).then_inc(s_ok, 1)
                take(6)
                for e in range(2):
                    v.wait_ge(bo_p, h + 2)
                    v.tensor_copy(H[:, ds(2 * h + e, 1)], acc[:, e, 0:T]).then_inc(bo_ok, 1)
            v.wait_ge(bo_ok, 8 + 2)
            head_norm(3)
            for k in range(8):
                c.tick(v.scalar_tensor_tensor(H[:, k], H[:, k], pc("b_norm_g", k % 2), RG[:, k], ALU.mult, ALU.mult))
            c.wait()
            h_lo(6)
            split_section(v, split_lo, SEC["b_out"], residual(SEC["b_out"], None))
            v.wait_ge(acc_free, SEC["mlp1_1"].o0 + 4)
            ln("ln1_1", "ln1_g", "ln1_b", 1)
            h_lo(7)
            mlp(1)
            v.nop().then_inc(n_h, 1)

        @block.tensor
        def _(pe):
            pe.sem_inc(w_used, 4)
            pe.sem_inc(acc_free, 4)
            pe.wait_ge(masks, 2)
            pe.wait_ge(x_in, 16)
            for q in range(4):
                for i in range(4):
                    d_, tk = 2 * q + i // 2, i % 2
                    m = pe.transpose(acc[:, q, i * P:i * P + P], XIN[:, tk, d_ * P:d_ * P + P], ident[:])
                m.then_inc(xt_p, 1)
            pe.wait_ge(par_in, 16 * len(pieces))
            for bk in range(2):
                for i in range(4 * bk, min(4 * bk + 4, NPT)):
                    n = min(P, NPAR - P * i)
                    m = pe.transpose(pm[:, bk, (i % 4) * P:(i % 4) * P + n], PRW[0:n, i, :], ident[0:n, 0:n])
                m.then_inc(par_t, 1)

            def ada_sums(n, src, done):
                for i in range(n):
                    m = pe.matmul(pm[:, 3, i:i + 1], src[:, i * P:i * P + P], ones[:, 0:1], start=True, stop=True)
                m.then_inc(done, 1)
            pe.wait_ge(ada_part, 1)
            ada_sums(16, ADA, ada_sum)
            norm_pe(pe, "mix")

            def h_ready(n):
                pe.wait_ge(n_hl, n + 1)
            h_ready(0)
            pe_section(pe, SEC["conv_b"], hrhs)
            pe_section(pe, SEC["conv_a"], hrhs)

            def small_tok(w_, src, done):
                pe.wait_ge(dt_in, 16 * 8)
                for tk in range(NT):
                    for k in range(DT):
                        m = pe.matmul(pm[:, 2, tk * NH:tk * NH + NH], src[:, k, tk * P:tk * P + P], w_[:, k],
                                      start=k == 0, stop=k == DT - 1)
                m.then_inc(done, 1)
            small_tok(ws1, H, dt_p)
            pe_section(pe, SEC["xbc"], hrhs)
            pe_section(pe, SEC["z"], hrhs)
            pe_section(pe, SEC["g"], hrhs)
            norm_pe(pe, "conv")
            pe.wait_ge(rest_part, 1)
            ada_sums(32, ADA2, rest_sum)
            pe.wait_ge(xbc_ok, 1)
            pe.wait_ge(mod_ok, 1)
            for q in range(8):
                if q >= 3:
                    pe.wait_ge(xs_ok, q - 2)
                for i in range(4):
                    d_, tk = 4 * (q % 4) + i, q // 4
                    m = pe.transpose(pm[:, q % 3, i * P:i * P + P], XBC[:, d_, tk * P:tk * P + P], ident[:])
                m.then_inc(xs_t, 1)
            pe.wait_ge(acc_free, SEC["conv_out"].o0 + 4)
            for gi in range(NG):
                b_, c_ = XBC[:, 16 + gi], XBC[:, 20 + gi]
                pe.matmul(acc[:, gi, 0:T], b_[:, 0:P], c_, start=True, stop=True)
                pe.matmul(acc[:, gi, T:T + P], b_[:, P:], c_[:, P:], start=True, stop=True).then_inc(cb_p, 1)
            pe.wait_ge(xs_ok, 8)
            pe.sem_inc(seg_p, 2)
            pe.sem_inc(y_p, 2)
            for gi in range(NG):
                with pe.Fori(0, 4) as j:
                    for u in range(2):
                        h = 2 * j + 8 * gi + u
                        pe.wait_ge(l_ok, h + 1)
                        pe.wait_ge(e_ok, h + 1)
                        o_ = pm[:, u]
                        kw = dict(skip_group_check=True)
                        pe.matmul(o_[:, 0:2 * P], LS[:, u, 0:P], maskf[:, 0:2 * P], start=True, stop=False, **kw)
                        pe.matmul(o_[:, P:2 * P], LS[:, u, 2 * P:], maskf[:, 0:P], start=False, stop=False, **kw)
                        pe.matmul(o_[:, 2 * P:3 * P], LS[:, u, P:2 * P], maskf[:, 0:P], start=False, stop=True, **kw)\
                          .then_inc(seg_p, 1)
                    for u in range(2):
                        h = 2 * j + 8 * gi + u
                        pe.wait_ge(m_ok, h + 1)
                        if u == 0:
                            pe.wait_ge(y_ok, j + 4 * gi + 1)
                        o_ = pm[64 * u:64 * u + 64, 2, 0:T]
                        pe.matmul(o_, XD[:, u, 0], ES[:, u, 0:T], start=True, stop=False, skip_group_check=True)
                        pe.matmul(o_[:, P:], XD[:, u, 1], ES[:, u, T:T + P], start=False, stop=True,
                                  skip_group_check=True).then_inc(y_p, 1)
            pe.wait_ge(ysq, 1)
            for gi in range(NG):
                for k in range(4):
                    i = 4 * gi + k
                    sq = H[:, i] if i < 8 else SQ2[:, i - 8]
                    m = pe.matmul(pm[:, gi // 2, (gi % 2) * T:(gi % 2) * T + T], ones, sq, start=k == 0, stop=k == 3)
            m.then_inc(ysum, 1)
            pe.wait_ge(u_lo, 1)
            pe_section(pe, SEC["conv_out"], urhs)
            pe.wait_ge(ylo, 1)
            pe_section(pe, SEC["ssm_out"], yrhs)
            pe.wait_ge(mg_lo, 1)
            pe_section(pe, SEC["w_out"], urhs)
            norm_pe(pe, "ffn")
            h_ready(1)
            ffn_in_pe(pe)
            pe.wait_ge(hid_ok, 1)
            pe_section(pe, SEC["ffn_down"], hidrhs)
            norm_pe(pe, "final")
            h_ready(2)
            small_tok(ws2, X, ba_p)
            pe_section(pe, SEC["a_qkv"], hrhs)
            pe_section(pe, SEC["a_z"], hrhs)

            def l2_pe(i, tiles):
                pe.wait_ge(l2_sq, i + 1)
                for k in range(8):
                    o_ = acc[:, k // 2, (k % 2) * T:(k % 2) * T + T]
                    for m_ in range(tiles):
                        m = pe.matmul(o_, ones, SQX[:, k // tiles * tiles + m_], start=m_ == 0, stop=m_ == tiles - 1)
                m.then_inc(l2_sum, 1)
            pe.wait_ge(acc_free, SEC["a_out"].o0 + 4)
            l2_pe(0, 1)
            pe.wait_ge(l2_std, 1)
            l2_pe(1, 1)
            pe.wait_ge(bet_ok, 1)
            pe.wait_ge(qkn_ok, 1)
            for q in range(4):
                for i in range(4):
                    d_, tk = 4 * (q % 2) + i, q // 2
                    m = pe.transpose(pm[:, q, i * P:i * P + P], QKV[:, 16 + d_, tk * P:tk * P + P], ident[:])
                m.then_inc(vt_p, 1)
            pe.wait_ge(vt_ok, 4)
            pe.sem_inc(go_p, 2)
            kw = dict(skip_group_check=True)
            pe.wait_ge(qkn_ok, 1)
            with pe.Fori(0, A_HEADS // 2) as j:
                for u in range(2):
                    kk, qk, sf, sb_ = (bank(u, i) for i in range(4))
                    pe.wait_ge(ks_ok, 2 * j + u + 1)
                    pe.wait_ge(go_ok, 2 * j + u + 1)
                    k_, q_ = QKV[:, ds(2 * j + u + 8, 1)], QKV[:, ds(2 * j + u, 1)]
                    for dst, r in ((kk, k_), (qk, q_)):
                        for tk in range(NT):
                            m = pe.matmul(dst[:, tk * T:tk * T + T], KS[:, u, tk * P:tk * P + P], r, start=True, stop=True)
                    m.then_inc(kq_p, 1)
                    pe.wait_ge(gl_l, 2 * j + u + 1)
                    ge = maskb[:, P:2 * P]
                    pe.matmul(sf[:, 0:T], LF[:, u, 0:P], maskf[:, 0:T], start=True, stop=False, **kw)
                    pe.matmul(sf[:, P:T], LF[:, u, T:], maskf[:, 0:P], start=False, stop=False, **kw)
                    pe.matmul(sf[:, T:3 * P], LF[:, u, P:T], maskf[:, 0:P], start=False, stop=True, **kw)
                    pe.matmul(sb_[:, 0:T], LB[:, u, 0:P], maskb[:, 0:T], start=True, stop=False, **kw)
                    pe.matmul(sb_[:, 0:P], LB[:, u, T:], ge, start=False, stop=False, **kw)
                    pe.matmul(sb_[:, T:3 * P], LB[:, u, P:T], ge, start=False, stop=True, **kw).then_inc(gs_p, 1)
                for lv in range(7):
                    for u in range(2):
                        pe.wait_ge(am_ok, 14 * j + 2 * lv + u + 1)
                        if lv:
                            pe.wait_ge(xz_ok, 14 * j + 2 * (lv - 1) + u + 1)
                        for s_ in range(4):
                            cs_ = slice(s_ * P, s_ * P + P)
                            r = XI[:, u, cs_] if lv else ident[:]
                            m = pe.matmul(bank(u, 0)[:, cs_], AM[:, u, lv % 2, cs_], r, start=True, stop=True)
                        m.then_inc(p_p, 1)
                    for u in range(2):
                        if lv == 0:
                            continue
                        pe.wait_ge(ps_ok, 12 * j + 2 * (lv - 1) + u + 1)
                        if lv == 1:
                            pe.wait_ge(qd_ok, 2 * j + u + 1)
                        for s_ in range(4):
                            cs_ = slice(s_ * P, s_ * P + P)
                            if lv < 6:
                                pe.matmul(bank(u, 1)[:, cs_], ZI[:, u, cs_], PS[:, u, cs_], start=True, stop=True)
                            m = pe.matmul(bank(u, 2)[:, cs_], PS[:, u, cs_], ZI[:, u, cs_], start=True, stop=True)
                        m.then_inc(vw_p, 1)
                for u in range(2):
                    b3 = bank(u, 3)
                    hc = ds((2 * j + u) * P, P)
                    pe.wait_ge(xz_ok, 14 * j + 12 + u + 1)
                    pe.matmul(b3[:, 0:P], ZI[:, u, 0:P], VT[:, 0, hc], start=True, stop=True)
                    pe.matmul(b3[:, P:T], ZI[:, u, 3 * P:], VT[:, 1, hc], start=True, stop=True).then_inc(s1_p, 1)
                for u in range(2):
                    b3 = bank(u, 3)
                    pe.wait_ge(vn1, 2 * j + u + 1)
                    pe.matmul(b3[:, T:3 * P], KDX[:, u, 0:P], VN[:, u, 0:P], start=True, stop=True)
                    pe.matmul(b3[:, 3 * P:], KDX[:, u, P:], VN[:, u, 3 * P:], start=True, stop=True).then_inc(r_p, 1)
                for u in range(2):
                    b3 = bank(u, 3)
                    pe.wait_ge(rh_ok, 2 * j + u + 1)
                    pe.matmul(b3[:, 0:P], ZI[:, u, P:2 * P], RH[:, u, 0:P], start=True, stop=True)
                    pe.matmul(b3[:, P:T], ZI[:, u, 2 * P:3 * P], RH[:, u, P:], start=True, stop=True).then_inc(s2_p, 1)
                for u in range(2):
                    o_ = bank(u, 1)
                    pe.wait_ge(vn2, 2 * j + u + 1)
                    pe.matmul(o_[:, 0:T], VN[:, u, 0:P], DF[:, u, 0:T], start=True, stop=False, **kw)
                    pe.matmul(o_[:, P:T], VN[:, u, P:T], DF[:, u, T:], start=False, stop=False, **kw)
                    pe.matmul(o_[:, 0:T], VN[:, u, 3 * P:], DB[:, u, 0:T], start=False, stop=False, **kw)
                    pe.matmul(o_[:, 0:P], VN[:, u, T:3 * P], DB[:, u, T:], start=False, stop=True, **kw).then_inc(go_p, 1)
            l2_pe(2, 1)
            h_ready(3)
            pe_section(pe, SEC["a_out"], hrhs)
            norm_pe(pe, "ln1_0")
            h_ready(4)

            def mlp(k):
                pe_section(pe, SEC[f"mlp1_{k}"], hrhs)
                pe.wait_ge(hid_lo, 32 * k + 32 + 4)
                pe_section(pe, SEC[f"mlp2_{k}"], hidrhs)
                norm_pe(pe, f"ln2_{k}")
            mlp(0)
            h_ready(5)
            pe_section(pe, SEC["b_qk"], hrhs)
            pe_section(pe, SEC["b_v"], hrhs, tok_major=True)
            pe_section(pe, SEC["b_r"], hrhs)
            for k in range(DT):
                m = pe.matmul(pm[0:NH, 2, 0:T], ws3[:, k], X[:, k], start=k == 0, stop=k == DT - 1)
            m.then_inc(gl_p, 1)
            pe.wait_ge(gl_ok, 1)
            pe.wait_ge(gw_in, 16 * 2)
            pe.wait_ge(acc_free, SEC["b_out"].o0 + 4)
            for d in range(2):
                for k in range(4):
                    i = 4 * d + k
                    m = pe.matmul(acc[:, i // 2, (i % 2) * T:(i % 2) * T + T], gw[:, d, k * P:k * P + P], glt[:],
                                  start=True, stop=True)
            m.then_inc(lg_p, 1)
            pe.sem_inc(bo_p, 1)
            pe.sem_inc(sc_p, 2)
            pe.wait_ge(bs_ok, 1)
            with pe.Fori(0, B_HEADS) as h:
                pe.wait_ge(st_ok, h + 1)
                pe.wait_ge(bo_ok, 2 * h + 2)
                for tk in range(NT):
                    tc = slice(tk * P, tk * P + P)
                    m = pe.matmul(acc[:, 3, tc], QKH[:, 0, tc], QKH[:, 1, tc], start=True, stop=True)
                m.then_inc(dg_p, 1)
                for lv in range(8):
                    pe.wait_ge(kq_ok, 8 * h + lv + 3)
                    pe.wait_ge(s_ok, 8 * h + lv + 1)
                    for tk in range(NT):
                        tc = slice(tk * P, tk * P + P)
                        rc = tc if lv < 7 else slice((1 - tk) * P, (1 - tk) * P + P)
                        m = pe.matmul(pm[:, lv % 4, tc], KQ[:, lv % 2, 0, tc], KQ[:, lv % 2, 1, rc], start=True, stop=True)
                    m.then_inc(sc_p, 1)
                pe.wait_ge(s_ok, 8 * h + 8 + 4)
                for e in range(2):
                    for tk in range(NT):
                        m = pe.matmul(acc[:, e, 0:T], VH[:, tk, e * P:e * P + P], SS[:, tk], start=tk == 0, stop=tk == 1)
                m.then_inc(bo_p, 1)
            l2_pe(3, 2)
            h_ready(6)
            pe_section(pe, SEC["b_out"], hrhs)
            norm_pe(pe, "ln1_1")
            h_ready(7)
            mlp(1)
            pe.wait_ge(n_h, 9)
            for q in range(4):
                for i in range(4):
                    d_, tk = 4 * (q % 2) + i, q // 2
                    m = pe.transpose(pm[:, q, i * P:i * P + P], X[:, d_, tk * P:tk * P + P], ident[:])
                m.then_inc(ot_p, 1)
        running.close()


_INS = ["x", "c", "w_ada_mix", "b_ada_mix", "norm_mix_w", "w_in", "conv_dw_w", "conv_dw_b", "conv_ln_w",
        "conv_ln_b", "w_conv_out", "ssm_conv_w", "ssm_conv_b", "dt_bias", "a_log", "d_skip", "ssm_norm_w",
        "w_ssm_out", "w_out", "w_ada_ffn", "b_ada_ffn", "norm_ffn_w", "w_ffn_in", "w_ffn_down", "final_norm_w",
        "a_w_in_2", "a_conv_2", "a_alog_2", "a_dt_bias_2", "a_norm_g_2", "a_w_out_2", "b_w_in_2", "b_gate_w2_2",
        "b_gate_b_2", "b_norm_g_2", "b_w_out_2", "ln1_g_2", "ln1_b_2", "mlp_w1_2", "mlp_w2_2", "ln2_g_2", "ln2_b_2"]


def kernel(**inputs):
    import numpy as _np
    import concourse.bacc as _bacc
    from concourse.bass_utils import run_bass_kernel_spmd as _run

    nc = _bacc.Bacc("TRN2", target_bir_lowering=False, num_devices=1)
    arrays, args = {}, {}
    for name in _INS:
        x = _np.ascontiguousarray(inputs[name])
        arrays[f"in_{name}"] = x
        args[name] = nc.dram_tensor(f"in_{name}", x.shape, mybir.dt.from_np(x.dtype), kind="ExternalInput").ap()
    out = nc.dram_tensor("out_x", (1, T, D), F32, kind="ExternalOutput").ap()
    program(nc, args, out)
    return _run(nc, [arrays], core_ids=[0]).results[0]["out_x"]
```

```python
import math
from contextlib import ExitStack

import concourse.bass as bass
from concourse import mybir

F32 = mybir.dt.float32
F32R = mybir.dt.float32r
I32 = mybir.dt.int32
ALU = mybir.AluOpType
ACT = mybir.ActivationFunctionType

P = 128
T = 256
NT = T // P
D = 1024
DT = D // P
KT = 8
COLS = 256
D_INNER = 2048
NH = 32
NG = 4
D_FF = 2816
FF_T = D_FF // P
FF_CHUNKS = [6, 6, 5, 5]
D_FF2 = 4096
CW = 31
SW = 4
AW = 5
A_HEADS = 8
B_HEADS = 4
RMS_EPS = 1e-6
LN_EPS = 1e-5
ALPHA = (2 * 2) ** 0.25


def ds(a, n):
    return bass.ds(a, n)


class Chain:

    def __init__(self, eng, sem):
        self.eng, self.sem, self.n, self.off = eng, sem, 0, 0

    def link(self, ins):
        self.tick(ins)
        self.wait()

    def tick(self, ins):
        ins.then_inc(self.sem, 1)
        self.n += 1

    def wait(self, back=0):
        self.eng.wait_ge(self.sem, self.n - back + self.off)

    def loop(self, j, per, times):
        self.start, self.per, self.times = self.n, per, times
        self.off = j * per

    def done(self):
        assert self.n - self.start == self.per, (self.n - self.start, self.per)
        self.n, self.off = self.start + self.per * self.times, 0


class Section:

    def __init__(self, name, src, nb, kts=(KT,), lo="vector"):
        self.name, self.src, self.nb, self.kts = name, src, nb, list(kts)
        self.lo = lo
        self.step = 1
        self.chunks = len(self.kts)


def program(nc, a, out):
    def cols(w, c0, kt=KT):
        v = w.rearrange("(k p) c -> p k c", p=P)
        return lambda b: v[:, 0:kt, ds(b * COLS + c0, COLS)]

    def pairs(w, c0, c1):
        v = w.rearrange("(k p) c -> p k c", p=P)
        return lambda j, which: v[:, :, ds(j * COLS + (c1 if which else c0), COLS)]

    w_in = a["w_in"][0]
    a_in = a["a_w_in_2"][0]
    b_in = a["b_w_in_2"][0]
    OFF_Z, OFF_XBC = 2 * D, 2 * D + D_INNER
    OFF_DT = OFF_XBC + D_INNER + 2 * NG * P
    OFF_G = OFF_DT + NH
    A_QKV, A_Z = 3 * D, 3 * D
    A_BA = A_Z + D
    B_QK, B_V, B_R = D, D, 2 * D
    B_GL = 3 * D
    SECS = [
        Section("conv_b", cols(w_in, D), 4),
        Section("conv_a", cols(w_in, 0), 4),
        Section("xbc", cols(w_in, OFF_XBC), 12, lo="gpsimd"),
        Section("z", cols(w_in, OFF_Z), 8, lo="gpsimd"),
        Section("g", cols(w_in, OFF_G), 8, lo="gpsimd"),
        Section("conv_out", cols(a["w_conv_out"][0], 0), 4, lo="gpsimd"),
        Section("ssm_out", a["w_ssm_out"][0], 8, (8, 8), lo="gpsimd"),
        Section("w_out", cols(a["w_out"][0], 0), 4, lo="gpsimd"),
        Section("ffn_in", pairs(a["w_ffn_in"][0], 0, D_FF), 22),
        Section("ffn_down", a["w_ffn_down"][0], 16, FF_CHUNKS),
        Section("a_qkv", cols(a_in, 0), 12, lo="gpsimd"),
        Section("a_z", cols(a_in, A_Z), 4),
        Section("a_out", cols(a["a_w_out_2"][0], 0), 4),
        Section("mlp1_0", cols(a["mlp_w1_2"][0], 0), 16),
        Section("mlp2_0", a["mlp_w2_2"][0], 16, (8, 8, 8, 8)),
        Section("b_qk", cols(b_in, 0), 4),
        Section("b_v", cols(b_in, B_V), 4),
        Section("b_r", cols(b_in, B_R), 4),
        Section("b_out", cols(a["b_w_out_2"][0], 0), 4),
        Section("mlp1_1", cols(a["mlp_w1_2"][1], 0), 16),
        Section("mlp2_1", a["mlp_w2_2"][1], 16, (8, 8, 8, 8)),
    ]
    SEC = {s.name: s for s in SECS}
    ADA_FIRST = [("w_ada_mix", b) for b in range(8)]
    ADA_REST = [("w_ada_mix", b) for b in range(8, 12)] + [("w_ada_ffn", b) for b in range(12)]
    order = [("ada", n) for n in range(len(ADA_FIRST))]
    w = t = o = 0
    before = None
    for s in SECS:
        s.step = 2 if s.name in ("conv_out", "ssm_out", "w_out") else 1
        s.g0, s.w0, s.t0, s.o0 = len(order), w, t, o
        s.ahead = before is not None and before.lo == s.lo
        if before:
            before.next = s
        for b in range(s.nb):
            order.append(("w", w + b))
            if s.step == 2:
                order.append(("ada", sum(k == "ada" for k, _ in order)))
        w, t, o = w + s.nb, t + 2 * s.nb, o + 2 * s.nb // s.chunks
        before = s
    before.next = None
    ADA_AT = [i for i, (k, _) in enumerate(order) if k == "ada"]
    assert len(ADA_AT) == len(ADA_FIRST) + len(ADA_REST)

    def kt_of(s, u):
        return s.kts[u % s.chunks]

    def over_blocks(eng, s, body, chain=None, per=0):
        turns = (s.nb - 1) // 4
        if turns:
            with eng.Fori(0, turns) as j:
                if chain:
                    chain.loop(j, per, turns)
                for u in range(4):
                    body(4 * j + u, u, False, j)
                if chain:
                    chain.done()
        for b in range(4 * turns, s.nb):
            body(b, b % 4, b == s.nb - 1, turns)

    with ExitStack() as ctx:
        TILE = T * 4
        base = (nc.sbuf_base + 63) // 64 * 64

        def at(name, tile, shape, dt=F32):
            return nc.alloc_sbuf_tensor_at(name, shape, dt, offset=base + int(tile * TILE))

        def psum(name, shape):
            return ctx.enter_context(nc.psum_tensor(name, shape, F32))

        def sem(name):
            return ctx.enter_context(nc.semaphore(name))

        raw = at("raw", 0, [P, 4, KT, COLS])
        whi = at("whi", 32, [P, 4, KT, P], F32R)
        wlo = at("wlo", 48, [P, 4, KT, P], F32R)
        X = at("X", 64, [P, DT, T])
        H = at("H", 72, [P, DT, T])
        HH = at("HH", 80, [P, DT, T], F32R)
        HL = at("HL", 88, [P, DT, T], F32R)
        maskf = at("maskf", 96, [P, 3 * P])
        maskb = at("maskb", 97.5, [P, 3 * P])
        slo = at("slo", 99, [P, 2 * P])
        suo = at("suo", 100, [P, 2 * P])
        ident = at("ident", 101, [P, P])
        ones = maskf[:, P:2 * P]
        par = at("par", 102, [P, 768])
        SM = 105
        small_at = [0]

        def small(name, n, dt=F32):
            ap = at(name, SM + small_at[0] / 256, [P, n], dt)
            small_at[0] += (n + 7) // 8 * 8
            assert small_at[0] <= 3 * 256
            return ap

        sc = small("sc", 8)
        dtb = small("dtb", 2 * NH)
        gab = small("gab", 64)
        dtt = small("dtt", 2 * NH)
        dat = small("dat", 2 * NH)
        spt = [small(f"spt{i}", 64) for i in range(4)]
        dsk = small("dsk", 32 + 16)
        AR = 108

        def ar(name, tile, shape, dt=F32):
            return at(name, AR + tile, shape, dt)

        UP = ar("UP", 0, [P, DT, T + CW - 1])
        UH = ar("UH", 0, [P, DT, T], F32R)
        ACC = ar("ACC", 9, [P, DT, T])
        UL = ar("UL", 9, [P, DT, T], F32R)
        XP = ar("XP", 17, [P, 4, T + SW - 1])
        XBC = ar("XBC", 22, [P, 24, T])
        Z = ar("Z", 46, [P, 16, T])
        YL = ar("YL", 46, [P, 16, T], F32R)
        G = ar("G", 62, [P, 16, T])
        CB = ar("CB", 78, [P, NG, 3 * P])
        LS = ar("LS", 84, [P, 2, 3 * P])
        ES = ar("ES", 87, [P, 2, 3 * P])
        XD = ar("XD", 90, [P, 2, NT, 64])
        XT = at("XT", 72, [P, 2, NT, 512])
        YSQ = at("YSQ", 80, [P, 16, T])
        YH = at("YH", 80, [P, 16, T], F32R)
        PRW = ar("PRW", 78, [P, 6, P])
        XIN = ar("XIN", 22, [P, NT, D])
        ADA = ar("ADA", 30, [P, 2 * D])
        MOD = ar("MOD", 95, [P, 48])
        NR = ar("NR", 96, [P, 2, T])
        HIDH = ar("HIDH", 0, [P, 32, T], F32R)
        HIDL = ar("HIDL", 32, [P, 32, T], F32R)
        TMP = ar("TMP", 64, [P, 4, T])
        TMQ = ar("TMQ", 68, [P, 4, T])

        acc = psum("acc", [P, 4, 512])
        pm = psum("pm", [P, 4, 512])

        landed = [sem(f"landed{i}") for i in range(4)]
        raw_used = sem("raw_used")
        ada_used = sem("ada_used")
        hi_ready = sem("hi_ready")
        w_used = sem("w_used")
        acc_free = sem("acc_free")
        vchain, achain, gchain = sem("vchain"), sem("achain"), sem("gchain")
        par_in, x_in = sem("par_in"), sem("x_in")
        masks = sem("masks")
        par_t, par_ok = sem("par_t"), sem("par_ok")
        silu_c = sem("silu_c")
        ada_part, ada_sum, mod_ok = sem("ada_part"), sem("ada_sum"), sem("mod_ok")
        xt_p, x_ok = sem("xt_p"), sem("x_ok")
        n_xc, n_mean, n_sq, n_sum, n_std, n_t, n_hh, n_hl = (sem(f"norm_{k}") for k in
                                                   ("xc", "mean", "sq", "sum", "std", "t", "hh", "hl"))
        ln_ok, full_ok, conv_ok, o_ok = sem("ln_ok"), sem("full_ok"), sem("conv_ok"), sem("o_ok")
        evac_a = sem("evac_a")
        evac_v = sem("evac_v")
        out_sem = sem("out_sem")
        running = ExitStack()
        block = running.enter_context(nc.Block())

        rows, prow = [], {}

        def param(name, ap, n):
            prow[name] = sum(r[1] for r in rows)
            rows.append((ap, n))

        def vec(v):
            return v.rearrange("(t p) -> t p", p=P)

        param("c", vec(a["c"][0]), 8)
        param("b_ada_mix", vec(a["b_ada_mix"][0]), 24)
        param("b_ada_ffn", vec(a["b_ada_ffn"][0]), 24)
        param("norm_mix_w", vec(a["norm_mix_w"][0]), 8)
        param("conv_ln_w", vec(a["conv_ln_w"][0]), 8)
        param("conv_ln_b", vec(a["conv_ln_b"][0]), 8)
        param("conv_dw_b", vec(a["conv_dw_b"][0]), 8)
        param("ssm_conv_b", vec(a["ssm_conv_b"][0]), 24)
        param("ssm_norm_w", vec(a["ssm_norm_w"][0]), 16)
        param("norm_ffn_w", vec(a["norm_ffn_w"][0]), 8)
        param("final_norm_w", vec(a["final_norm_w"]), 8)
        param("ssm_conv_w", a["ssm_conv_w"][0].rearrange("w (t p) -> (w t) p", p=P), SW * 24)
        param("conv_dw_w", a["conv_dw_w"][0].rearrange("w (t p) -> (w t) p", p=P), CW * DT)
        param("a_conv", a["a_conv_2"][0].rearrange("w (t p) -> (w t) p", p=P), AW * 24)
        param("a_norm_g", a["a_norm_g_2"], 1)
        param("b_norm_g", vec(a["b_norm_g_2"][0]), 2)
        param("gate_b", a["b_gate_b_2"][0].rearrange("d (t p) -> (d t) p", p=P), 8)
        for k in ("ln1_g", "ln1_b", "ln2_g", "ln2_b"):
            param(k, a[k + "_2"].rearrange("l (t p) -> (l t) p", p=P), 16)
        NPAR = sum(n for _, n in rows)
        NPT = -(-NPAR // P)
        assert NPT <= 6

        def pc(name, i, n=1):
            return par[:, ds(i + prow[name], n)]

        pieces, r0 = [], 0
        for ap, n in rows:
            done = 0
            while done < n:
                m = min(n - done, P - (r0 + done) % P)
                pieces.append((ap[done:done + m, :], (r0 + done) % P, (r0 + done) // P, m))
                done += m
            r0 += n

        def bcast(v, n):
            return bass.AP(tensor=v.tensor, offset=v.offset, ap=[[0, P], [1, n]])

        def ada_src(name, b):
            w = a[name][0].rearrange("(k p) c -> p k c", p=P)
            if b < 8:
                return w[:, b, 0:2 * D]
            return w[:, 2 * (b - 8):2 * (b - 8) + 2, 2 * D:3 * D]

        @block.sync
        def _(sp):
            sp.dma_start(XIN[:], a["x"][0].rearrange("(t p) d -> p t d", p=P)).then_inc(x_in, 16)

            def slot_free(gb, w):
                if not isinstance(gb, int):
                    sp.wait_ge(raw_used, 2 * (w - 3))
                elif gb >= 4:
                    kind, n = order[gb - 4]
                    if kind == "w":
                        sp.wait_ge(raw_used, 2 * (n + 1))
                    else:
                        sp.wait_ge(ada_used, n + 1)

            def load_ada(n):
                name, b = (ADA_FIRST + ADA_REST)[n]
                gb = ADA_AT[n]
                slot_free(gb, None)
                dst = raw[:, gb % 4].rearrange("p k c -> p (k c)")
                if b >= 8:
                    dst = dst.rearrange("p (k c) -> p k c", k=2)
                sp.dma_start(dst, ada_src(name, b)).then_inc(landed[gb % 4], 16)

            for n in range(len(ADA_FIRST)):
                load_ada(n)

            def load(s, b, u, j):
                slot = (s.g0 + s.step * u) % 4
                slot_free(b * s.step + s.g0, b + s.w0)
                k = kt_of(s, u)
                if s.name == "ffn_in":
                    src = s.src(2 * j + u // 2, u % 2)
                elif s.chunks == 1:
                    src = s.src(b)
                else:
                    pair = 2 * j + u // 2 if s.chunks == 2 else j
                    k0 = sum(s.kts[:u % s.chunks])
                    src = s.src.rearrange("(k p) c -> p k c", p=P)[:, k0:k0 + k, ds(pair * COLS, COLS)]
                sp.dma_start(raw[:, slot, 0:k, :], src).then_inc(landed[slot], 16)
                if s.step == 2:
                    load_ada(order[s.g0 + 2 * b + 1][1])

            for n, s in enumerate(SECS):
                if s.name == "ffn_in":
                    sp.wait_ge(raw_used, 2 * s.w0)
                    sp.wait_ge(ada_used, len(ADA_AT))
                over_blocks(sp, s, lambda b, u, last, j, s=s: load(s, b, u, j))
            sp.wait_ge(out_sem, 16 * 2)

        def landed_wait(eng, s, b, u):
            gb = s.g0 + s.step * u
            eng.wait_ge(landed[gb % 4], 16 * (gb // 4 + 1) + 4 * s.step * (b - u))

        def split_hi(act, s, b, u, h):
            k = kt_of(s, u)
            if h == 0:
                landed_wait(act, s, b, u)
            tt = 2 * b + s.t0 + h
            act.wait_ge(w_used, tt + 1)
            act.activation(whi[:, (s.t0 + 2 * u + h) % 4, 0:k], raw[:, (s.g0 + s.step * u) % 4, 0:k, h * P:h * P + P],
                           ACT.Copy).then_inc(hi_ready, 1)

        def split_lo(v, s, b, u, h):
            k = kt_of(s, u)
            slot = (s.t0 + 2 * u + h) % 4
            if h == 0:
                landed_wait(v, s, b, u)
            v.wait_ge(w_used, 2 * b + s.t0 + h + 1)
            v.wait_ge(hi_ready, 2 * b + s.t0 + h + 1)
            v.tensor_tensor(wlo[:, slot, 0:k], raw[:, (s.g0 + s.step * u) % 4, 0:k, h * P:h * P + P],
                            whi[:, slot, 0:k].bitcast(F32), ALU.subtract).then_inc(raw_used, 1)

        def split_section(eng, split, s, evac, chain=None, per=0, extra=None):
            if split and not s.ahead:
                if split is split_lo:
                    eng.wait_ge(raw_used, 2 * s.w0)
                for h in range(2):
                    split(eng, s, 0, 0, h)

            def body(b, u, last, j):
                for h in range(2):
                    if split and not last:
                        split(eng, s, b + 1, u + 1, h)
                    elif split and s.next and s.next.ahead:
                        split(eng, s.next, 0, 0, h)
                if evac and (u + 1) % s.chunks == 0:
                    for h in range(2):
                        evac(b, u, h, j)
                if extra:
                    extra(b)
            over_blocks(eng, s, body, chain, per)

        def tile_done(eng, s, b, h):
            eng.wait_ge(w_used, 2 * b + s.t0 + h + 5)

        def out_slot(s, u, h):
            if s.chunks == 1:
                return (s.o0 + 2 * u + h) % 4
            if s.chunks == 2:
                return (s.o0 + u // 2 * 2 + h) % 4
            return (s.o0 + h) % 4

        def pe_section(pe, s, rhs, tok_major=False, free=None, ready=None):
            pe.wait_ge(acc_free, s.o0 + 4)
            over_blocks(pe, s, pe_block(pe, s, rhs, tok_major, free, ready))

        def pe_block(pe, s, rhs, tok_major=False, free=None, ready=None):
            def body(b, u, last, j, only=(0, 1)):
                k = kt_of(s, u)
                k0 = sum(s.kts[:u % s.chunks])
                first, final = u % s.chunks == 0, (u + 1) % s.chunks == 0
                for h in only:
                    tt = 2 * b + s.t0 + h
                    pe.wait_ge(hi_ready, tt + 1)
                    pe.wait_ge(raw_used, 2 * (b + s.w0) + h + 1)
                    if first:
                        if free:
                            free(b, u, h, j)
                        elif s.chunks == 1:
                            pe.wait_ge(acc_free, 2 * b + s.o0 + h + 1)
                        elif s.chunks == 2:
                            pe.wait_ge(acc_free, 4 * j + s.o0 + u // 2 * 2 + h + 1)
                        else:
                            pe.wait_ge(acc_free, 2 * j + s.o0 + h + 3)
                    slot, q = (s.t0 + 2 * u + h) % 4, out_slot(s, u, h)
                    if tok_major:
                        for tk in range(NT):
                            o_ = acc[:, q, tk * P:tk * P + P]
                            for i in range(k):
                                hh, hl = rhs(i)
                                pe.matmul(o_, hh[:, tk * P:tk * P + P], whi[:, slot, i], start=i == 0, stop=False)
                                pe.matmul(o_, hl[:, tk * P:tk * P + P], whi[:, slot, i], start=False, stop=False)
                                m = pe.matmul(o_, hh[:, tk * P:tk * P + P], wlo[:, slot, i], start=False, stop=i == k - 1)
                    else:
                        for i in range(k):
                            if ready and u == 0 and h == 0:
                                ready(i)
                            hh, hl = rhs(k0 + i)
                            pe.matmul(acc[:, q, 0:T], whi[:, slot, i], hh, start=first and i == 0, stop=False)
                            pe.matmul(acc[:, q, 0:T], whi[:, slot, i], hl, start=False, stop=False)
                            m = pe.matmul(acc[:, q, 0:T], wlo[:, slot, i], hh, start=False, stop=final and i == k - 1)
                    m.then_inc(w_used, 1)
            return body

        def hrhs(k):
            return HH[:, k], HL[:, k]

        def urhs(k):
            return UH[:, k], UL[:, k]

        def yrhs(k):
            return YH[:, k], YL[:, k]

        def hidrhs(k):
            return HIDH[:, k], HIDL[:, k]

        def each(ap, n):
            return bass.AP(tensor=ap.tensor, offset=ap.offset, ap=[ap.ap[0], [0, n], [1, T]])

        norm_list = [("mix", 0, X), ("conv", 1, ACC), ("ffn", 0, X), ("final", 0, X), ("ln1_0", 1, X), ("ln2_0", 1, X),
                     ("ln1_1", 1, X), ("ln2_1", 1, X)]
        NORM = {}
        for n, (name, mean, src) in enumerate(norm_list):
            NORM[name] = (n, mean, sum(m for _, m, _ in norm_list[:n]), src)
        HN = {"mix": 0, "ffn": 1, "final": 2, "gdn": 3, "ln1_0": 4, "ln2_0": 5, "gla": 6, "ln1_1": 7, "ln2_1": 8}
        FULL = {"mix": 0, "final": 1, "ln1_0": 2, "ln2_0": 3, "ln1_1": 4}
        BEFORE = {"ffn": "w_out", "final": "ffn_down", "ln1_0": "a_out", "ln2_0": "mlp2_0", "ln1_1": "b_out",
                  "ln2_1": "mlp2_1"}

        def src_ready(eng, name, k):
            if name == "mix":
                eng.wait_ge(x_ok, k // 2 + 1)
            elif name == "conv":
                eng.wait_ge(conv_ok, 1)
            else:
                eng.wait_ge(acc_free, SEC[BEFORE[name]].o0 + 4 + k + 1)

        def norm_pe(pe, name):
            n, mean, nm, src = NORM[name]
            if mean:
                for k in range(DT):
                    src_ready(pe, name, k)
                    m = pe.matmul(pm[:, 0, 0:T], ones, src[:, k], start=k == 0, stop=k == DT - 1)
                m.then_inc(n_mean, 1)
            sq = SQ[name]
            for k in range(DT):
                pe.wait_ge(n_sq, 8 * n + k + 1)
                m = pe.matmul(pm[:, 1, 0:T], ones, sq[:, k], start=k == 0, stop=k == DT - 1)
            m.then_inc(n_sum, 1)

        def norm_act(act, name, shift, dst=None):
            n, mean, nm, src = NORM[name]
            sq = SQ[name]
            for k in range(DT):
                if mean:
                    act.wait_ge(n_xc, 8 * nm + k + 1)
                else:
                    src_ready(act, name, k)
                act.activation(sq[:, k], src[:, k], ACT.Square).then_inc(n_sq, 1)
            act.wait_ge(n_sum, n + 1)
            inv_sqrt(act, NR[:, 1], pm[:, 1, 0:T], D, 1 if mean else 0, n_std)
            for k in range(DT):
                act.wait_ge(n_t, 8 * n + k + 1)
                if name == "conv":
                    act.activation(H[:, k], sq[:, k], ACT.Silu, bias=shift(k)).then_inc(u_s, 1)
                    act.wait_ge(u_s, k + 1)
                    act.activation(UH[:, k], H[:, k], ACT.Copy).then_inc(u_hi, 1)
                else:
                    d_ = (HH if dst is None else dst)[:, k]
                    if shift is None:
                        act.activation(d_, sq[:, k], ACT.Copy).then_inc(n_hh, 1)
                    else:
                        act.activation(d_, sq[:, k], ACT.Identity, bias=shift(k)).then_inc(n_hh, 1)

        def inv_sqrt(act, dst, x, size, eps, done):
            act.activation(dst, x, ACT.Ln, bias=sc[:, eps:eps + 1], scale=1.0 / size).then_inc(ln_ok, 1)
            ln_count[0] += 1
            act.wait_ge(ln_ok, ln_count[0])
            act.activation(dst, dst, ACT.Exp, scale=-0.5).then_inc(done, 1)
        ln_count = [0]

        def norm_dve(v, name, scale, shift):
            n, mean, nm, src = NORM[name]
            sq = SQ[name]
            if mean:
                v.wait_ge(n_mean, nm + 1)
                for k in range(DT):
                    v.scalar_tensor_tensor(src[:, k], pm[:, 0, 0:T], -1.0 / D, src[:, k], ALU.mult, ALU.add)\
                     .then_inc(n_xc, 1)
            v.wait_ge(n_std, n + 1)
            for k in range(DT):
                v.scalar_tensor_tensor(sq[:, k], src[:, k], scale(k), NR[:, 1], ALU.mult, ALU.mult).then_inc(n_t, 1)
            if name == "ln2_1":
                return
            for k in range(DT):
                if name == "conv":
                    v.wait_ge(u_hi, k + 1)
                    v.tensor_tensor(UL[:, k], H[:, k], UH[:, k].bitcast(F32), ALU.subtract).then_inc(u_lo, 1)
                    continue
                v.wait_ge(n_hh, 8 * HN[name] + k + 1)
                if shift is None:
                    v.tensor_tensor(HL[:, k], sq[:, k], HH[:, k].bitcast(F32), ALU.subtract).then_inc(n_hl, 1)
                else:
                    v.scalar_tensor_tensor(HL[:, k], sq[:, k], shift(k), HH[:, k].bitcast(F32), ALU.add, ALU.subtract)\
                     .then_inc(n_hl, 1)

        def norm_pool(pool, name, shift, dst):
            n = NORM[name][0]
            for k in range(DT):
                pool.wait_ge(n_t, 8 * n + k + 1)
                pool.tensor_scalar(dst[:, k], SQ[name][:, k], shift(k) if shift else 0.0, None, ALU.add)\
                    .then_inc(full_ok, 1)

        def mod_col(i):
            return lambda k: MOD[:, i + k:i + k + 1]

        def par_col(name, i=0):
            return lambda k: pc(name, i + k)

        SQX = ar("SQX", 72, [P, DT, T])
        SQ = {name: SQX for name in NORM}
        SQ["mix"], SQ["conv"] = ACC, H

        ADA2 = ar("ADA2", 22, [P, 4 * D])
        NR4 = ar("NR4", 86, [P, NG, T])
        QKV = ar("QKV", 0, [P, 24, T])
        ZA = ar("ZA", 24, [P, 8, T])
        VT = ar("VT", 32, [P, NT, D])
        lm = ar("lm", 84, [P, 7, 2, P])
        gm = ar("gm", 80, [P, 7, P])
        KS = ar("KS", 40, [P, 2, T])
        LF = ar("LF", 42, [P, 2, 3 * P])
        LB = ar("LB", 45, [P, 2, 3 * P])
        DF = ar("DF", 48, [P, 2, 3 * P])
        DB = ar("DB", 51, [P, 2, 3 * P])
        ATT = ar("ATT", 54, [P, 2, 4 * P])
        KDX = ar("KDX", 58, [P, 2, 2 * P])
        AM = ar("AM", 60, [P, 2, 2, 4 * P])
        XI = ar("XI", 68, [P, 2, 4 * P])
        ZI = ar("ZI", 72, [P, 2, 4 * P])
        PS = ar("PS", 76, [P, 2, 4 * P])
        VN = ar("VN", 20, [P, 2, 4 * P])
        RH = ar("RH", 16, [P, 2, 2 * P])
        QK2 = ar("QK2", 0, [P, 8, T])
        VT2 = ar("VT2", 8, [P, NT, D])
        RG = ar("RG", 16, [P, 8, T])
        LA = ar("LA", 24, [P, 8, T])
        LT = ar("LT", 32, [P, 8, T])
        BS = ar("BS", 40, [P, 8, T])
        onet = ar("onet", 48, [P, T])
        gw = ar("gw", 49, [NH, 2, 512])
        glt = ar("glt", 53, [NH, T])
        BH = ar("BH", 54, [P, 2, T])
        QKH = ar("QKH", 56, [P, 2, T])
        VH = ar("VH", 58, [P, NT, T])
        DD = ar("DD", 60, [P, 2, 2, T])
        KQ = ar("KQ", 64, [P, 2, 2, T])
        SS = ar("SS", 68, [P, NT, T])
        XOUT = ar("XOUT", 0, [P, NT, D])

        ws1 = ar("ws1", 91, [P, DT, NH])
        ws2 = ar("ws2", 92, [P, DT, NH])
        ws3 = ar("ws3", 93, [P, DT, NH])

        dt_in, ba_in, gl_in = sem("dt_in"), sem("ba_in"), sem("gl_in")
        dt_p, dt_ok, sp_x, sp_e = sem("dt_p"), sem("dt_ok"), sem("sp_x"), sem("sp_e")
        ez = sem("ez")
        rest_part, rest_sum = sem("rest_part"), sem("rest_sum")
        u_s, u_hi, u_lo = sem("u_s"), sem("u_hi"), sem("u_lo")
        xbc_ok = sem("xbc_ok")
        xs_t, xs_ok, cb_p, cb_ok = sem("xs_t"), sem("xs_ok"), sem("cb_p"), sem("cb_ok")
        l_ok, seg_p, e_ok, m_ok, y_p, y_ok = (sem(k) for k in ("l_ok", "seg_p", "e_ok", "m_ok", "y_p", "y_ok"))
        ysq, ysum, ystd, yn, yhi, ylo = (sem(k) for k in ("ysq", "ysum", "ystd", "yn", "yhi", "ylo"))
        mg_ok, mg_hi, mg_lo = sem("mg_ok"), sem("mg_hi"), sem("mg_lo")
        hid_lo = sem("hid_lo")
        x_hi, x_lo = sem("x_hi"), sem("x_lo")
        mask2 = sem("mask2")
        yz_ok, hid_ok = sem("yz_ok"), sem("hid_ok")
        qkv_ok, ba_p, bet_ok, qkn_ok = (sem(k) for k in ("qkv_ok", "ba_p", "bet_ok", "qkn_ok"))
        l2_sq, l2_sum, l2_std = (sem(k) for k in ("l2_sq", "l2_sum", "l2_std"))
        vt_p, vt_ok, at_ok, am_ok, p_p, ps_ok, vw_p, xz_ok = (sem(k) for k in (
            "vt_p", "vt_ok", "at_ok", "am_ok", "p_p", "ps_ok", "vw_p", "xz_ok"))
        ks_ok, kq_p, gl_l, gs_p, gd_ok, qd_ok, s1_p, vn1, r_p, rh_ok, s2_p, vn2, go_p, go_ok = (sem(k) for k in (
            "ks_ok", "kq_p", "gl_l", "gs_p", "gd_ok", "qd_ok", "s1_p", "vn1", "r_p", "rh_ok", "s2_p", "vn2",
            "go_p", "go_ok"))
        mod0_ok = sem("mod0_ok")
        gz, gw_in, gl_p, gl_ok, lg_p, lt_ok, lt_e, bs_ok = (sem(k) for k in (
            "gz", "gw_in", "gl_p", "gl_ok", "lg_p", "lt_ok", "lt_e", "bs_ok"))
        st_ok, dd_ok, ee_ok, kq_ok, sc_p, s_ok, dg_p, dg_ok, bo_p, bo_ok = (sem(k) for k in (
            "st_ok", "dd_ok", "ee_ok", "kq_ok", "sc_p", "s_ok", "dg_p", "dg_ok", "bo_p", "bo_ok"))
        ot_p, ot_ok = sem("ot_p"), sem("ot_ok")
        cs = small("cs", 8)
        bet = small("bet", 2 * 16)[:].rearrange("p (t c) -> p t c", t=NT)
        gd = small("gd", 2 * 16)[:].rearrange("p (t c) -> p t c", t=NT)
        EV = {"xbc": 0, "ffn_in": 24, "a_qkv": 46, "mlp1_0": 70, "mlp1_1": 102}

        def bank(u, i):
            return (pm if u else acc)[:, i]

        def ffn_in_pe(pe):
            s = SEC["ffn_in"]

            def free(b, u, h, j):
                m = 2 * j + u // 2
                if u % 2 == 0:
                    pe.wait_ge(evac_a, 2 * m + EV["ffn_in"] + h - 1)
                else:
                    pe.wait_ge(acc_free, 4 * m + s.o0 + 2 * h + 2)
            pe_section(pe, s, hrhs, free=free, ready=lambda k: pe.wait_ge(n_hl, 8 * HN["ffn"] + k + 1))

        @block.gpsimd
        def _(pool):
            c = Chain(pool, gchain)
            c.link(pool.memset(ident[:], 0.0))
            c.link(pool.affine_select(out=ident[:], in_=ident[:], compare_op=ALU.not_equal, fill=1.0, base=0,
                                      pattern=[[-1, P]], channel_multiplier=1))
            pool.nop().then_inc(masks, 1)

            def tri(ap, cm, step, base_):
                c.link(pool.affine_select(out=ap, in_=ap, compare_op=ALU.is_ge, fill=0.0, base=base_,
                                          pattern=[[step, P]], channel_multiplier=cm))
            for m in (maskf, maskb, slo, suo):
                c.link(pool.memset(m[:], 1.0))
            tri(maskf[:, 0:P], -1, 1, 0)
            tri(maskf[:, 2 * P:], -1, 1, 0)
            tri(maskb[:, P:2 * P], 1, -1, 0)
            tri(maskb[:, 2 * P:], 1, -1, 0)
            tri(slo[:, 0:P], 1, -1, -1)
            tri(suo[:, 0:P], -1, 1, -1)
            pool.nop().then_inc(masks, 1)

            def lo_section(s):
                split_section(pool, split_lo, s, None)
            pool.wait_ge(mod0_ok, 1)
            norm_pool(pool, "mix", mod_col(0), H)
            lo_section(SEC["xbc"])
            lo_section(SEC["z"])
            lo_section(SEC["g"])
            for k in ("conv_out", "ssm_out", "w_out"):
                lo_section(SEC[k])
            pool.wait_ge(ylo, 16)
            for lv in range(7):
                b = 1 << lv
                nb = P // (2 * b)
                for d in range(2):
                    c.link(pool.memset(lm[:, lv, d], 0.0))
                    v = lm[:, lv, d].rearrange("p (n t b) -> p n t b", n=nb, t=2)[:, :, 1 - d]
                    c.link(pool.memset(v, 1.0))
                    lo_, hi_ = (0, b - 1) if d == 0 else (b, 2 * b - 1)
                    c.link(pool.affine_select(out=v, in_=v, compare_op=ALU.is_ge, fill=0.0, base=-lo_,
                                              pattern=[[-2 * b, nb], [0, b]], channel_multiplier=1))
                    c.link(pool.affine_select(out=v, in_=v, compare_op=ALU.is_ge, fill=0.0, base=hi_,
                                              pattern=[[2 * b, nb], [0, b]], channel_multiplier=-1))
            c.link(pool.tensor_tensor(gm[:], lm[:, :, 0], lm[:, :, 1], ALU.add))
            pool.nop().then_inc(mask2, 1)
            lo_section(SEC["a_qkv"])
            norm_pool(pool, "final", None, X)
            with pool.Fori(0, A_HEADS // 2) as j:
                c.loop(j, 0, A_HEADS // 2)
                for lv in range(7):
                    for u in range(2):
                        if lv == 0:
                            pool.wait_ge(at_ok, 2 * j + u + 1)
                        if lv >= 2:
                            pool.wait_ge(p_p, 14 * j + 2 * (lv - 2) + u + 1)
                        if lv == 2:
                            pool.wait_ge(xz_ok, 14 * j + u + 1)
                        m = lm[:, lv]
                        mask = bass.AP(tensor=m.tensor, offset=m.offset, ap=[m.ap[0], [P, 2], [0, 2], [1, P]])
                        pool.tensor_tensor(AM[:, u, lv % 2].rearrange("p (d t c) -> p d t c", d=2, t=2),
                                           ATT[:, u].rearrange("p (d t c) -> p d t c", d=2, t=2), mask,
                                           ALU.mult).then_inc(am_ok, 1)
                c.done()
            norm_pool(pool, "ln1_0", par_col("ln1_b"), X)
            norm_pool(pool, "ln2_0", par_col("ln2_b"), X)
            pool.wait_ge(n_hl, 8 * HN["ln2_0"] + 8)
            pool.memset(gw[:], 0.0).then_inc(gz, 1)
            pool.sem_inc(dd_ok, 1)
            with pool.Fori(0, B_HEADS) as h:
                c.loop(h, 0, B_HEADS)
                for lv in range(8):
                    b = 1 << lv
                    nb = T // (2 * b)
                    if lv == 0:
                        pool.wait_ge(st_ok, h + 1)
                    pool.wait_ge(kq_ok, 8 * h + lv + 1)

                    def half(ap, side):
                        return ap.rearrange("p (n t b) -> p n t b", n=nb, t=2)[:, :, side]

                    def edge(ap, side, i):
                        e = half(ap, side)[:, :, i:i + 1]
                        return bass.AP(tensor=e.tensor, offset=e.offset, ap=[e.ap[0], [2 * b, nb], [0, b]])
                    kd, qd = DD[:, lv % 2, 0], DD[:, lv % 2, 1]
                    f, r = BH[:, 0], BH[:, 1]
                    pool.tensor_tensor(half(kd, 0), edge(f, 0, b - 1), half(f, 0), ALU.subtract)
                    pool.tensor_tensor(half(kd, 1), edge(r, 1, 0), half(r, 1), ALU.subtract)
                    pool.tensor_tensor(half(qd, 0), half(r, 0), edge(r, 1, 0), ALU.subtract)
                    pool.tensor_tensor(half(qd, 1), half(f, 1), edge(f, 0, b - 1), ALU.subtract).then_inc(dd_ok, 1)
                c.done()
            norm_pool(pool, "ln1_1", par_col("ln1_b", 8), X)

        @block.scalar
        def _(act):
            c = Chain(act, achain)
            for ap, p0, i, m in pieces:
                act.dma_start(PRW[p0:p0 + m, i, :], ap).then_inc(par_in, 16)
            act.dma_start(dtb[:, 0:NH], bcast(a["dt_bias"][0], NH)).then_inc(dt_in, 16)
            act.dma_start(dtb[:, NH:], bcast(a["a_log"][0], NH)).then_inc(dt_in, 16)
            act.dma_start(dsk[:, 0:NH], bcast(a["d_skip"][0], NH)).then_inc(dt_in, 16)
            act.dma_start(gab[:, 0:16], bcast(a["a_dt_bias_2"][0].rearrange("d h -> (d h)"), 16)).then_inc(dt_in, 16)
            act.dma_start(gab[:, 16:32], bcast(a["a_alog_2"][0].rearrange("d h -> (d h)"), 16)).then_inc(dt_in, 16)
            for w_, src, off in ((ws1, w_in, OFF_DT), (ws2, a_in, A_BA), (ws3, b_in, B_GL)):
                act.dma_start(w_[:], src.rearrange("(k p) c -> p k c", p=P)[:, :, off:off + NH]).then_inc(dt_in, 16)
            for q in range(4):
                act.wait_ge(xt_p, q + 1)
                act.activation(X[:, 2 * q:2 * q + 2], acc[:, q].rearrange("p (d t) -> p d t", d=2), ACT.Copy)\
                   .then_inc(x_ok, 1)
            act.wait_ge(par_ok, 2)
            act.activation(cs[:], pc("c", 0, 8), ACT.Silu).then_inc(silu_c, 1)
            norm_act(act, "mix", mod_col(0))

            def o_hi(i):
                act.wait_ge(o_ok, i + 1)
                act.activation(HH[:], H[:], ACT.Copy).then_inc(n_hh, 8)

            def conv_b(b, u, h, j):
                tile_done(act, SEC["conv_b"], b, h)
                act.activation(G[:, ds(2 * b + h, 1)], acc[:, out_slot(SEC["conv_b"], u, h), 0:T], ACT.Sigmoid)\
                   .then_inc(acc_free, 1)
            split_section(act, split_hi, SEC["conv_b"], conv_b)
            split_section(act, split_hi, SEC["conv_a"], None)
            act.wait_ge(sp_x, 1)
            act.activation(spt[2][:], spt[1][:], ACT.Exp, scale=-1.0).then_inc(sp_e, 1)
            act.wait_ge(dt_in, 16 * 8)
            act.activation(dtb[:, NH:], dtb[:, NH:], ACT.Exp).then_inc(ez, 1)
            act.activation(gab[:, 16:32], gab[:, 16:32], ACT.Exp).then_inc(ez, 1)

            def conv_first(s, dst, w, bias):
                def evac(b, u, h, j):
                    tile_done(act, s, b, h)
                    act.activation(dst[:, ds(2 * b + h, 1)], acc[:, out_slot(s, u, h), 0:T], ACT.Identity,
                                   scale=pc(w[0], 2 * b + h + w[1]), bias=pc(bias, 2 * b + h) if bias else 0.0)\
                       .then_inc(evac_a, 1)
                return evac
            split_section(act, split_hi, SEC["xbc"], conv_first(SEC["xbc"], XBC, ("ssm_conv_w", 3 * 24), "ssm_conv_b"))

            def table_evac(s, dst, func):
                def evac(b, u, h, j):
                    tile_done(act, s, b, h)
                    act.activation(dst[:, ds(2 * b + h, 1)], acc[:, out_slot(s, u, h), 0:T], func)\
                       .then_inc(acc_free, 1)
                return evac
            split_section(act, split_hi, SEC["z"], table_evac(SEC["z"], Z, ACT.Silu))
            act.wait_ge(acc_free, SEC["xbc"].o0 + 24 + 4)
            act.activation(XBC[:], XBC[:], ACT.Silu).then_inc(xbc_ok, 1)
            act.sem_inc(e_ok, 2)
            gates = table_evac(SEC["g"], G, ACT.Sigmoid)
            with act.Fori(0, NG // 2) as j:
                for q in range(8):
                    b, ub, hb = 4 * j + q // 2, q // 2, q % 2
                    split_hi(act, SEC["g"], b + 1, ub + 1, hb)
                    for u in range(2):
                        act.wait_ge(seg_p, 16 * j + 2 * q + u + 3)
                        act.wait_ge(y_p, 16 * j + 2 * q + u + 1)
                        act.activation(ES[:, u], pm[:, u, 0:3 * P], ACT.Exp).then_inc(e_ok, 1)
                    gates(b, ub, hb, j)
            norm_act(act, "conv", par_col("conv_ln_b"))
            act.wait_ge(ysum, 1)
            inv_sqrt(act, NR4[:], pm[:, 0:2].rearrange("p b (g t) -> p (b g) t", g=2), D_INNER // NG, 0, ystd)
            for k in range(16):
                if k % 4 == 0:
                    act.wait_ge(yn, k // 4 + 1)
                act.activation(YH[:, k], XBC[:, k], ACT.Copy, scale=pc("ssm_norm_w", k)).then_inc(yhi, 1)
            split_section(act, split_hi, SEC["conv_out"], None)
            split_section(act, split_hi, SEC["ssm_out"], None)
            act.wait_ge(mg_ok, 1)
            act.activation(UH[:], H[:], ACT.Copy).then_inc(mg_hi, 1)
            split_section(act, split_hi, SEC["w_out"], None)
            act.wait_ge(mod_ok, 1)
            norm_act(act, "ffn", mod_col(24))

            def ffn_gate(b, u, h, j):
                if u % 2 == 0:
                    tile_done(act, SEC["ffn_in"], b, h)
                    q = (u // 2) * 2 + h
                    act.wait_ge(acc_free, 2 * b + SEC["ffn_in"].o0 + 2 * h - 2)
                    act.activation(TMP[:, q], acc[:, out_slot(SEC["ffn_in"], u, h), 0:T], ACT.Silu)\
                       .then_inc(evac_a, 1)
            split_section(act, split_hi, SEC["ffn_in"], ffn_gate)
            split_section(act, split_hi, SEC["ffn_down"], None)
            norm_act(act, "final", None)
            split_section(act, split_hi, SEC["a_qkv"], conv_first(SEC["a_qkv"], QKV, ("a_conv", 2 * 24), None))
            split_section(act, split_hi, SEC["a_z"], table_evac(SEC["a_z"], ZA, ACT.Silu))
            act.wait_ge(acc_free, SEC["a_qkv"].o0 + 24 + 4)
            act.activation(QKV[:], QKV[:], ACT.Silu).then_inc(qkv_ok, 1)
            act.wait_ge(ba_p, 1)
            act.activation(bet[:], pm[:, 2, 0:2 * NH].rearrange("p (t c) -> p t c", t=NT)[:, :, 0:16], ACT.Sigmoid)\
               .then_inc(bet_ok, 1)
            act.wait_ge(sp_x, 2)
            act.activation(spt[2][:, 0:32], spt[1][:, 0:32], ACT.Exp, scale=-1.0).then_inc(sp_e, 1)
            def l2_act(i, size):
                act.wait_ge(l2_sum, i + 1)
                inv_sqrt(act, SQX[:], acc[:].rearrange("p b (h t) -> p (b h) t", h=2), size, 0, l2_std)
            l2_act(0, 1)
            l2_act(1, 1)
            for q in range(4):
                act.wait_ge(vt_p, q + 1)
                act.activation(VT[:, q // 2, ds((q % 2) * 512, 512)], pm[:, q], ACT.Copy).then_inc(vt_ok, 1)
            with act.Fori(0, A_HEADS // 2) as j:
                for u in range(2):
                    act.wait_ge(go_p, 2 * j + u + 1)
                    act.activation(KS[:, u], QKV[:, ds(2 * j + u + 8, 1)], ACT.Copy).then_inc(ks_ok, 1)
                for u in range(2):
                    act.wait_ge(gs_p, 2 * j + u + 1)
                    act.activation(DF[:, u], bank(u, 2)[:, 0:3 * P], ACT.Exp)
                    act.activation(DB[:, u], bank(u, 3)[:, 0:3 * P], ACT.Exp).then_inc(gd_ok, 1)
                for lv in range(1, 7):
                    for u in range(2):
                        act.wait_ge(p_p, 14 * j + 2 * lv + u + 1)
                        act.activation(PS[:, u], bank(u, 0), ACT.Copy).then_inc(ps_ok, 1)
            l2_act(2, P)
            o_hi(0)
            split_section(act, split_hi, SEC["a_out"], None)
            norm_act(act, "ln1_0", par_col("ln1_b"))

            def mlp(k):
                s = SEC[f"mlp1_{k}"]

                def relu(b, u, h, j):
                    q = (2 * u + h) % 4
                    tile_done(act, s, b, h)
                    act.wait_ge(hid_lo, 2 * b + 32 * k + h + 1)
                    act.activation(TMP[:, q], acc[:, out_slot(s, u, h), 0:T], ACT.Relu).then_inc(acc_free, 1)
                    act.wait_ge(acc_free, 2 * b + s.o0 + h + 5)
                    act.activation(HIDH[:, ds(2 * b + h, 1)], TMP[:, q], ACT.Square).then_inc(evac_a, 1)
                split_section(act, split_hi, s, relu)
                split_section(act, split_hi, SEC[f"mlp2_{k}"], None)
                norm_act(act, f"ln2_{k}", par_col("ln2_b", 8 * k), X if k else None)
            mlp(0)

            act.wait_ge(gz, 1)
            for d in range(2):
                act.dma_start(gw[16 * d:16 * d + 16, d, :], a["b_gate_w2_2"][0, d]).then_inc(gw_in, 16)

            def b_qk(b, u, h, j):
                tile_done(act, SEC["b_qk"], b, h)
                act.activation(QK2[:, ds(2 * b + h, 1)], acc[:, out_slot(SEC["b_qk"], u, h), 0:T], ACT.Copy,
                               scale=P ** -0.5 if b < 2 else 1.0).then_inc(acc_free, 1)

            def b_v(b, u, h, j):
                tile_done(act, SEC["b_v"], b, h)
                act.activation(VT2[:, :, ds((2 * b + h) * P, P)],
                               acc[:, out_slot(SEC["b_v"], u, h), 0:T].rearrange("p (t c) -> p t c", t=NT), ACT.Copy)\
                   .then_inc(acc_free, 1)
            split_section(act, split_hi, SEC["b_qk"], b_qk)
            split_section(act, split_hi, SEC["b_v"], b_v)
            split_section(act, split_hi, SEC["b_r"], table_evac(SEC["b_r"], RG, ACT.Silu))
            act.wait_ge(gl_p, 1)
            act.activation(glt[:], pm[0:NH, 2, 0:T], ACT.Copy).then_inc(gl_ok, 1)
            act.wait_ge(lt_ok, 1)
            act.activation(LT[:], LT[:], ACT.Exp, scale=-1.0).then_inc(lt_e, 1)
            act.wait_ge(lt_e, 1)
            act.activation(LT[:], LT[:], ACT.Ln, bias=1.0).then_inc(lt_e, 1)
            act.sem_inc(ee_ok, 1)
            with act.Fori(0, B_HEADS) as h:
                act.wait_ge(bs_ok, 1)
                act.wait_ge(kq_ok, 8 * h + 2)
                act.wait_ge(dd_ok, 8 * h + 1)
                act.wait_ge(bo_p, h + 1)
                act.activation(BH[:], BS[:].rearrange("p (d h) t -> p d h t", d=2)[:, :, ds(h, 1)], ACT.Copy)
                act.activation(QKH[:, 1], QK2[:, ds(h, 1)], ACT.Copy)
                act.activation(QKH[:, 0], QK2[:, ds(h + 4, 1)], ACT.Copy)
                act.activation(VH[:], VT2[:, :, ds(h * T, T)], ACT.Copy).then_inc(st_ok, 1)
                for lv in range(8):
                    act.wait_ge(dd_ok, 8 * h + lv + 2)
                    act.activation(DD[:, lv % 2], DD[:, lv % 2], ACT.Exp, scale=1.0 / 16).then_inc(ee_ok, 1)
            l2_act(3, T)
            o_hi(1)
            split_section(act, split_hi, SEC["b_out"], None)
            norm_act(act, "ln1_1", par_col("ln1_b", 8))
            mlp(1)
            for q in range(4):
                act.wait_ge(ot_p, q + 1)
                act.activation(XOUT[:, q // 2, ds((q % 2) * 512, 512)], pm[:, q], ACT.Copy).then_inc(ot_ok, 1)
            for tk in range(NT):
                act.wait_ge(ot_ok, 2 * tk + 2)
                act.dma_start(out[0].rearrange("(t p) d -> p t d", p=P)[:, tk], XOUT[:, tk]).then_inc(out_sem, 16)

        @block.vector
        def _(v):
            c = Chain(v, vchain)
            c.link(v.memset(sc[:, 0:1], RMS_EPS))
            c.link(v.memset(sc[:, 1:2], LN_EPS))
            for bk in range(2):
                v.wait_ge(par_t, bk + 1)
                n = min(512, NPAR - 512 * bk)
                v.tensor_copy(par[:, 512 * bk:512 * bk + n], pm[:, bk, 0:n]).then_inc(par_ok, 1)
            v.wait_ge(par_ok, 2)
            v.wait_ge(silu_c, 1)

            def ada_step(dst, src, k, first, free):
                if first:
                    ins = v.tensor_scalar(dst, src, cs[:, k:k + 1], None, ALU.mult)
                else:
                    ins = v.scalar_tensor_tensor(dst, src, cs[:, k:k + 1], dst, ALU.mult, ALU.add)
                if free:
                    ins.then_inc(ada_used, 1)
                else:
                    c.link(ins)

            for n, (name, b) in enumerate(ADA_FIRST):
                v.wait_ge(landed[n % 4], 16 * (n // 4 + 1))
                if n:
                    v.wait_ge(ada_used, n)
                ada_step(ADA[:], raw[:, n % 4].rearrange("p k c -> p (k c)"), b, b == 0, True)
            v.wait_ge(ada_used, len(ADA_FIRST))
            v.nop().then_inc(ada_part, 1)
            v.wait_ge(ada_sum, 1)
            c.link(v.tensor_tensor(MOD[:, 0:16], pm[:, 3, 0:16], pc("b_ada_mix", 0, 16), ALU.add))
            c.link(v.scalar_tensor_tensor(MOD[:, 8:16], MOD[:, 8:16], 1.0, pc("norm_mix_w", 0, 8), ALU.add, ALU.mult))
            v.nop().then_inc(mod0_ok, 1)
            norm_dve(v, "mix", mod_col(8), mod_col(0))

            def o_lo(i, name):
                v.nop().then_inc(o_ok, 1)
                v.wait_ge(n_hh, 8 * HN[name] + 8)
                v.tensor_tensor(HL[:], H[:], HH[:].bitcast(F32), ALU.subtract).then_inc(n_hl, 8)
            c.link(v.memset(UP[:], 0.0))
            split_section(v, split_lo, SEC["conv_b"], None)

            def conv_a(b, u, h, j):
                tile_done(v, SEC["conv_a"], b, h)
                v.tensor_tensor(UP[:, ds(2 * b + h, 1), CW - 1:], acc[:, out_slot(SEC["conv_a"], u, h), 0:T],
                                G[:, ds(2 * b + h, 1)], ALU.mult).then_inc(acc_free, 1)
            v.wait_ge(acc_free, 8 + 4)
            split_section(v, split_lo, SEC["conv_a"], conv_a)

            def softplus(n, x, dst):
                ax, e, s_, = spt[1][:, 0:x.shape[1]], spt[2][:, 0:x.shape[1]], spt[3][:, 0:x.shape[1]]
                c.link(v.scalar_tensor_tensor(ax, x, -1.0, x, ALU.mult, ALU.max))
                v.nop().then_inc(sp_x, 1)
                v.wait_ge(sp_e, n + 1)
                c.link(v.tensor_scalar(ax, e, 2.0, None, ALU.add))
                c.link(v.reciprocal(ax, ax))
                c.link(v.tensor_tensor(e, e, ax, ALU.mult))
                c.link(v.tensor_tensor(s_, e, e, ALU.mult))
                c.link(v.tensor_scalar(ax, s_, 1.0 / 17, None, ALU.mult))
                for k in range(7, 0, -1):
                    c.link(v.scalar_tensor_tensor(ax, ax, 1.0 / (2 * k + 1), s_, ALU.add, ALU.mult))
                c.link(v.scalar_tensor_tensor(ax, ax, 1.0, e, ALU.add, ALU.mult))
                c.link(v.tensor_scalar(ax, ax, 2.0, None, ALU.mult))
                c.link(v.scalar_tensor_tensor(dst, x, 0.0, ax, ALU.max, ALU.add))

            v.wait_ge(dt_in, 16 * 8)
            v.wait_ge(dt_p, 1)
            for tk in range(NT):
                c.link(v.tensor_tensor(spt[0][:, tk * NH:tk * NH + NH], pm[:, 2, tk * NH:tk * NH + NH],
                                       dtb[:, 0:NH], ALU.add))
            softplus(0, spt[0][:, 0:2 * NH], dtt[:])
            v.wait_ge(ez, 1)
            for tk in range(NT):
                c.link(v.scalar_tensor_tensor(dat[:, tk * NH:tk * NH + NH], dtt[:, tk * NH:tk * NH + NH], -1.0,
                                              dtb[:, NH:], ALU.mult, ALU.mult))
            c.link(v.tensor_copy(dsk[0:64, NH:], dsk[0:64, 0:NH:2]))
            c.link(v.tensor_copy(dsk[64:P, NH:], dsk[64:P, 1:NH:2]))

            def conv_rest(s, dst, w, taps):
                def evac(b, u, h, j):
                    i = 2 * b + h
                    q = acc[:, out_slot(s, u, h), :]
                    v.wait_ge(evac_a, EV[s.name] + 2 * b + h + 1)
                    for n, (tap, sh) in enumerate(taps):
                        o0_, o1 = (sh, T) if sh > 0 else (0, T + sh)
                        d_ = dst[:, ds(i, 1), o0_:o1]
                        x_ = q[:, o0_ - sh:o1 - sh]
                        ins = v.scalar_tensor_tensor(d_, x_, pc(w, i + 24 * tap), d_, ALU.mult, ALU.add)
                        if n == len(taps) - 1:
                            ins.then_inc(acc_free, 1)
                        else:
                            c.link(ins)
                return evac
            split_section(v, None, SEC["xbc"], conv_rest(SEC["xbc"], XBC, "ssm_conv_w", [(2, 1), (1, 2), (0, 3)]),
                          c, 4 * 2 * 2)
            def tap(pair, w_, u):
                i = 2 * pair + u
                src = UP[:, ds(i, 1), w_:w_ + T]
                d_ = ACC[:, ds(i, 1)]
                wt = pc("conv_dw_w", i + w_ * DT)
                if w_ == 0:
                    c.tick(v.tensor_scalar(d_, src, wt, pc("conv_dw_b", i), ALU.mult, ALU.add))
                else:
                    c.wait(1)
                    c.tick(v.scalar_tensor_tensor(d_, src, wt, d_, ALU.mult, ALU.add))
            with v.Fori(0, DT // 4) as j:
                c.loop(j, 2 * CW, DT // 4)
                for w_ in range(CW):
                    for u in range(2):
                        tap(j, w_, u)
                c.done()
            for gi in range(NG):
                v.wait_ge(cb_p, gi + 1)
                v.tensor_tensor(CB[:, gi], acc[:, gi, 0:3 * P], maskf[:], ALU.mult).then_inc(cb_ok, 1)

            def xs_copy(g_, slot, tk):
                v.wait_ge(xs_t, 2 * g_ + tk + 1)
                v.tensor_copy(XT[:, slot, tk], pm[:, 3]).then_inc(xs_ok, 1)
            for tk in range(NT):
                xs_copy(0, 0, tk)
            v.wait_ge(cb_ok, 4)
            v.sem_inc(y_ok, 1)
            steps = [(w_, u) for w_ in range(CW) for u in range(2)]
            with v.Fori(0, NG // 2) as j:
                c.loop(j, 8 * 4 + 2 * CW, NG // 2)
                for q in range(8):
                    gq = q // 4
                    h0 = 16 * j + 2 * q
                    for u in range(2):
                        h = h0 + u
                        v.wait_ge(seg_p, h + 1)
                        v.tensor_scalar(LS[:, u, 0:P], slo[:, 0:P], dat[:, ds(h, 1)], None, ALU.mult)
                        v.tensor_scalar(LS[:, u, P:], slo[:], dat[:, ds(h + NH, 1)], None, ALU.mult).then_inc(l_ok, 1)
                    if q % 4 == 0:
                        v.wait_ge(xs_ok, 4 * j + 2 * gq + 3)
                    for u in range(2):
                        h = h0 + u
                        v.wait_ge(y_p, h + 1)
                        hc = (2 * (q % 4) + u) * 64
                        for tk in range(NT):
                            c.tick(v.tensor_scalar(XD[:, u, tk], XT[:, gq, tk, hc:hc + 64],
                                                   dtt[:, ds(h + tk * NH, 1)], None, ALU.mult))
                    scaled = c.n
                    for w_, u in steps[q * 62 // 8:(q + 1) * 62 // 8]:
                        tap(j + 2, w_, u)
                    if q % 4 in (1, 2):
                        xs_copy(2 * j + gq + 1, 1 - gq, q % 4 - 1)
                    c.wait(c.n - scaled)
                    for u in range(2):
                        v.wait_ge(e_ok, h0 + u + 3)
                        v.tensor_tensor(ES[:, u], ES[:, u], CB[:, ds(2 * j + gq, 1)], ALU.mult).then_inc(m_ok, 1)
                    v.wait_ge(y_p, h0 + 4)
                    yi = 8 * j + q
                    yt = XBC[:, ds(yi, 1)]
                    ins = v.scalar_tensor_tensor(yt, yt, dsk[:, ds(yi + NH, 1)], pm[:, 2, 0:T], ALU.mult, ALU.add)
                    ins.then_inc(y_ok, 1)
                    v.wait_ge(y_ok, yi + 2)
                    v.tensor_tensor(yt, yt, Z[:, ds(yi, 1)], ALU.mult).then_inc(yz_ok, 1)
                c.done()
            c.wait()
            v.nop().then_inc(conv_ok, 1)
            v.wait_ge(yz_ok, 16)
            v.wait_ge(w_used, SEC["conv_out"].t0 + 4)
            v.tensor_tensor(YSQ[:], XBC[:, 0:16], XBC[:, 0:16], ALU.mult).then_inc(ysq, 1)
            norm_dve(v, "conv", par_col("conv_ln_w"), par_col("conv_ln_b"))
            v.wait_ge(ystd, 1)
            for gi in range(NG):
                v.tensor_tensor(XBC[:, 4 * gi:4 * gi + 4], XBC[:, 4 * gi:4 * gi + 4], each(NR4[:, gi], 4), ALU.mult)\
                 .then_inc(yn, 1)
            for k in range(16):
                v.wait_ge(yhi, k + 1)
                v.scalar_tensor_tensor(YL[:, k], XBC[:, k], pc("ssm_norm_w", k), YH[:, k].bitcast(F32), ALU.mult,
                                       ALU.subtract).then_inc(ylo, 1)
            v.wait_ge(ylo, 16)

            def ada_rest(n):
                name, b = ADA_REST[n]
                n8 = n + len(ADA_FIRST)
                gb = ADA_AT[n8]
                v.wait_ge(landed[gb % 4], 16 * (gb // 4 + 1))
                v.wait_ge(ada_used, n8)
                r = raw[:, gb % 4].rearrange("p k c -> p (k c)")
                if b < 8:
                    ada_step(ADA2[:, D:3 * D], r, b, b == 0, True)
                else:
                    dst = ADA2[:, 0:D] if name == "w_ada_mix" else ADA2[:, 3 * D:]
                    ada_step(dst, r[:, 0:D], 2 * (b - 8), b == 8, False)
                    ada_step(dst, r[:, D:], 2 * (b - 8) + 1, False, True)

            def conv_out(b, u, h, j):
                tile_done(v, SEC["conv_out"], b, h)
                i = 2 * b + h
                v.tensor_tensor(H[:, ds(i, 1)], acc[:, out_slot(SEC["conv_out"], u, h), 0:T], G[:, ds(i, 1)], ALU.mult)\
                 .then_inc(acc_free, 1)
            split_section(v, None, SEC["conv_out"], conv_out, extra=ada_rest)

            def ssm_out(b, u, h, j):
                s = SEC["ssm_out"]
                tile_done(v, s, b, h)
                i = 4 * j + 2 * (u // 2) + h
                gt = G[:, ds(i + 8, 1)]
                v.tensor_tensor(gt, acc[:, out_slot(s, u, h), 0:T], gt, ALU.mult).then_inc(acc_free, 1)
                v.wait_ge(acc_free, 4 * j + s.o0 + 2 * (u // 2) + h + 5)
                c.tick(v.tensor_tensor(H[:, ds(i, 1)], H[:, ds(i, 1)], gt, ALU.add))
            v.wait_ge(acc_free, SEC["ssm_out"].o0 + 4)
            split_section(v, None, SEC["ssm_out"], ssm_out, c, 4, extra=lambda b: ada_rest(4 + b))
            c.wait()
            v.nop().then_inc(mg_ok, 1)
            v.wait_ge(mg_hi, 1)
            v.tensor_tensor(UL[:], H[:], UH[:].bitcast(F32), ALU.subtract).then_inc(mg_lo, 1)
            v.wait_ge(ada_used, 8 + 12)
            v.nop().then_inc(rest_part, 1)
            v.wait_ge(rest_sum, 1)
            c.link(v.tensor_tensor(MOD[:, 16:24], pm[:, 3, 0:8], pc("b_ada_mix", 16, 8), ALU.add))
            c.link(v.tensor_tensor(MOD[:, 24:40], pm[:, 3, 8:24], pc("b_ada_ffn", 0, 16), ALU.add))
            c.link(v.scalar_tensor_tensor(MOD[:, 32:40], MOD[:, 32:40], 1.0, pc("norm_ffn_w", 0, 8), ALU.add, ALU.mult))
            v.nop().then_inc(mod_ok, 1)

            def residual(s, scale):
                def evac(b, u, h, j):
                    tile_done(v, s, b, h)
                    i = 2 * b + h if s.chunks == 1 else 2 * j + h
                    xt_, ot = X[:, ds(i, 1)], acc[:, out_slot(s, u, h), 0:T]
                    if scale is None:
                        v.scalar_tensor_tensor(xt_, xt_, ALPHA, ot, ALU.mult, ALU.add).then_inc(acc_free, 1)
                    else:
                        v.scalar_tensor_tensor(xt_, ot, MOD[:, ds(i + scale, 1)], xt_, ALU.mult, ALU.add)\
                         .then_inc(acc_free, 1)
                return evac
            split_section(v, None, SEC["w_out"], residual(SEC["w_out"], 16), extra=lambda b: ada_rest(12 + b))
            v.wait_ge(ada_used, 8 + 16)
            v.nop().then_inc(rest_part, 1)
            v.wait_ge(rest_sum, 2)
            c.link(v.tensor_tensor(MOD[:, 40:48], pm[:, 3, 24:32], pc("b_ada_ffn", 16, 8), ALU.add))
            norm_dve(v, "ffn", mod_col(32), mod_col(24))

            def ffn_up(b, u, h, j):
                s = SEC["ffn_in"]
                if u % 2 == 1:
                    tile_done(v, s, b, h)
                    q = (u // 2) * 2 + h
                    pair2 = 4 * j + 2 * (u // 2) + h
                    v.wait_ge(evac_a, EV["ffn_in"] + 4 * j + 2 * (u // 2) + h + 1)
                    v.tensor_tensor(TMQ[:, q], acc[:, out_slot(s, u, h), 0:T], TMP[:, q], ALU.mult)\
                     .then_inc(acc_free, 2)
                    v.wait_ge(acc_free, 8 * j + s.o0 + 4 * (u // 2) + 2 * h + 6)
                    c.link(v.tensor_copy(HIDH[:, ds(pair2, 1)], TMQ[:, q]))
                    c.tick(v.tensor_tensor(HIDL[:, ds(pair2, 1)], TMQ[:, q],
                                           HIDH[:, ds(pair2, 1)].bitcast(F32), ALU.subtract))
                    c.wait()
            split_section(v, split_lo, SEC["ffn_in"], ffn_up, c, 8)
            v.nop().then_inc(hid_ok, 1)
            split_section(v, split_lo, SEC["ffn_down"], residual(SEC["ffn_down"], 40))
            norm_dve(v, "final", par_col("final_norm_w"), None)
            split_section(v, None, SEC["a_qkv"],
                          conv_rest(SEC["a_qkv"], QKV, "a_conv", [(0, 2), (1, 1), (3, -1), (4, -2)]), c, 4 * 2 * 3)
            split_section(v, split_lo, SEC["a_z"], None)
            v.wait_ge(ba_p, 1)
            v.wait_ge(bet_ok, 1)
            for tk in range(NT):
                c.link(v.tensor_tensor(spt[0][:, 16 * tk:16 * tk + 16], pm[:, 2, NH * tk + 16:NH * tk + NH],
                                       gab[:, 0:16], ALU.add))
            softplus(1, spt[0][:, 0:32], gd[:].rearrange("p t c -> p (t c)"))
            v.wait_ge(ez, 2)
            for tk in range(NT):
                c.link(v.scalar_tensor_tensor(gd[:, tk], gd[:, tk], -1.0, gab[:, 16:32], ALU.mult, ALU.mult))
            v.wait_ge(qkv_ok, 1)
            for i in range(2):
                q8 = QKV[:, 8 * i:8 * i + 8]
                v.tensor_tensor(SQX[:], q8, q8, ALU.mult).then_inc(l2_sq, 1)
                v.wait_ge(l2_std, i + 1)
                flat = "p k t -> p (k t)"
                c.link(v.scalar_tensor_tensor(q8.rearrange(flat), q8.rearrange(flat), P ** -0.5 if i == 0 else 1.0,
                                              SQX[:].rearrange(flat), ALU.mult, ALU.mult))
            v.nop().then_inc(qkn_ok, 1)
            v.wait_ge(vt_ok, 4)
            v.wait_ge(mask2, 1)
            v.sem_inc(go_ok, 2)
            with v.Fori(0, A_HEADS // 2) as j:
                NK = 2 * (2 + 3) + 2 * 6
                c.loop(j, NK, A_HEADS // 2)

                def gcol(t_, d, tk, u):
                    return t_[:, tk, ds(2 * j + u + 8 * d, 1)]
                for u in range(2):
                    v.wait_ge(go_p, 2 * j + u + 1)
                    v.tensor_scalar(LF[:, u, 0:P], slo[:, 0:P], gcol(gd, 0, 0, u), None, ALU.mult)
                    v.tensor_scalar(LF[:, u, P:], slo[:], gcol(gd, 0, 1, u), None, ALU.mult)
                    v.tensor_scalar(LB[:, u, 0:P], suo[:, 0:P], gcol(gd, 1, 1, u), None, ALU.mult)
                    v.tensor_scalar(LB[:, u, P:], suo[:], gcol(gd, 1, 0, u), None, ALU.mult).then_inc(gl_l, 1)
                for u in range(2):
                    kk, qk = bank(u, 0), bank(u, 1)
                    v.wait_ge(gd_ok, 2 * j + u + 1)
                    c.tick(v.tensor_tensor(DF[:, u], DF[:, u], maskf[:], ALU.mult))
                    c.link(v.tensor_tensor(DB[:, u], DB[:, u], maskb[:], ALU.mult))
                    v.wait_ge(kq_p, 2 * j + u + 1)
                    for n, (dd_, d0, tk, d) in enumerate(((DF, 0, 0, 0), (DF, 2, 1, 0), (DB, 2, 0, 1), (DB, 1, 1, 1))):
                        ins = v.scalar_tensor_tensor(ATT[:, u, n * P:n * P + P], dd_[:, u, d0 * P:d0 * P + P],
                                                     gcol(bet, d, tk, u), kk[:, (0 if tk == 0 else 3) * P:][:, 0:P],
                                                     ALU.mult, ALU.mult)
                    c.tick(v.tensor_tensor(KDX[:, u, 0:P], DF[:, u, P:2 * P], kk[:, P:2 * P], ALU.mult))
                    v.tensor_tensor(KDX[:, u, P:], DB[:, u, 0:P], kk[:, 2 * P:3 * P], ALU.mult).then_inc(at_ok, 1)
                    v.wait_ge(at_ok, 2 * j + u + 1)
                    c.tick(v.tensor_tensor(DF[:, u, 0:2 * P], DF[:, u, 0:2 * P], qk[:, 0:2 * P], ALU.mult))
                    c.tick(v.tensor_tensor(DF[:, u, 2 * P:], DF[:, u, 2 * P:], qk[:, 3 * P:], ALU.mult))
                    v.tensor_tensor(DB[:, u, 0:2 * P], DB[:, u, 0:2 * P], qk[:, 2 * P:], ALU.mult)
                    v.tensor_tensor(DB[:, u, 2 * P:], DB[:, u, 2 * P:], qk[:, 0:P], ALU.mult).then_inc(qd_ok, 1)
                id4 = bass.AP(tensor=ident[:].tensor, offset=ident[:].offset, ap=[ident[:].ap[0], [0, 4], [1, P]])
                for lv in range(7):
                    for u in range(2):
                        x4 = XI[:, u].rearrange("p (s c) -> p s c", s=4)
                        z4 = ZI[:, u].rearrange("p (s c) -> p s c", s=4)
                        if lv == 0:
                            v.wait_ge(am_ok, 14 * j + u + 1)
                            c.tick(v.tensor_tensor(z4, id4, AM[:, u, 0].rearrange("p (s c) -> p s c", s=4), ALU.subtract))
                            v.wait_ge(p_p, 14 * j + u + 1)
                            v.tensor_tensor(x4, id4, bank(u, 0).rearrange("p (s c) -> p s c", s=4), ALU.subtract)\
                             .then_inc(xz_ok, 1)
                        else:
                            v.wait_ge(vw_p, 12 * j + 2 * (lv - 1) + u + 1)
                            if lv < 6:
                                c.tick(v.tensor_tensor(XI[:, u], XI[:, u], bank(u, 1), ALU.subtract))
                            v.tensor_tensor(ZI[:, u], ZI[:, u], bank(u, 2), ALU.subtract).then_inc(xz_ok, 1)
                for u in range(2):
                    v.wait_ge(s1_p, 2 * j + u + 1)
                    b3 = bank(u, 3)
                    v.tensor_scalar(VN[:, u, 0:P], b3[:, 0:P], gcol(bet, 0, 0, u), None, ALU.mult)
                    v.tensor_scalar(VN[:, u, 3 * P:], b3[:, P:2 * P], gcol(bet, 1, 1, u), None, ALU.mult).then_inc(vn1, 1)
                for u in range(2):
                    v.wait_ge(r_p, 2 * j + u + 1)
                    b3 = bank(u, 3)
                    hc = ds((2 * j + u) * P, P)
                    v.tensor_tensor(RH[:, u, 0:P], VT[:, 1, hc], b3[:, 2 * P:3 * P], ALU.subtract)
                    v.tensor_tensor(RH[:, u, P:], VT[:, 0, hc], b3[:, 3 * P:], ALU.subtract).then_inc(rh_ok, 1)
                for u in range(2):
                    v.wait_ge(s2_p, 2 * j + u + 1)
                    b3 = bank(u, 3)
                    v.tensor_scalar(VN[:, u, P:2 * P], b3[:, 0:P], gcol(bet, 0, 1, u), None, ALU.mult)
                    v.tensor_scalar(VN[:, u, 2 * P:3 * P], b3[:, P:2 * P], gcol(bet, 1, 0, u), None, ALU.mult)\
                     .then_inc(vn2, 1)
                for u in range(2):
                    v.wait_ge(go_p, 2 * j + u + 3)
                    v.tensor_copy(H[:, ds(2 * j + u, 1)], bank(u, 1)[:, 0:T]).then_inc(go_ok, 1)
                c.done()
            v.wait_ge(go_ok, 8 + 2)

            def head_norm(i):
                v.tensor_tensor(SQX[:], H[:], H[:], ALU.mult).then_inc(l2_sq, 1)
                v.wait_ge(l2_std, i + 1)
                c.link(v.tensor_tensor(H[:], H[:], SQX[:], ALU.mult))
            head_norm(2)
            flat = "p k t -> p (k t)"
            c.link(v.scalar_tensor_tensor(H[:].rearrange(flat), H[:].rearrange(flat), pc("a_norm_g", 0),
                                          ZA[:].rearrange(flat), ALU.mult, ALU.mult))
            o_lo(0, "gdn")
            v.wait_ge(full_ok, 8 * FULL["final"] + 8)
            split_section(v, split_lo, SEC["a_out"], residual(SEC["a_out"], None))
            norm_dve(v, "ln1_0", par_col("ln1_g"), par_col("ln1_b"))

            def mlp(k):
                s = SEC[f"mlp1_{k}"]
                if k == 0:
                    v.sem_inc(hid_lo, 4)

                def lo(b, u, h, j):
                    q = (2 * u + h) % 4
                    i = 2 * b + h
                    v.wait_ge(evac_a, EV[s.name] + 2 * b + h + 1)
                    c.link(v.tensor_tensor(TMQ[:, q], TMP[:, q], TMP[:, q], ALU.mult))
                    v.tensor_tensor(HIDL[:, ds(i, 1)], TMQ[:, q], HIDH[:, ds(i, 1)].bitcast(F32), ALU.subtract)\
                     .then_inc(hid_lo, 1)
                split_section(v, split_lo, s, lo, c, 8)
                s2 = SEC[f"mlp2_{k}"]
                v.wait_ge(full_ok, 8 * FULL[f"ln1_{k}"] + 8)
                split_section(v, split_lo, s2, residual(s2, None))
                norm_dve(v, f"ln2_{k}", par_col("ln2_g", 8 * k), par_col("ln2_b", 8 * k))
            mlp(0)
            for name in ("b_qk", "b_v", "b_r"):
                split_section(v, split_lo, SEC[name], None)
            c.link(v.memset(onet[:], 1.0))
            v.wait_ge(lg_p, 1)
            for d in range(2):
                for k in range(4):
                    i = 4 * d + k
                    c.tick(v.tensor_scalar(LA[:, i], acc[:, i // 2, (i % 2) * T:(i % 2) * T + T], pc("gate_b", i), None, ALU.add))
            c.wait()
            flat = "p k t -> p (k t)"
            v.scalar_tensor_tensor(LT[:].rearrange(flat), LA[:].rearrange(flat), -1.0, LA[:].rearrange(flat),
                                   ALU.mult, ALU.max).then_inc(lt_ok, 1)
            v.wait_ge(lt_e, 2)
            c.link(v.scalar_tensor_tensor(LA[:].rearrange(flat), LA[:].rearrange(flat), 0.0, LT[:].rearrange(flat),
                                          ALU.min, ALU.subtract))
            for i in range(8):
                c.tick(v.tensor_tensor_scan(BS[:, i], onet[:], LA[:, i], 0.0, ALU.mult, ALU.add))
            c.wait()
            v.tensor_tensor(BS[:, 4:8], LA[:, 4:8], BS[:, 4:8], ALU.subtract).then_inc(bs_ok, 1)
            v.sem_inc(kq_ok, 2)
            v.sem_inc(s_ok, 4)
            v.sem_inc(bo_ok, 2)
            with v.Fori(0, B_HEADS) as h:
                diag = SS[:, 0, 0:P]
                diag = bass.AP(tensor=diag.tensor, offset=diag.offset, ap=[diag.ap[0], [T + P, 2], [1, P]])
                cross = SS[:, 0, P:T]
                cross = bass.AP(tensor=cross.tensor, offset=cross.offset, ap=[cross.ap[0], [P, 2], [1, P]])
                id2 = bass.AP(tensor=ident[:].tensor, offset=ident[:].offset, ap=[ident[:].ap[0], [0, 2], [1, P]])
                v.wait_ge(dg_p, h + 1)
                v.wait_ge(bo_p, h + 1)
                v.scalar_tensor_tensor(diag, acc[:, 3, 0:T].rearrange("p (t c) -> p t c", t=2), 2.0, id2,
                                       ALU.mult, ALU.mult).then_inc(dg_ok, 1)
                def scores(lv):
                    return pm[:, lv % 4, 0:T].rearrange("p (t c) -> p t c", t=2)

                def take(lv):
                    m = gm[:, lv]
                    mask = bass.AP(tensor=m.tensor, offset=m.offset, ap=[m.ap[0], [0, 2], [1, P]])
                    v.copy_predicated(diag, mask.bitcast(I32), scores(lv)).then_inc(s_ok, 1)

                for lv in range(8):
                    v.wait_ge(ee_ok, 8 * h + lv + 2)
                    if lv == 2:
                        v.wait_ge(dg_ok, h + 1)
                    if lv > 2:
                        v.wait_ge(s_ok, 8 * h + lv + 2)
                    v.wait_ge(sc_p, 8 * h + lv + 1)
                    v.tensor_tensor(KQ[:, lv % 2], DD[:, lv % 2], QKH[:], ALU.mult).then_inc(kq_ok, 1)
                    if lv >= 2:
                        take(lv - 2)
                v.wait_ge(s_ok, 8 * h + 6 + 4)
                v.wait_ge(sc_p, 8 * h + 8 + 2)
                v.tensor_copy(cross, scores(7)).then_inc(s_ok, 1)
                take(6)
                for e in range(2):
                    v.wait_ge(bo_p, h + 2)
                    v.tensor_copy(H[:, ds(2 * h + e, 1)], acc[:, e, 0:T]).then_inc(bo_ok, 1)
            v.wait_ge(bo_ok, 8 + 2)
            head_norm(3)
            for k in range(8):
                c.tick(v.scalar_tensor_tensor(H[:, k], H[:, k], pc("b_norm_g", k % 2), RG[:, k], ALU.mult, ALU.mult))
            c.wait()
            o_lo(1, "gla")
            v.wait_ge(full_ok, 8 * FULL["ln2_0"] + 8)
            split_section(v, split_lo, SEC["b_out"], residual(SEC["b_out"], None))
            norm_dve(v, "ln1_1", par_col("ln1_g", 8), par_col("ln1_b", 8))
            mlp(1)

        @block.tensor
        def _(pe):
            pe.sem_inc(w_used, 4)
            pe.sem_inc(acc_free, 4)
            pe.wait_ge(masks, 2)
            pe.wait_ge(x_in, 16)
            for q in range(4):
                for i in range(4):
                    d_, tk = 2 * q + i // 2, i % 2
                    m = pe.transpose(acc[:, q, i * P:i * P + P], XIN[:, tk, d_ * P:d_ * P + P], ident[:])
                m.then_inc(xt_p, 1)
            pe.wait_ge(par_in, 16 * len(pieces))
            for bk in range(2):
                for i in range(4 * bk, min(4 * bk + 4, NPT)):
                    n = min(P, NPAR - P * i)
                    m = pe.transpose(pm[:, bk, (i % 4) * P:(i % 4) * P + n], PRW[0:n, i, :], ident[0:n, 0:n])
                m.then_inc(par_t, 1)

            def ada_sums(n, src, done, i0=0):
                for i in range(i0, n):
                    m = pe.matmul(pm[:, 3, i:i + 1], src[:, i * P:i * P + P], ones[:, 0:1], start=True, stop=True)
                m.then_inc(done, 1)
            pe.wait_ge(ada_part, 1)
            ada_sums(16, ADA, ada_sum)
            norm_pe(pe, "mix")

            def h_parts(name):
                return lambda k: pe.wait_ge(n_hl, 8 * HN[name] + k + 1)
            pe_section(pe, SEC["conv_b"], hrhs, ready=h_parts("mix"))
            pe_section(pe, SEC["conv_a"], hrhs)

            def small_tok(w_, src, done):
                pe.wait_ge(dt_in, 16 * 8)
                for tk in range(NT):
                    for k in range(DT):
                        m = pe.matmul(pm[:, 2, tk * NH:tk * NH + NH], src[:, k, tk * P:tk * P + P], w_[:, k],
                                      start=k == 0, stop=k == DT - 1)
                m.then_inc(done, 1)
            pe.wait_ge(full_ok, 8 * FULL["mix"] + 8)
            small_tok(ws1, H, dt_p)
            pe_section(pe, SEC["xbc"], hrhs)
            pe_section(pe, SEC["z"], hrhs)
            pe.wait_ge(xbc_ok, 1)

            def xs_turn(g_, tk):
                pe.wait_ge(xs_ok, 2 * g_ + tk + 1)
                for i in range(4):
                    m = pe.transpose(pm[:, 3, i * P:i * P + P], XBC[:, 4 * g_ + i, tk * P:tk * P + P], ident[:])
                m.then_inc(xs_t, 1)
            pe.sem_inc(xs_ok, 1)
            pe.wait_ge(acc_free, SEC["g"].o0 + 4)
            for gi in range(NG):
                b_, c_ = XBC[:, 16 + gi], XBC[:, 20 + gi]
                pe.matmul(acc[:, gi, 0:T], b_[:, 0:P], c_, start=True, stop=True)
                pe.matmul(acc[:, gi, T:T + P], b_[:, P:], c_[:, P:], start=True, stop=True).then_inc(cb_p, 1)
            for tk in range(NT):
                xs_turn(0, tk)
            pe.wait_ge(cb_ok, 4)
            pe.sem_inc(seg_p, 2)
            pe.sem_inc(y_p, 2)
            gate_tile = pe_block(pe, SEC["g"], hrhs)
            for j in range(NG // 2):
                for q in range(8):
                    h0 = 16 * j + 2 * q
                    for u in range(2):
                        pe.wait_ge(l_ok, h0 + u + 1)
                        pe.wait_ge(e_ok, h0 + u + 1)
                        o_ = pm[:, u]
                        kw = dict(skip_group_check=True)
                        pe.matmul(o_[:, 0:2 * P], LS[:, u, 0:P], maskf[:, 0:2 * P], start=True, stop=False, **kw)
                        pe.matmul(o_[:, P:2 * P], LS[:, u, 2 * P:], maskf[:, 0:P], start=False, stop=False, **kw)
                        pe.matmul(o_[:, 2 * P:3 * P], LS[:, u, P:2 * P], maskf[:, 0:P], start=False, stop=True, **kw)\
                          .then_inc(seg_p, 1)
                    if q % 4 in (1, 2):
                        xs_turn(2 * j + q // 4 + 1, q % 4 - 1)
                    gate_tile(4 * j + q // 2, q // 2, False, j, only=(q % 2,))
                    for u in range(2):
                        pe.wait_ge(m_ok, h0 + u + 1)
                        if u == 0:
                            pe.wait_ge(y_ok, 8 * j + q + 1)
                        o_ = pm[64 * u:64 * u + 64, 2, 0:T]
                        pe.matmul(o_, XD[:, u, 0], ES[:, u, 0:T], start=True, stop=False, skip_group_check=True)
                        pe.matmul(o_[:, P:], XD[:, u, 1], ES[:, u, T:T + P], start=False, stop=True,
                                  skip_group_check=True).then_inc(y_p, 1)
            norm_pe(pe, "conv")
            pe.wait_ge(ysq, 1)
            pe.wait_ge(n_std, NORM["conv"][0] + 1)
            for gi in range(NG):
                for k in range(4):
                    m = pe.matmul(pm[:, gi // 2, (gi % 2) * T:(gi % 2) * T + T], ones, YSQ[:, 4 * gi + k],
                                  start=k == 0, stop=k == 3)
            m.then_inc(ysum, 1)
            pe_section(pe, SEC["conv_out"], urhs, ready=lambda k: pe.wait_ge(u_lo, k + 1))
            pe.wait_ge(ylo, 16)
            pe_section(pe, SEC["ssm_out"], yrhs)
            pe.wait_ge(rest_part, 1)
            ada_sums(24, ADA2, rest_sum)
            pe.wait_ge(mg_lo, 1)
            pe_section(pe, SEC["w_out"], urhs)
            pe.wait_ge(rest_part, 2)
            ada_sums(32, ADA2, rest_sum, 24)
            norm_pe(pe, "ffn")
            ffn_in_pe(pe)
            pe.wait_ge(hid_ok, 1)
            pe_section(pe, SEC["ffn_down"], hidrhs)
            norm_pe(pe, "final")
            pe_section(pe, SEC["a_qkv"], hrhs, ready=h_parts("final"))
            pe.wait_ge(full_ok, 8 * FULL["final"] + 8)
            small_tok(ws2, X, ba_p)
            pe_section(pe, SEC["a_z"], hrhs)

            def l2_pe(i, tiles):
                pe.wait_ge(l2_sq, i + 1)
                for k in range(8):
                    o_ = acc[:, k // 2, (k % 2) * T:(k % 2) * T + T]
                    for m_ in range(tiles):
                        m = pe.matmul(o_, ones, SQX[:, k // tiles * tiles + m_], start=m_ == 0, stop=m_ == tiles - 1)
                m.then_inc(l2_sum, 1)
            pe.wait_ge(acc_free, SEC["a_out"].o0 + 4)
            l2_pe(0, 1)
            pe.wait_ge(l2_std, 1)
            l2_pe(1, 1)
            pe.wait_ge(bet_ok, 1)
            pe.wait_ge(qkn_ok, 1)
            for q in range(4):
                for i in range(4):
                    d_, tk = 4 * (q % 2) + i, q // 2
                    m = pe.transpose(pm[:, q, i * P:i * P + P], QKV[:, 16 + d_, tk * P:tk * P + P], ident[:])
                m.then_inc(vt_p, 1)
            pe.wait_ge(vt_ok, 4)
            pe.sem_inc(go_p, 2)
            kw = dict(skip_group_check=True)
            pe.wait_ge(qkn_ok, 1)
            with pe.Fori(0, A_HEADS // 2) as j:
                for u in range(2):
                    kk, qk, sf, sb_ = (bank(u, i) for i in range(4))
                    pe.wait_ge(ks_ok, 2 * j + u + 1)
                    pe.wait_ge(go_ok, 2 * j + u + 1)
                    k_, q_ = QKV[:, ds(2 * j + u + 8, 1)], QKV[:, ds(2 * j + u, 1)]
                    for dst, r in ((kk, k_), (qk, q_)):
                        for tk in range(NT):
                            m = pe.matmul(dst[:, tk * T:tk * T + T], KS[:, u, tk * P:tk * P + P], r, start=True, stop=True)
                    m.then_inc(kq_p, 1)
                    pe.wait_ge(gl_l, 2 * j + u + 1)
                    ge = maskb[:, P:2 * P]
                    pe.matmul(sf[:, 0:T], LF[:, u, 0:P], maskf[:, 0:T], start=True, stop=False, **kw)
                    pe.matmul(sf[:, P:T], LF[:, u, T:], maskf[:, 0:P], start=False, stop=False, **kw)
                    pe.matmul(sf[:, T:3 * P], LF[:, u, P:T], maskf[:, 0:P], start=False, stop=True, **kw)
                    pe.matmul(sb_[:, 0:T], LB[:, u, 0:P], maskb[:, 0:T], start=True, stop=False, **kw)
                    pe.matmul(sb_[:, 0:P], LB[:, u, T:], ge, start=False, stop=False, **kw)
                    pe.matmul(sb_[:, T:3 * P], LB[:, u, P:T], ge, start=False, stop=True, **kw).then_inc(gs_p, 1)
                for lv in range(7):
                    for u in range(2):
                        pe.wait_ge(am_ok, 14 * j + 2 * lv + u + 1)
                        if lv:
                            pe.wait_ge(xz_ok, 14 * j + 2 * (lv - 1) + u + 1)
                        for s_ in range(4):
                            cs_ = slice(s_ * P, s_ * P + P)
                            r = XI[:, u, cs_] if lv else ident[:]
                            m = pe.matmul(bank(u, 0)[:, cs_], AM[:, u, lv % 2, cs_], r, start=True, stop=True)
                        m.then_inc(p_p, 1)
                    for u in range(2):
                        if lv == 0:
                            continue
                        pe.wait_ge(ps_ok, 12 * j + 2 * (lv - 1) + u + 1)
                        if lv == 1:
                            pe.wait_ge(qd_ok, 2 * j + u + 1)
                        for s_ in range(4):
                            cs_ = slice(s_ * P, s_ * P + P)
                            if lv < 6:
                                pe.matmul(bank(u, 1)[:, cs_], ZI[:, u, cs_], PS[:, u, cs_], start=True, stop=True)
                            m = pe.matmul(bank(u, 2)[:, cs_], PS[:, u, cs_], ZI[:, u, cs_], start=True, stop=True)
                        m.then_inc(vw_p, 1)
                for u in range(2):
                    b3 = bank(u, 3)
                    hc = ds((2 * j + u) * P, P)
                    pe.wait_ge(xz_ok, 14 * j + 12 + u + 1)
                    pe.matmul(b3[:, 0:P], ZI[:, u, 0:P], VT[:, 0, hc], start=True, stop=True)
                    pe.matmul(b3[:, P:T], ZI[:, u, 3 * P:], VT[:, 1, hc], start=True, stop=True).then_inc(s1_p, 1)
                for u in range(2):
                    b3 = bank(u, 3)
                    pe.wait_ge(vn1, 2 * j + u + 1)
                    pe.matmul(b3[:, T:3 * P], KDX[:, u, 0:P], VN[:, u, 0:P], start=True, stop=True)
                    pe.matmul(b3[:, 3 * P:], KDX[:, u, P:], VN[:, u, 3 * P:], start=True, stop=True).then_inc(r_p, 1)
                for u in range(2):
                    b3 = bank(u, 3)
                    pe.wait_ge(rh_ok, 2 * j + u + 1)
                    pe.matmul(b3[:, 0:P], ZI[:, u, P:2 * P], RH[:, u, 0:P], start=True, stop=True)
                    pe.matmul(b3[:, P:T], ZI[:, u, 2 * P:3 * P], RH[:, u, P:], start=True, stop=True).then_inc(s2_p, 1)
                for u in range(2):
                    o_ = bank(u, 1)
                    pe.wait_ge(vn2, 2 * j + u + 1)
                    pe.matmul(o_[:, 0:T], VN[:, u, 0:P], DF[:, u, 0:T], start=True, stop=False, **kw)
                    pe.matmul(o_[:, P:T], VN[:, u, P:T], DF[:, u, T:], start=False, stop=False, **kw)
                    pe.matmul(o_[:, 0:T], VN[:, u, 3 * P:], DB[:, u, 0:T], start=False, stop=False, **kw)
                    pe.matmul(o_[:, 0:P], VN[:, u, T:3 * P], DB[:, u, T:], start=False, stop=True, **kw).then_inc(go_p, 1)
            l2_pe(2, 1)
            pe_section(pe, SEC["a_out"], hrhs, ready=h_parts("gdn"))
            norm_pe(pe, "ln1_0")

            def mlp(k):
                pe_section(pe, SEC[f"mlp1_{k}"], hrhs, ready=h_parts(f"ln1_{k}"))
                pe.wait_ge(hid_lo, 32 * k + 32 + 4)
                pe_section(pe, SEC[f"mlp2_{k}"], hidrhs)
                norm_pe(pe, f"ln2_{k}")
            mlp(0)
            pe_section(pe, SEC["b_qk"], hrhs, ready=h_parts("ln2_0"))
            pe_section(pe, SEC["b_v"], hrhs, tok_major=True)
            pe_section(pe, SEC["b_r"], hrhs)
            pe.wait_ge(full_ok, 8 * FULL["ln2_0"] + 8)
            for k in range(DT):
                m = pe.matmul(pm[0:NH, 2, 0:T], ws3[:, k], X[:, k], start=k == 0, stop=k == DT - 1)
            m.then_inc(gl_p, 1)
            pe.wait_ge(gl_ok, 1)
            pe.wait_ge(gw_in, 16 * 2)
            pe.wait_ge(acc_free, SEC["b_out"].o0 + 4)
            for d in range(2):
                for k in range(4):
                    i = 4 * d + k
                    m = pe.matmul(acc[:, i // 2, (i % 2) * T:(i % 2) * T + T], gw[:, d, k * P:k * P + P], glt[:],
                                  start=True, stop=True)
            m.then_inc(lg_p, 1)
            pe.sem_inc(bo_p, 1)
            pe.sem_inc(sc_p, 2)
            pe.wait_ge(bs_ok, 1)
            with pe.Fori(0, B_HEADS) as h:
                pe.wait_ge(st_ok, h + 1)
                pe.wait_ge(bo_ok, 2 * h + 2)
                for tk in range(NT):
                    tc = slice(tk * P, tk * P + P)
                    m = pe.matmul(acc[:, 3, tc], QKH[:, 0, tc], QKH[:, 1, tc], start=True, stop=True)
                m.then_inc(dg_p, 1)
                for lv in range(8):
                    pe.wait_ge(kq_ok, 8 * h + lv + 3)
                    pe.wait_ge(s_ok, 8 * h + lv + 1)
                    for tk in range(NT):
                        tc = slice(tk * P, tk * P + P)
                        rc = tc if lv < 7 else slice((1 - tk) * P, (1 - tk) * P + P)
                        m = pe.matmul(pm[:, lv % 4, tc], KQ[:, lv % 2, 0, tc], KQ[:, lv % 2, 1, rc], start=True, stop=True)
                    m.then_inc(sc_p, 1)
                pe.wait_ge(s_ok, 8 * h + 8 + 4)
                for e in range(2):
                    for tk in range(NT):
                        m = pe.matmul(acc[:, e, 0:T], VH[:, tk, e * P:e * P + P], SS[:, tk], start=tk == 0, stop=tk == 1)
                m.then_inc(bo_p, 1)
            l2_pe(3, 2)
            pe_section(pe, SEC["b_out"], hrhs, ready=h_parts("gla"))
            norm_pe(pe, "ln1_1")
            mlp(1)
            pe.wait_ge(n_hh, 8 * HN["ln2_1"] + 8)
            for q in range(4):
                for i in range(4):
                    d_, tk = 4 * (q % 2) + i, q // 2
                    m = pe.transpose(pm[:, q, i * P:i * P + P], X[:, d_, tk * P:tk * P + P], ident[:])
                m.then_inc(ot_p, 1)
        running.close()


_INS = ["x", "c", "w_ada_mix", "b_ada_mix", "norm_mix_w", "w_in", "conv_dw_w", "conv_dw_b", "conv_ln_w",
        "conv_ln_b", "w_conv_out", "ssm_conv_w", "ssm_conv_b", "dt_bias", "a_log", "d_skip", "ssm_norm_w",
        "w_ssm_out", "w_out", "w_ada_ffn", "b_ada_ffn", "norm_ffn_w", "w_ffn_in", "w_ffn_down", "final_norm_w",
        "a_w_in_2", "a_conv_2", "a_alog_2", "a_dt_bias_2", "a_norm_g_2", "a_w_out_2", "b_w_in_2", "b_gate_w2_2",
        "b_gate_b_2", "b_norm_g_2", "b_w_out_2", "ln1_g_2", "ln1_b_2", "mlp_w1_2", "mlp_w2_2", "ln2_g_2", "ln2_b_2"]


def kernel(**inputs):
    import numpy as _np
    import concourse.bacc as _bacc
    from concourse.bass_utils import run_bass_kernel_spmd as _run

    nc = _bacc.Bacc("TRN2", target_bir_lowering=False, num_devices=1)
    arrays, args = {}, {}
    for name in _INS:
        x = _np.ascontiguousarray(inputs[name])
        arrays[f"in_{name}"] = x
        args[name] = nc.dram_tensor(f"in_{name}", x.shape, mybir.dt.from_np(x.dtype), kind="ExternalInput").ap()
    out = nc.dram_tensor("out_x", (1, T, D), F32, kind="ExternalOutput").ap()
    program(nc, args, out)
    return _run(nc, [arrays], core_ids=[0]).results[0]["out_x"]
```
